# Optimizing a Trainium2 kernel written in Bass

```python
import jax
import jax.numpy as jnp
from jax import lax
import numpy as np

D_MODEL = 1024
BATCH = 1
SEQ = 512
DEPTH = 2

CHUNK = 64
Q_BLOCK = 128
EPS = 1e-6

SSD_HEAD_DIM = 64
SSD_WIDTH = D_MODEL // 2
SSD_HEADS = SSD_WIDTH // SSD_HEAD_DIM
SSD_GROUPS = 2
SSD_STATE = 64
CONV_WIDTH = 4
XBC_WIDTH = SSD_WIDTH + 2 * SSD_GROUPS * SSD_STATE

POOL_WINDOWS = (2, 4, 8, 16)
POOL_GROUPS = len(POOL_WINDOWS)
POOL_WIDTH = D_MODEL // 4
POOL_GROUP_DIM = POOL_WIDTH // POOL_GROUPS

SB_HEAD_DIM = 64
SB_WIDTH = D_MODEL // 4
SB_HEADS = SB_WIDTH // SB_HEAD_DIM

MIX_WIDTH = SSD_WIDTH + POOL_WIDTH + SB_WIDTH
IN_WIDTH = SSD_WIDTH + XBC_WIDTH + SSD_HEADS + POOL_WIDTH + 3 * SB_WIDTH

PEER_HEADS = 8
PEER_TOPK = 16
N_KEYS = 128
N_EXPERTS = N_KEYS * N_KEYS
PEER_QDIM = 256
PEER_HALF = PEER_QDIM // 2
PEER_BLOCK = 128

kernel_name = "hybrid_ssd_pool_stickbreak_peer"

def rms_norm(x, g):
    xf = x.astype(jnp.float32)
    y = xf * lax.rsqrt(jnp.mean(xf * xf, axis=-1, keepdims=True) + EPS)
    return (y * g.astype(jnp.float32)).astype(x.dtype)

def modulate(h, shift, scale):
    return h * (1.0 + scale[:, None, :]) + shift[:, None, :]

def causal_depthwise_conv(x, w, b):
    out = lax.conv_general_dilated(
        x, w[:, None, :], window_strides=(1,), padding=[(CONV_WIDTH - 1, 0)],
        dimension_numbers=('NWC', 'WIO', 'NWC'), feature_group_count=x.shape[-1])
    return out + b

def ssd_chunked(x, dt, a_neg, bm, cm):
    bsz, s, h, p = x.shape
    g, n = bm.shape[-2:]
    k = h // g
    nc = s // CHUNK
    xdt = (x * dt[..., None]).reshape(bsz, nc, CHUNK, g, k, p)
    bm = bm.reshape(bsz, nc, CHUNK, g, n)
    cm = cm.reshape(bsz, nc, CHUNK, g, n)
    a_cs = jnp.cumsum((dt * a_neg).reshape(bsz, nc, CHUNK, g, k), axis=2)
    seg = a_cs[:, :, :, None] - a_cs[:, :, None]
    pos = jnp.arange(CHUNK)
    tril = (pos[:, None] >= pos[None, :])[:, :, None, None]
    decay_ls = jnp.exp(jnp.where(tril, seg, -jnp.inf))
    cb = jnp.einsum('bclgn,bcsgn->bclsg', cm, bm)
    y_diag = jnp.einsum('bclsg,bclsgk,bcsgkp->bclgkp', cb, decay_ls, xdt)
    decay_states = jnp.exp(a_cs[:, :, -1:] - a_cs)
    states = jnp.einsum('bclgn,bclgk,bclgkp->bcgkpn', bm, decay_states, xdt)
    chunk_decay = jnp.exp(a_cs[:, :, -1])

    def step(carry, inp):
        s_c, d_c = inp
        return d_c[..., None, None] * carry + s_c, carry

    _, prev = lax.scan(step, jnp.zeros_like(states[:, 0]),
                       (jnp.moveaxis(states, 1, 0), jnp.moveaxis(chunk_decay, 1, 0)))
    prev = jnp.moveaxis(prev, 0, 1)
    y_off = jnp.einsum('bclgn,bcgkpn,bclgk->bclgkp', cm, prev, jnp.exp(a_cs))
    return (y_diag + y_off).reshape(bsz, s, h, p)

def multiscale_pool(xp, w_pool, scale):
    bsz, s, _ = xp.shape
    xf = xp.astype(jnp.float32).reshape(bsz, s, POOL_GROUPS, POOL_GROUP_DIM)
    cs = jnp.concatenate([jnp.zeros_like(xf[:, :1]), jnp.cumsum(xf, axis=1)], axis=1)
    t = jnp.arange(s)
    means = []
    for gi, w in enumerate(POOL_WINDOWS):
        cs_g = cs[:, :, gi]
        lo = jnp.maximum(t + 1 - w, 0)
        cnt = jnp.minimum(t + 1, w).astype(jnp.float32)
        means.append((cs_g[:, 1:] - cs_g[:, lo]) / cnt[None, :, None])
    pooled = (jnp.stack(means, axis=2) - xf).astype(xp.dtype)
    mixed = jnp.einsum('bsgc,gcd->bsgd', pooled, w_pool)
    return mixed.reshape(bsz, s, POOL_WIDTH) * scale

def stick_breaking_attention(q, k, v):
    bsz, s, h, d = q.shape
    nb = s // Q_BLOCK
    kf = k.transpose(0, 2, 1, 3)
    vf = v.transpose(0, 2, 1, 3)
    qb = q.reshape(bsz, nb, Q_BLOCK, h, d).transpose(1, 0, 3, 2, 4)
    key_pos = jnp.arange(s)
    inv_sqrt_d = d ** -0.5

    def block(args):
        q_blk, i = args
        qpos = i * Q_BLOCK + jnp.arange(Q_BLOCK)
        z = jnp.einsum('bhqd,bhsd->bhqs', q_blk, kf).astype(jnp.float32) * inv_sqrt_d
        mask = key_pos[None, :] < qpos[:, None]
        log_beta = jax.nn.log_sigmoid(z)
        log_keep = jnp.where(mask, log_beta - z, 0.0)
        later = lax.cumsum(log_keep, axis=3, reverse=True) - log_keep
        w = jnp.where(mask, jnp.exp(log_beta + later), 0.0)
        return jnp.einsum('bhqs,bhsd->bhqd', w.astype(vf.dtype), vf)

    out = lax.map(block, (qb, jnp.arange(nb)))
    return out.transpose(1, 0, 3, 2, 4).reshape(bsz, s, h * d)

def token_mixer(h, w_in, conv_w, conv_b, dt_bias, a_log, d_skip, ssd_norm_g,
                pool_w, pool_scale, w_out):
    bsz, s, _ = h.shape
    proj = h @ w_in
    cuts = [SSD_WIDTH, SSD_WIDTH + XBC_WIDTH, SSD_WIDTH + XBC_WIDTH + SSD_HEADS,
            SSD_WIDTH + XBC_WIDTH + SSD_HEADS + POOL_WIDTH]
    z, xbc, dt_raw, xp, qkv = jnp.split(proj, cuts, axis=-1)

    xbc = jax.nn.silu(causal_depthwise_conv(xbc, conv_w, conv_b))
    xs, bm, cm = jnp.split(xbc, [SSD_WIDTH, SSD_WIDTH + SSD_GROUPS * SSD_STATE], axis=-1)
    dt = jax.nn.softplus(dt_raw.astype(jnp.float32) + dt_bias.astype(jnp.float32))
    a_neg = -jnp.exp(a_log.astype(jnp.float32))
    xs4 = xs.reshape(bsz, s, SSD_HEADS, SSD_HEAD_DIM).astype(jnp.float32)
    y = ssd_chunked(xs4, dt, a_neg,
                    bm.reshape(bsz, s, SSD_GROUPS, SSD_STATE).astype(jnp.float32),
                    cm.reshape(bsz, s, SSD_GROUPS, SSD_STATE).astype(jnp.float32))
    y = y + d_skip.astype(jnp.float32)[:, None] * xs4
    y = y.reshape(bsz, s, SSD_WIDTH) * jax.nn.silu(z.astype(jnp.float32))
    yg = y.reshape(bsz, s, SSD_GROUPS, SSD_WIDTH // SSD_GROUPS)
    yg = yg * lax.rsqrt(jnp.mean(yg * yg, axis=-1, keepdims=True) + EPS)
    y_ssd = (yg.reshape(bsz, s, SSD_WIDTH) * ssd_norm_g.astype(jnp.float32)).astype(h.dtype)

    y_pool = multiscale_pool(xp, pool_w, pool_scale)

    q, k, v = jnp.split(qkv, 3, axis=-1)
    shp = (bsz, s, SB_HEADS, SB_HEAD_DIM)
    y_sb = stick_breaking_attention(q.reshape(shp), k.reshape(shp), v.reshape(shp))

    mixed = jnp.concatenate([y_ssd, y_pool.astype(h.dtype), y_sb.astype(h.dtype)], axis=-1)
    return mixed @ w_out

def peer_ffn(h, w_q, keys, u_tab, v_tab):
    bsz, s, d = h.shape
    t = bsz * s
    ht = h.reshape(t, d)
    q = (ht @ w_q).reshape(t, PEER_HEADS, 2, PEER_HALF)
    sc = jnp.einsum('thid,hikd->thik', q, keys).astype(jnp.float32)
    top_s, top_i = lax.top_k(sc, PEER_TOPK)
    cand = top_s[:, :, 0, :, None] + top_s[:, :, 1, None, :]
    best_s, best_pos = lax.top_k(cand.reshape(t, PEER_HEADS, PEER_TOPK * PEER_TOPK), PEER_TOPK)
    i1 = jnp.take_along_axis(top_i[:, :, 0], best_pos // PEER_TOPK, axis=-1)
    i2 = jnp.take_along_axis(top_i[:, :, 1], best_pos % PEER_TOPK, axis=-1)
    experts = i1 * N_KEYS + i2
    gates = jax.nn.softmax(best_s, axis=-1).astype(h.dtype)
    nb = t // PEER_BLOCK

    def block(args):
        hb, eb, gb = args
        act = jnp.einsum('thkd,td->thk', u_tab[eb], hb)
        coef = gb * jax.nn.gelu(act, approximate=False)
        return jnp.einsum('thk,thkd->td', coef, v_tab[eb])

    out = lax.map(block, (ht.reshape(nb, PEER_BLOCK, d),
                          experts.reshape(nb, PEER_BLOCK, PEER_HEADS, PEER_TOPK),
                          gates.reshape(nb, PEER_BLOCK, PEER_HEADS, PEER_TOPK)))
    return out.reshape(bsz, s, d)

def setup_inputs(seed: int = 0):
    key = jax.random.key(seed)
    ks = jax.random.split(key, 22)
    L, D = DEPTH, D_MODEL
    f32 = jnp.float32
    nrm = jax.random.normal
    dt0 = jnp.exp(jax.random.uniform(ks[9], (L, SSD_HEADS), f32,
                                     float(np.log(1e-3)), float(np.log(1e-1))))
    return {
        'x': nrm(ks[0], (BATCH, SEQ, D), f32),
        'c': nrm(ks[1], (BATCH, D), f32),
        'ada_w': nrm(ks[2], (L, D, 6 * D), f32) * (0.5 * D ** -0.5),
        'ada_b': nrm(ks[3], (L, 6 * D), f32) * 0.01,
        'mix_norm_g': 1.0 + 0.05 * nrm(ks[4], (L, D), f32),
        'ffn_norm_g': 1.0 + 0.05 * nrm(ks[5], (L, D), f32),
        'w_in': nrm(ks[6], (L, D, IN_WIDTH), f32) * D ** -0.5,
        'conv_w': nrm(ks[7], (L, CONV_WIDTH, XBC_WIDTH), f32) * CONV_WIDTH ** -0.5,
        'conv_b': nrm(ks[8], (L, XBC_WIDTH), f32) * 0.01,
        'dt_bias': dt0 + jnp.log(-jnp.expm1(-dt0)),
        'a_log': jnp.log(jax.random.uniform(ks[10], (L, SSD_HEADS), f32, 1.0, 16.0)),
        'd_skip': 1.0 + 0.05 * nrm(ks[11], (L, SSD_HEADS), f32),
        'ssd_norm_g': 1.0 + 0.05 * nrm(ks[12], (L, SSD_WIDTH), f32),
        'pool_w': nrm(ks[13], (L, POOL_GROUPS, POOL_GROUP_DIM, POOL_GROUP_DIM), f32) * POOL_GROUP_DIM ** -0.5,
        'pool_scale': 1.0 + 0.1 * nrm(ks[14], (L, POOL_WIDTH), f32),
        'w_out': nrm(ks[15], (L, MIX_WIDTH, D), f32) * MIX_WIDTH ** -0.5,
        'peer_wq': nrm(ks[16], (L, D, PEER_HEADS * PEER_QDIM), f32) * D ** -0.5,
        'peer_keys': nrm(ks[17], (L, PEER_HEADS, 2, N_KEYS, PEER_HALF), f32) * PEER_HALF ** -0.5,
        'peer_u': nrm(ks[18], (L, N_EXPERTS, D), f32) * D ** -0.5,
        'peer_v': nrm(ks[19], (L, N_EXPERTS, D), f32),
        'final_norm_g': 1.0 + 0.05 * nrm(ks[20], (D,), f32),
    }

def reference(x, c, ada_w, ada_b, mix_norm_g, ffn_norm_g, w_in, conv_w, conv_b, dt_bias,
              a_log, d_skip, ssd_norm_g, pool_w, pool_scale, w_out, peer_wq, peer_keys,
              peer_u, peer_v, final_norm_g):
    cond = jax.nn.silu(c)
    for l in range(DEPTH):
        mod = cond @ ada_w[l] + ada_b[l]
        sh1, sc1, g1, sh2, sc2, g2 = jnp.split(mod, 6, axis=-1)
        h = modulate(rms_norm(x, mix_norm_g[l]), sh1, sc1)
        mix = token_mixer(h, w_in[l], conv_w[l], conv_b[l], dt_bias[l], a_log[l], d_skip[l],
                          ssd_norm_g[l], pool_w[l], pool_scale[l], w_out[l])
        x = x + g1[:, None, :] * mix
        h = modulate(rms_norm(x, ffn_norm_g[l]), sh2, sc2)
        x = x + g2[:, None, :] * peer_ffn(h, peer_wq[l], peer_keys[l], peer_u[l], peer_v[l])
    return rms_norm(x, final_norm_g)


_drawn_inputs = setup_inputs


def setup_inputs(seed=0):
    import zlib

    import numpy as np

    out = dict(_drawn_inputs(seed))
    spreads = {}
    factors = {'conv_b': 3.489}
    for name, (base, spread) in spreads.items():
        noise = np.random.default_rng([zlib.crc32(name.encode()), seed]).standard_normal(out[name].shape)
        drawn = base * np.exp(spread * noise) if base else spread * noise
        out[name] = jnp.asarray(drawn.astype(out[name].dtype))
    for name, factor in factors.items():
        out[name] = (out[name] * factor).astype(out[name].dtype)
    return out
```

```python
from contextlib import ExitStack, contextmanager

import concourse.bass as bass
from concourse import mybir

F32 = mybir.dt.float32
F32R = mybir.dt.float32r
U32 = mybir.dt.uint32
ALU = mybir.AluOpType
ACT = mybir.ActivationFunctionType
AX = mybir.AxisListType

P = 128
LAYERS = 2
D = 1024
KT = D // P
T = 512
NT = T // P
EPS = 1e-6

HEADS = 8
HD = 64
SB_HEADS = 4

Z0, XS0, B0, C0, XP0, Q0, K0, V0 = 0, 4, 8, 9, 10, 12, 14, 16
N_IN = 18
N_OUT = KT
N_Q = 16
N_KEYS = 128
N_U = N_KEYS
OUT0 = N_IN
WQ0 = OUT0 + N_OUT
U0 = WQ0 + N_Q
STREAM = U0 + N_U
assert STREAM % 2 == 0 and U0 % 2 == 0 and WQ0 % 2 == 0 and OUT0 % 2 == 0

PAD = 16
PJW = PAD + T

ADA_CHUNK = 512
ADA_CHUNKS = 6 * D // ADA_CHUNK
ADA_TILES = ADA_CHUNK // P

SEGS = 16
PH = 8
TOPK = 16
HK = PH * TOPK
assert HK == P

GROUP = 4
GROUPS = N_KEYS // GROUP
OUTS = GROUPS * KT
GCHUNK = 64
GCHUNKS = T // GCHUNK
QUAD = 4
QUADS = T // QUAD

PARAMS = [("ada_b", 48), ("g_mix", KT), ("g_ffn", KT), ("conv_w", 24), ("conv_b", 6), ("ssd_g", 4),
          ("pool_scale", 2), ("d_skip", 4), ("dt_bias", HEADS), ("a_log", HEADS),
          ("w_dt", KT * HEADS), ("pool_w", 2 * P)]
PCOL = {}
_c = 0
for _n, _w in PARAMS:
    PCOL[_n] = (_c, _w)
    _c += _w
NPAR = _c

DVE_STEPS = 487
ACT_STEPS = 8


class Steps:

    def __init__(self, eng, sem, settled=None):
        self.eng, self.sem, self.settled, self.base, self.n = eng, sem, settled, 0, 0

    def settle(self):
        self.eng.sem_inc(self.settled, 1)

    def link(self, ins):
        ins.then_inc(self.sem, 1)
        self.n += 1
        self.eng.wait_ge(self.sem, self.base + self.n)

    @contextmanager
    def loop(self, i, times, per):
        base, n = self.base, self.n
        self.base, self.n = base + n + i * per, 0
        yield
        assert self.n == per, (self.n, per)
        self.base, self.n = base, n + times * per


def build(nc, xT, cT, final_g, adaw, wst, vst, params, keysT, g_dram, outT):
    vst = vst.rearrange("l g p b d -> l g p (b d)")
    ctx = ExitStack()
    with ctx:
        def sb(name, shape, dt=F32, where=ctx):
            return where.enter_context(nc.sbuf_tensor(name, shape, dt))

        def sem(name):
            return ctx.enter_context(nc.semaphore(name))

        ident = sb("ident", [P, P])
        tri_le = sb("tri_le", [P, P])
        tri_ge = sb("tri_ge", [P, P])
        tri_lt = sb("tri_lt", [P, P])
        ones = sb("ones", [P, P])
        iota = sb("iota", [P, P])
        inv_count = sb("inv_count", [P, 2, T])
        x = sb("x", [P, KT, T])
        cond = sb("cond", [P, KT])
        fin_g = sb("fin_g", [P, KT])
        par = sb("par", [P, NPAR])
        mod = sb("mod", [P, 6, KT])
        gs = sb("gs", [P, 2, KT])
        hH = sb("hH", [P, KT, T], F32R)
        hL = sb("hL", [P, KT, T], F32R)
        w_raw = sb("w_raw", [P, 2, D])
        w_hi = [sb(f"w_hi{s}", [P, KT, P], F32R) for s in range(2)]
        w_lo = [sb(f"w_lo{s}", [P, KT, P], F32R) for s in range(2)]
        tiny = sb("tiny", [P, 16, 32])

        def pcol(name, n=None):
            a, w = PCOL[name]
            return par[:, a:a + w]

        mixer = ExitStack()
        pj = sb("pj", [P, N_IN, PJW], where=mixer)
        h32 = sb("h32", [P, KT, T], where=mixer)
        nrm = sb("nrm", [P, 4, T], where=mixer)
        ada_stack = ExitStack()
        ada_buf = sb("ada_buf", [P, 2, KT, ADA_CHUNK], where=ada_stack)
        ada_stack.close()
        scan = ExitStack()
        xbc = sb("xbc", [P, 6, T], where=scan)
        xdt = sb("xdt", [P, NT, T], where=scan)
        y_tok = sb("y_tok", [P, NT, T], where=scan)
        xdd = sb("xdd", [P, T], where=scan)
        b_tok = sb("b_tok", [P, NT, P], where=scan)
        cbm = sb("cbm", [P, 2, NT, P], where=scan)
        state = sb("state", [P, 4 * HD], where=scan)
        seg = sb("seg", [P, 2, T], where=scan)
        smat = sb("smat", [P, 2, T], where=scan)
        scan.close()
        W4 = [T - P * i for i in range(NT)]
        O4 = [sum(W4[:i]) for i in range(NT)]
        WA = sum(W4)
        v_tok = sb("v_tok", [P, NT, 2 * P], where=mixer)
        zs = sb("zs", [P, WA], where=mixer)
        ez = sb("ez", [P, WA], where=mixer)
        nlk = sb("nlk", [P, WA], where=mixer)
        arg = sb("arg", [P, WA], where=mixer)
        pool_a = sb("pool_a", [P, 2, PJW], where=mixer)
        pool_b = sb("pool_b", [P, 2, PJW], where=mixer)
        pool_c = sb("pool_c", [P, 2, PJW], where=mixer)
        pooled = sb("pooled", [P, 2, T], where=mixer)
        mixer.close()
        mixed = h32

        router = ExitStack()
        sb("r_pad", [P, N_IN * PJW], where=router)
        sb("r_h32", [P, KT * T], where=router)
        sb("r_nrm", [P, 4 * T], where=router)
        keys = sb("keys", [P, SEGS, N_KEYS], where=router)
        qT = sb("qT", [P, 2, T], where=router)
        idxT = sb("idxT", [P, 3, T], where=router)
        topv = sb("topv", [P, NT, SEGS, TOPK], where=router)
        topi = sb("topi", [P, NT, SEGS, TOPK], where=router)
        router.close()
        r2 = ExitStack()
        v16 = sb("v16", [P, NT, TOPK], where=r2)
        i16 = sb("i16", [P, NT, TOPK], U32, where=r2)
        sc2 = sb("sc2", [P, NT, N_KEYS], where=r2)
        cand = sb("cand", [P, PH, TOPK * TOPK], where=r2)
        cand2 = sb("cand2", [P, PH, TOPK * TOPK], where=r2)
        bestv = sb("bestv", [P, PH, TOPK], where=r2)
        bestp = sb("bestp", [P, PH, TOPK], U32, where=r2)
        posu = sb("posu", [P, 2, HK], U32, where=r2)
        posf = sb("posf", [P, 2, HK], where=r2)
        pick = sb("pick", [P, HK, TOPK], where=r2)
        route = sb("route", [P, 3, HK], where=r2)
        gsum = sb("gsum", [P, 2, PH], where=r2)
        r2.close()
        r3 = ExitStack()
        oneh = sb("oneh", [P, 2, QUAD, P], where=r3)
        gateh = sb("gateh", [P, 2, QUAD, P], where=r3)
        stage = [sb(f"stage{s}", [P, N_KEYS, GCHUNK], where=r3) for s in range(2)]
        r3.close()

        ex = ExitStack()
        v_raw = sb("v_raw", [P, GROUP, D], where=ex)
        v_hi = sb("v_hi", [P, GROUP, D], F32R, where=ex)
        v_lo = sb("v_lo", [P, GROUP, D], F32R, where=ex)
        c_hi = [sb(f"c_hi{s}", [P, GROUP, T], F32R, where=ex) for s in range(2)]
        c_lo = [sb(f"c_lo{s}", [P, GROUP, T], F32R, where=ex) for s in range(2)]
        gates = [sb(f"gates{s}", [P, GCHUNKS, GROUP, GCHUNK], where=ex) for s in range(2)]
        act_g = sb("act_g", [P, 2, T], where=ex)
        coef = sb("coef", [P, 2, T], where=ex)
        ex.close()

        bank = [ctx.enter_context(nc.psum_tensor(f"bank{i}", [P, T], F32)) for i in range(8)]

        s_const = sem("const_ready")
        s_in = sem("inputs_in")
        s_cond = sem("cond_ready")
        s_gate = sem("layer_may_start")
        s_par = sem("params_in")
        s_keys = sem("keys_in")
        s_ada = [sem(f"ada_in{s}") for s in range(2)]
        s_adau = sem("ada_used")
        s_mod = sem("mod_ready")
        s_raw = [sem(f"w_raw_in{s}") for s in range(2)]
        s_wh = sem("w_hi_ready")
        s_wl = sem("w_lo_ready")
        s_tile = sem("tile_done")
        s_taken = sem("tile_taken")
        s_sq = sem("squares_ready")
        s_ssum = sem("square_sum_done")
        s_var = sem("variance_ready")
        s_root = sem("root_ready")
        s_h32 = sem("normed_ready")
        s_hh = sem("rhs_hi_ready")
        s_rhs = sem("rhs_ready")
        s_dve = sem("dve_steps")
        s_act = sem("act_steps")
        s_dset = sem("dve_waits_settled")
        s_pset = sem("pe_waits_settled")
        s_dtm = sem("dt_done")
        s_dt1 = sem("dt_abs_ready")
        s_dt2 = sem("dt_exp_ready")
        s_dt3 = sem("dt_one_plus_ready")
        s_dt4 = sem("dt_log_ready")
        s_dta = sem("dta_ready")
        s_acs = sem("decay_sums_done")
        s_acv = sem("decay_diffs_ready")
        s_dec = sem("decays_ready")
        s_conv = sem("conv_ready")
        s_xbc = sem("xbc_ready")
        s_tr = sem("transposes_done")
        s_trv = sem("transposes_taken")
        s_cb = sem("cb_done")
        s_cbv = sem("cb_taken")
        s_r = sem("decay_rows_done")
        s_seg = sem("segments_ready")
        s_exp = sem("segment_exp_ready")
        s_sm = sem("scan_matrix_ready")
        s_xdd = sem("decayed_x_ready")
        s_y = sem("y_done")
        s_yv = sem("y_taken")
        s_st = sem("state_ready")
        s_yt = sem("y_transposed")
        s_ygv = sem("y_gated")
        s_zs = sem("z_silu_ready")
        s_ysq = sem("y_squares_ready")
        s_yss = sem("y_square_sum_done")
        s_yvar = sem("y_variance_ready")
        s_yroot = sem("y_root_ready")
        s_pool = sem("pooled_ready")
        s_pm = sem("pool_mixed_done")
        s_vt = sem("v_tokens_done")
        s_vtv = sem("v_tokens_ready")
        s_z = sem("att_scores_done")
        s_zv = sem("att_scores_ready")
        s_lg = sem("att_log_ready")
        s_nlk = sem("att_keep_ready")
        s_cum = sem("att_sums_done")
        s_arg = sem("att_exponent_ready")
        s_w = sem("att_exp_ready")
        s_wm = sem("att_weights_ready")
        s_ay = sem("att_out_done")
        s_ayv = sem("att_out_taken")
        s_sc = sem("key_scores_done")
        s_scv = sem("key_scores_taken")
        s_shift = sem("gate_exponent_ready")
        s_gexp = sem("gate_exp_ready")
        s_rt = sem("route_ready")
        s_rtt = sem("route_transposed")
        s_idx = sem("route_rows_ready")
        s_oh = sem("one_hots_ready")
        s_gm = sem("gate_matrices_done")
        s_gv = sem("gate_matrices_taken")
        s_gst = [sem(f"gates_stored{s}") for s in range(2)]
        s_gin = [sem(f"gates_in{s}") for s in range(2)]
        s_vin = sem("v_raw_in")
        s_vh = sem("v_hi_ready")
        s_vl = sem("v_lo_ready")
        s_coef = sem("coef_ready")
        s_out = sem("out_sum_done")
        s_add = sem("out_sum_added")
        s_fin = sem("result_ready")
        s_ret = sem("result_stored")

        block = ctx.enter_context(nc.Block())
        @block.sync
        def _(sp):
            sp.dma_start(x[:, :, :], xT).then_inc(s_in, 16)
            sp.dma_start(cond[:, :], cT).then_inc(s_in, 16)
            sp.dma_start(fin_g[:, :], final_g).then_inc(s_in, 16)

            def load_w(l, n, s):
                sp.dma_start(w_raw[:, s, :], wst[l, n]).then_inc(s_raw[s], 16)

            def next_w(l, n, s):
                sp.wait_ge(s_wh, l * STREAM + n + 1)
                sp.wait_ge(s_wl, l * STREAM + n + 1)
                load_w(l, n + 2, s)

            def load_gates(l, g, s):
                sp.dma_start(gates[s][:, :, :, :],
                             g_dram[:, :, bass.ds(g * GROUP, GROUP), :].rearrange("c p b t -> p c b t")
                             ).then_inc(s_gin[s], 16)

            def load_v(l, g):
                sp.dma_start(v_raw[:, :, :].rearrange("p b d -> p (b d)"), vst[l, g]).then_inc(s_vin, 16)

            with sp.Fori(0, LAYERS) as l:
                sp.wait_ge(s_gate, l + 1)
                sp.dma_start(par[:, :], params[l]).then_inc(s_par, 16)
                load_w(l, 0, 0)
                load_w(l, 1, 1)
                for c in range(ADA_CHUNKS):
                    if c >= 2:
                        sp.wait_ge(s_adau, l * ADA_CHUNKS + c - 1)
                    sp.dma_start(ada_buf[:, c % 2, :, :], adaw[l, c]).then_inc(s_ada[c % 2], 16)
                with sp.Fori(0, OUT0 // 2) as i:
                    for s in range(2):
                        next_w(l, i * 2 + s, s)
                with sp.Fori(0, N_OUT // 2) as i:
                    for s in range(2):
                        next_w(l, i * 2 + OUT0 + s, s)
                sp.wait_ge(s_rhs, l * 3 + 2)
                sp.dma_start(keys[:, :, :], keysT[l]).then_inc(s_keys, 16)
                with sp.Fori(0, N_Q // 2) as i:
                    for s in range(2):
                        next_w(l, i * 2 + WQ0 + s, s)
                for s in range(2):
                    sp.wait_ge(s_gst[s], (l * (GCHUNKS // 2) + GCHUNKS // 2) * 16)
                load_gates(l, 0, 0)
                load_v(l, 0)
                load_gates(l, 1, 1)
                for j in range(GROUP):
                    next_w(l, U0 + j, j % 2)

                def after(g, s, last=False):
                    for j in range(GROUP):
                        if not (last and j >= 2):
                            next_w(l, g * GROUP + (U0 + GROUP + j), j % 2)
                    sp.wait_ge(s_vh, l * N_U + g * GROUP + GROUP)
                    sp.wait_ge(s_vl, l * N_U + g * GROUP + GROUP)
                    load_v(l, g + 1)
                    if not last:
                        sp.wait_ge(s_coef, l * N_U + g * GROUP + (GROUP + 2))
                        load_gates(l, g + 2, s)

                with sp.Fori(0, GROUPS // 2 - 1) as i:
                    after(i * 2, 0)
                    after(i * 2 + 1, 1)
                after(GROUPS - 2, 0, last=True)
            sp.wait_ge(s_fin, 1)
            sp.dma_start(outT, x[:, :, :]).then_inc(s_ret, 16)
            sp.wait_ge(s_ret, 16)

        @block.gpsimd
        def _(pool):
            pool.memset(ones[:, :], 1.0).then_inc(s_const, 1)
            pool.memset(ident[:, :], 0.0).then_inc(s_const, 1)
            pool.memset(tri_le[:, :], 1.0).then_inc(s_const, 1)
            pool.memset(tri_ge[:, :], 1.0).then_inc(s_const, 1)
            pool.memset(tri_lt[:, :], 1.0).then_inc(s_const, 1)
            pool.iota(iota[:, :], pattern=[[1, P]], base=0, channel_multiplier=0,
                      allow_small_or_imprecise_dtypes=True).then_inc(s_const, 1)
            pool.iota(inv_count[:, :, :], pattern=[[0, 2], [1, T]], base=1, channel_multiplier=0,
                      allow_small_or_imprecise_dtypes=True).then_inc(s_const, 1)
            pool.wait_ge(s_const, 7)
            pool.affine_select(out=ident[:, :], in_=ident[:, :], compare_op=ALU.not_equal, fill=1.0,
                               base=0, pattern=[[-1, P]], channel_multiplier=1).then_inc(s_const, 1)
            pool.affine_select(out=tri_le[:, :], in_=tri_le[:, :], compare_op=ALU.is_ge, fill=0.0,
                               base=0, pattern=[[1, P]], channel_multiplier=-1).then_inc(s_const, 1)
            pool.affine_select(out=tri_ge[:, :], in_=tri_ge[:, :], compare_op=ALU.is_ge, fill=0.0,
                               base=0, pattern=[[-1, P]], channel_multiplier=1).then_inc(s_const, 1)
            pool.affine_select(out=tri_lt[:, :], in_=tri_lt[:, :], compare_op=ALU.is_gt, fill=0.0,
                               base=0, pattern=[[1, P]], channel_multiplier=-1).then_inc(s_const, 1)

        @block.scalar
        def _(act):
            steps = Steps(act, s_act)

            def hi(l, half, s, n=None):
                act.wait_ge(s_raw[s], (l * (STREAM // 2) + half + 1) * 16)
                if n is not None:
                    act.wait_ge(s_tile, l * STREAM + n + 1)
                nc.scalar.activation(w_hi[s][:, :, :].rearrange("p a b -> p (a b)"), w_raw[:, s, :],
                                     ACT.Copy).then_inc(s_wh, 1)

            def norm_squares(gate_sem, gate_val):
                act.wait_ge(gate_sem, gate_val)
                for q in range(2):
                    ins = nc.scalar.activation(h32[:, 4 * q:4 * q + 4, :], x[:, 4 * q:4 * q + 4, :], ACT.Square)
                ins.then_inc(s_sq, 1)

            def root(sem_in, val, src, dst, sem_out):
                act.wait_ge(sem_in, val)
                nc.scalar.activation(dst, src, ACT.Sqrt).then_inc(sem_out, 1)

            def rhs_hi(sem_in, val):
                act.wait_ge(sem_in, val)
                for q in range(2):
                    ins = nc.scalar.activation(hH[:, 4 * q:4 * q + 4, :], h32[:, 4 * q:4 * q + 4, :], ACT.Copy)
                ins.then_inc(s_hh, 1)

            act.wait_ge(s_in, 48)
            nc.scalar.activation(tiny[:, 0, 0:KT], cond[:, :], ACT.Silu).then_inc(s_cond, 1)

            with act.Fori(0, LAYERS) as l:
                steps.base, steps.n = l * ACT_STEPS, 0
                hi(l, 0, 0)
                hi(l, 0, 1)
                norm_squares(s_gate, l + 1)
                root(s_var, l * 2 + 1, nrm[:, 0, :], nrm[:, 1, :], s_root)
                rhs_hi(s_h32, l * 2 + 1)
                act.wait_ge(s_dt1, l + 1)
                nc.scalar.activation(tiny[:, 3, :], tiny[:, 2, :], ACT.Exp)
                nc.scalar.activation(tiny[:, 4, 0:HEADS], pcol("a_log"), ACT.Exp).then_inc(s_dt2, 1)
                act.wait_ge(s_dt3, l + 1)
                nc.scalar.activation(tiny[:, 6, :], tiny[:, 5, :], ACT.Ln).then_inc(s_dt4, 1)
                with act.Fori(0, N_IN // 2) as i:
                    for s in range(2):
                        hi(l, i + 1, s, i * 2 + s)
                        nc.scalar.activation(pj[:, i * 2 + s, PAD:PJW], bank[s][:, :], ACT.Copy).then_inc(s_taken, 1)
                act.wait_ge(s_acv, l + 1)
                nc.scalar.activation(tiny[:, 9, :], tiny[:, 8, :], ACT.Exp)
                nc.scalar.activation(tiny[:, 11, :], tiny[:, 10, :], ACT.Exp)
                nc.scalar.activation(tiny[:, 13, :], tiny[:, 12, :], ACT.Exp).then_inc(s_dec, 1)
                for j in range(6):
                    act.wait_ge(s_conv, l * 6 + j + 1)
                    nc.scalar.activation(xbc[:, j, :], xbc[:, j, :], ACT.Silu).then_inc(s_xbc, 1)
                act.wait_ge(s_taken, l * STREAM + N_IN + 2)
                for j in range(4):
                    ins = nc.scalar.activation(pj[:, Z0 + j, PAD:PJW], pj[:, Z0 + j, PAD:PJW], ACT.Silu)
                ins.then_inc(s_zs, 1)
                for tt in range(NT):
                    for g in range(2):
                        act.wait_ge(s_seg, l * 8 + tt * 2 + g + 1)
                        nc.scalar.activation(seg[:, g, :], seg[:, g, :], ACT.Exp).then_inc(s_exp, 1)
                act.wait_ge(s_ygv, l * 4 + 4)
                nc.scalar.activation(y_tok[:, :, :], xbc[:, 0:4, :], ACT.Square).then_inc(s_ysq, 1)
                root(s_yvar, l * 2 + 1, nrm[:, 0, :], nrm[:, 1, :], s_yroot)
                root(s_yvar, l * 2 + 2, nrm[:, 0, :], nrm[:, 1, :], s_yroot)
                for h in range(SB_HEADS):
                    act.wait_ge(s_zv, l * 4 + h + 1)
                    steps.link(nc.scalar.activation(ez[:, :], zs[:, :], ACT.Abs))
                    steps.link(nc.scalar.activation(ez[:, :], ez[:, :], ACT.Exp, scale=-1.0))
                    nc.scalar.activation(ez[:, :], ez[:, :], ACT.Ln, bias=ones[:, 0:1]).then_inc(s_lg, 1)
                    act.wait_ge(s_arg, l * 4 + h + 1)
                    nc.scalar.activation(arg[:, :], arg[:, :], ACT.Exp).then_inc(s_w, 1)
                rhs_hi(s_ayv, l * 4 + 4)
                with act.Fori(0, N_OUT // 2) as i:
                    for s in range(2):
                        hi(l, i + (OUT0 // 2 + 1), s, i * 2 + (OUT0 + s))
                norm_squares(s_taken, l * STREAM + WQ0 + 2)
                root(s_var, l * 2 + 2, nrm[:, 0, :], nrm[:, 1, :], s_root)
                rhs_hi(s_h32, l * 2 + 2)
                with act.Fori(0, N_Q // 2) as i:
                    for s in range(2):
                        hi(l, i + (WQ0 // 2 + 1), s, i * 2 + (WQ0 + s))
                        act.wait_ge(s_sc, l * N_Q + i * 2 + s + 1)
                        nc.scalar.activation(qT[:, s, :], bank[s][:, :], ACT.Copy).then_inc(s_taken, 1)
                with act.Fori(0, NT) as tt:
                    act.wait_ge(s_shift, l * NT + tt + 1)
                    nc.scalar.activation(bestv[:, :, :], bestv[:, :, :], ACT.Exp).then_inc(s_gexp, 1)
                    act.wait_ge(s_rtt, l * NT + tt + 1)
                    nc.scalar.activation(idxT[:, :, bass.ds(tt * P, P)],
                                         bank[2][:, 0:3 * P].rearrange("p (a b) -> p a b", a=3),
                                         ACT.Copy).then_inc(s_idx, 1)
                def store_chunk(c2, s, first):
                    if not first:
                        act.wait_ge(s_gst[s], (l * (GCHUNKS // 2) + c2) * 16)
                    with act.Fori(0, GCHUNK // QUAD // 2) as j:
                        for u in range(2):
                            act.wait_ge(s_gm, l * QUADS + c2 * (2 * GCHUNK // QUAD) + j * 2 + (s * (GCHUNK // QUAD) + u + 3))
                            nc.scalar.activation(
                                stage[s][:, :, bass.ds(j * 2 * QUAD + u * QUAD, QUAD)].rearrange("p e t -> p t e"),
                                bank[2 + u][:, :].rearrange("p (t e) -> p t e", t=QUAD),
                                ACT.Copy).then_inc(s_gv, 1)
                    act.wait_ge(s_gv, l * QUADS + c2 * (2 * GCHUNK // QUAD) + ((s + 1) * (GCHUNK // QUAD)) + 2)
                    act.dma_start(g_dram[c2 * 2 + s].rearrange("p e t -> p (e t)"),
                                  stage[s][:, :, :].rearrange("p e t -> p (e t)")).then_inc(s_gst[s], 16)

                store_chunk(0, 0, True)
                store_chunk(0, 1, True)
                with act.Fori(1, GCHUNKS // 2) as c2:
                    store_chunk(c2, 0, False)
                    store_chunk(c2, 1, False)

                def u_phase(g, s, split_v=True, tail=False):
                    for j in range(GROUP):
                        if not (tail and j >= 2):
                            hi(l, g * (GROUP // 2) + (U0 // 2 + j // 2 + 1), j % 2, g * GROUP + (U0 + j))
                        else:
                            act.wait_ge(s_tile, l * STREAM + g * GROUP + (U0 + j + 1))
                        act.wait_ge(s_coef, l * N_U + g * GROUP + (j + 1))
                        nc.scalar.activation(act_g[:, j % 2, :], bank[j % 2][:, :], ACT.Gelu).then_inc(s_taken, 1)
                        if split_v:
                            if j == 0:
                                act.wait_ge(s_vin, (l * GROUPS + g) * 16)
                                act.wait_ge(s_out, l * OUTS + (g - 1) * KT + 1)
                            nc.scalar.activation(v_hi[:, j, :], v_raw[:, j, :], ACT.Copy).then_inc(s_vh, 1)

                for s in range(2):
                    act.wait_ge(s_gst[s], (l * (GCHUNKS // 2) + GCHUNKS // 2) * 16)
                u_phase(0, 0, split_v=False)
                with act.Fori(0, GROUPS // 2 - 1) as i:
                    u_phase(i * 2 + 1, 1)
                    u_phase(i * 2 + 2, 0)
                u_phase(GROUPS - 1, 1, tail=True)
                act.wait_ge(s_vin, (l * GROUPS + GROUPS) * 16)
                act.wait_ge(s_out, l * OUTS + (GROUPS - 1) * KT + 1)
                for j in range(GROUP):
                    nc.scalar.activation(v_hi[:, j, :], v_raw[:, j, :], ACT.Copy).then_inc(s_vh, 1)
                assert steps.n == ACT_STEPS, steps.n
            norm_squares(s_gate, LAYERS + 1)
            root(s_var, LAYERS * 2 + 1, nrm[:, 0, :], nrm[:, 1, :], s_root)

        @block.tensor
        def _(pe):
            mm = nc.tensor.matmul
            steps = Steps(pe, None, s_pset)

            def project(l, n, s):
                pe.wait_ge(s_wh, l * STREAM + n + 1)
                pe.wait_ge(s_wl, l * STREAM + n + 1)
                pe.wait_ge(s_taken, l * STREAM + n + 1)
                for k in range(KT):
                    for a, b in ((w_hi, hH), (w_hi, hL), (w_lo, hH)):
                        last = mm(bank[s][:, :], a[s][:, k, :], b[:, k, :],
                                  start=(k == 0 and a is w_hi and b is hH),
                                  stop=(k == KT - 1 and a is w_lo))
                last.then_inc(s_tile, 1)

            def norm_sum(val):
                pe.wait_ge(s_sq, val)
                for k in range(KT):
                    last = mm(bank[2][:, :], ones[:, :], h32[:, k, :], start=(k == 0), stop=(k == KT - 1))
                last.then_inc(s_ssum, 1)

            pe.sem_inc(s_taken, 2)
            pe.sem_inc(s_scv, 2)
            pe.sem_inc(s_sc, 2)
            pe.sem_inc(s_gv, 2)
            pe.sem_inc(s_gm, 2)
            pe.sem_inc(s_out, 1)
            pe.sem_inc(s_coef, 2)
            pe.sem_inc(s_add, 4)
            pe.wait_ge(s_const, 11)
            pe.wait_ge(s_cond, 1)

            with pe.Fori(0, LAYERS) as l:
                norm_sum(l * 2 + 1)
                for c in range(ADA_CHUNKS):
                    pe.wait_ge(s_ada[c % 2], (l * (ADA_CHUNKS // 2) + c // 2 + 1) * 16)
                    for j in range(ADA_TILES):
                        col = c * ADA_TILES + j
                        for k in range(KT):
                            last = mm(bank[3][:, col:col + 1], ada_buf[:, c % 2, k, j * P:(j + 1) * P],
                                      tiny[:, 0, k:k + 1], start=(k == 0), stop=(k == KT - 1))
                    last.then_inc(s_adau, 1)
                pe.wait_ge(s_h32, l * 2 + 1)
                w_dt = pcol("w_dt").rearrange("p (k h) -> p k h", k=KT)
                for tt in range(NT):
                    for k in range(KT):
                        last = mm(bank[4][:, tt * HEADS:(tt + 1) * HEADS], h32[:, k, tt * P:(tt + 1) * P],
                                  w_dt[:, k, :], start=(k == 0), stop=(k == KT - 1))
                last.then_inc(s_dtm, 1)
                pe.wait_ge(s_rhs, l * 3 + 1)
                steps.settle()
                with pe.Fori(0, N_IN // 2) as i:
                    for s in range(2):
                        project(l, i * 2 + s, s)
                pe.wait_ge(s_dta, l + 1)
                mm(bank[5][:, 0:32], tri_le[:, :], tiny[:, 7, :], start=True, stop=True)
                mm(bank[5][:, 32:64], ones[:, :], tiny[:, 7, :], start=True, stop=True).then_inc(s_acs, 1)
                pe.wait_ge(s_xbc, l * 6 + 6)
                for tt in range(NT):
                    if tt >= 2:
                        pe.wait_ge(s_trv, l * 5 + tt - 1)
                    for j in range(4):
                        last = nc.tensor.transpose(bank[2 + tt % 2][:, j * P:(j + 1) * P],
                                                   xbc[:, j, tt * P:(tt + 1) * P], ident[:, :])
                    last.then_inc(s_tr, 1)
                for tt in range(NT):
                    last = nc.tensor.transpose(bank[4][:, tt * P:(tt + 1) * P],
                                               xbc[:, 4, tt * P:(tt + 1) * P], ident[:, :])
                last.then_inc(s_tr, 1)
                pe.wait_ge(s_acv, l + 1)
                for g in range(2):
                    r = slice(64 * g, 64 * g + 64)
                    for tt in range(NT):
                        t = slice(tt * P, (tt + 1) * P)
                        last = mm(bank[5 + g][:, t], xbc[r, 4, t], xbc[r, 5, t], start=True, stop=True)
                    last.then_inc(s_cb, 1)
                dta = tiny[:, 7, :].rearrange("p (t h) -> p t h", t=NT)

                def decay_rows(tt, g):
                    for h in range(4):
                        last = mm(bank[7 if g == 0 else 2][:, h * P:(h + 1) * P],
                                  dta[:, tt, 4 * g + h:4 * g + h + 1].broadcast_to([P, P]), tri_le[:, :],
                                  start=True, stop=True)
                    last.then_inc(s_r, 1)

                pe.wait_ge(s_trv, l * 5 + 5)
                for tt in range(NT):
                    for g in range(2):
                        if tt >= 1:
                            pe.wait_ge(s_seg, l * 8 + tt * 2 + g - 1)
                        decay_rows(tt, g)
                    if tt == 0:
                        pe.wait_ge(s_cbv, l * 2 + 2)
                    else:
                        pe.wait_ge(s_yv, l * NT + tt)
                    for g in range(2):
                        pe.wait_ge(s_sm, l * 8 + tt * 2 + g + 1)
                        for h in range(4):
                            hh = 4 * g + h
                            last = mm(bank[3][:, hh * HD:(hh + 1) * HD], smat[:, g, h * P:(h + 1) * P],
                                      xdt[:, tt, hh * HD:(hh + 1) * HD], start=True, stop=True)
                    if tt >= 1:
                        pe.wait_ge(s_st, l * 3 + tt)
                        for g in range(2):
                            r = slice(64 * g, 64 * g + 64)
                            last = mm(bank[4 + 2 * g][:, 0:256], xbc[r, 5, tt * P:(tt + 1) * P],
                                      state[r, :], start=True, stop=True)
                    if tt < NT - 1:
                        pe.wait_ge(s_xdd, l * 3 + tt + 1)
                        for g in range(2):
                            r = slice(64 * g, 64 * g + 64)
                            last = mm(bank[5][r, 0:256], b_tok[:, tt, r], xdd[:, g * 256:(g + 1) * 256],
                                      start=True, stop=True)
                    last.then_inc(s_y, 1)
                pe.wait_ge(s_yv, l * NT + NT)
                pe.wait_ge(s_seg, l * 8 + 8)
                for j in range(4):
                    b = (2, 3, 4, 5)[j]
                    for tt in range(NT):
                        last = nc.tensor.transpose(bank[b][:, tt * P:(tt + 1) * P],
                                                   y_tok[:, tt, j * P:(j + 1) * P], ident[:, :])
                    last.then_inc(s_yt, 1)
                pe.wait_ge(s_ysq, l + 1)
                for g in range(2):
                    for k in range(2):
                        last = mm(bank[6 + g][:, :], ones[:, :], y_tok[:, 2 * g + k, :], start=(k == 0), stop=(k == 1))
                    last.then_inc(s_yss, 1)
                pe.wait_ge(s_pool, l + 1)
                pw = pcol("pool_w").rearrange("p (j c) -> p j c", j=2)
                for j in range(2):
                    mm(bank[2 + j][:, :], pw[:, j, :], pooled[:, j, :], start=True, stop=True).then_inc(s_pm, 1)
                for j in range(2):
                    for tt in range(NT):
                        last = nc.tensor.transpose(bank[4 + j][:, tt * P:(tt + 1) * P],
                                                   pj[:, V0 + j, PAD + tt * P:PAD + (tt + 1) * P], ident[:, :])
                last.then_inc(s_vt, 1)
                pe.wait_ge(s_vtv, l + 1)
                zb = [(2, 0), (3, 0), (4, 0), (4, 256)]
                cb = [(5, 0), (6, 0), (7, 0), (7, 256)]
                for h in range(SB_HEADS):
                    r = slice(64 * (h % 2), 64 * (h % 2) + 64)
                    for i in range(NT):
                        b, o = zb[i]
                        last = mm(bank[b][:, o:o + W4[i]], pj[r, K0 + h // 2, PAD + i * P:PAD + (i + 1) * P],
                                  pj[r, Q0 + h // 2, PAD + i * P:PJW], start=True, stop=True)
                    last.then_inc(s_z, 1)
                    pe.wait_ge(s_nlk, l * 4 + h + 1)
                    for i in range(NT):
                        b, o = cb[i]
                        for j in range(i, NT):
                            last = mm(bank[b][:, o + (j - i) * P:o + W4[i]], tri_ge[:, :] if j == i else ones[:, :],
                                      nlk[:, O4[j]:O4[j] + W4[j]], start=(j == i), stop=(j == NT - 1))
                    last.then_inc(s_cum, 1)
                    pe.wait_ge(s_wm, l * 4 + h + 1)
                    for i in range(NT):
                        last = mm(bank[2][r, i * P:T], v_tok[:, i, h * HD:(h + 1) * HD], arg[:, O4[i]:O4[i] + W4[i]],
                                  start=(i == 0), stop=(i == NT - 1))
                    last.then_inc(s_ay, 1)
                    pe.wait_ge(s_ayv, l * 4 + h + 1)
                pe.wait_ge(s_rhs, l * 3 + 2)
                steps.settle()
                with pe.Fori(0, N_OUT // 2) as i:
                    for s in range(2):
                        project(l, i * 2 + (OUT0 + s), s)
                norm_sum(l * 2 + 2)
                pe.wait_ge(s_rhs, l * 3 + 3)
                pe.wait_ge(s_keys, (l + 1) * 16)
                steps.settle()
                with pe.Fori(0, N_Q // 2) as i:
                    for s in range(2):
                        project(l, i * 2 + (WQ0 + s), s)
                        pe.wait_ge(s_taken, l * STREAM + i * 2 + (WQ0 + s + 3))
                        pe.wait_ge(s_scv, l * N_Q + i * 2 + (s + 1))
                        for tt in range(NT):
                            last = mm(bank[2 + s][:, tt * P:(tt + 1) * P], qT[:, s, tt * P:(tt + 1) * P],
                                      keys[:, bass.ds(i * 2 + s, 1), :].rearrange("p a b -> p (a b)"),
                                      start=True, stop=True)
                        last.then_inc(s_sc, 1)
                pe.wait_ge(s_scv, l * N_Q + N_Q + 2)
                steps.settle()
                with pe.Fori(0, NT) as tt:
                    pe.wait_ge(s_rt, l * NT + tt + 1)
                    for a in range(3):
                        last = nc.tensor.transpose(bank[2][:, a * P:(a + 1) * P], route[:, a, :], ident[:, :])
                    last.then_inc(s_rtt, 1)
                pe.wait_ge(s_idx, l * NT + NT)
                steps.settle()
                with pe.Fori(0, QUADS // 2) as i:
                    for u in range(2):
                        pe.wait_ge(s_oh, l * QUADS + i * 2 + (u + 1))
                        pe.wait_ge(s_gv, l * QUADS + i * 2 + (u + 1))
                        for q in range(QUAD):
                            last = mm(bank[2 + u][:, q * P:(q + 1) * P], oneh[:, u, q, :], gateh[:, u, q, :],
                                      start=True, stop=True)
                        last.then_inc(s_gm, 1)

                def first_product(g):
                    for j in range(GROUP):
                        project(l, g * GROUP + (U0 + j), j % 2)

                def second_product(g, s):
                    pe.wait_ge(s_vh, l * N_U + g * GROUP + GROUP)
                    pe.wait_ge(s_vl, l * N_U + g * GROUP + GROUP)
                    pe.wait_ge(s_coef, l * N_U + g * GROUP + (GROUP + 2))
                    for k in range(KT):
                        pe.wait_ge(s_add, l * OUTS + g * KT + (k + 1))
                        kk = slice(k * P, (k + 1) * P)
                        for b in range(GROUP):
                            for v, c in ((v_hi, c_hi), (v_hi, c_lo), (v_lo, c_hi)):
                                last = mm(bank[2 + k % 4][:, :], v[:, b, kk], c[s][:, b, :],
                                          start=(b == 0 and v is v_hi and c is c_hi),
                                          stop=(b == GROUP - 1 and v is v_lo))
                        last.then_inc(s_out, 1)

                first_product(0)
                with pe.Fori(0, GROUPS // 2 - 1) as i:
                    first_product(i * 2 + 1)
                    second_product(i * 2, 0)
                    first_product(i * 2 + 2)
                    second_product(i * 2 + 1, 1)
                first_product(GROUPS - 1)
                second_product(GROUPS - 2, 0)
                second_product(GROUPS - 1, 1)
            norm_sum(LAYERS * 2 + 1)

        @block.vector
        def _(dve):
            steps = Steps(dve, s_dve, s_dset)
            link = steps.link
            v = nc.vector

            def lo(l, half, s, n=None):
                if n is not None:
                    dve.wait_ge(s_tile, l * STREAM + n + 1)
                dve.wait_ge(s_wh, l * STREAM + half * 2 + (s + 1))
                v.tensor_tensor(w_lo[s][:, :, :].rearrange("p a b -> p (a b)"), w_raw[:, s, :],
                                w_hi[s][:, :, :].rearrange("p a b -> p (a b)").bitcast(F32),
                                ALU.subtract).then_inc(s_wl, 1)

            def inv_root(psum, count, sem_var, sem_root, root_val):
                v.tensor_scalar(nrm[:, 0, :], psum, 1.0 / count, EPS, ALU.mult, ALU.add).then_inc(sem_var, 1)
                dve.wait_ge(sem_root, root_val)
                link(v.reciprocal(nrm[:, 2, :], nrm[:, 1, :]))
                link(v.tensor_tensor(nrm[:, 3, :], nrm[:, 2, :], nrm[:, 2, :], ALU.mult))
                link(v.tensor_tensor(nrm[:, 3, :], nrm[:, 3, :], nrm[:, 0, :], ALU.mult))
                link(v.tensor_scalar(nrm[:, 3, :], nrm[:, 3, :], -0.5, 1.5, ALU.mult, ALU.add))
                link(v.tensor_tensor(nrm[:, 2, :], nrm[:, 2, :], nrm[:, 3, :], ALU.mult))

            def normed(l, which):
                dve.wait_ge(s_ssum, l * 2 + which + 1)
                inv_root(bank[2][:, :], D, s_var, s_root, l * 2 + which + 1)
                link(v.tensor_tensor(h32[:, :, :], x[:, :, :],
                                     nrm[:, 2, :].unsqueeze(1).broadcast_to([P, KT, T]), ALU.mult))

            def modulated(which):
                for k in range(KT):
                    ins = v.tensor_scalar(h32[:, k, :], h32[:, k, :], gs[:, which, k:k + 1],
                                          mod[:, 3 * which, k:k + 1], ALU.mult, ALU.add)
                ins.then_inc(s_h32, 1)

            def rhs_lo(l, which):
                dve.wait_ge(s_hh, l * 3 + which)
                v.tensor_tensor(hL[:, :, :], h32[:, :, :], hH[:, :, :].bitcast(F32),
                                ALU.subtract).then_inc(s_rhs, 1)

            dve.wait_ge(s_const, 11)
            for j, p0, w in ((0, 0, 2), (0, 64, 4), (1, 0, 8), (1, 64, 16)):
                ins = v.tensor_scalar(inv_count[p0:p0 + 64, j, :], inv_count[p0:p0 + 64, j, :], float(w), None, ALU.min)
            ins.then_inc(s_const, 1)
            dve.wait_ge(s_const, 12)
            v.reciprocal(inv_count[:, :, :], inv_count[:, :, :]).then_inc(s_const, 1)
            dve.wait_ge(s_const, 13)
            dve.wait_ge(s_in, 48)
            v.memset(tiny[:, 15, 0:1], 0.0).then_inc(s_gate, 1)

            with dve.Fori(0, LAYERS) as l:
                steps.base, steps.n = l * DVE_STEPS, 0
                lo(l, 0, 0)
                lo(l, 0, 1)
                dve.wait_ge(s_par, (l + 1) * 16)
                v.memset(pj[:, :, 0:PAD], 0.0)
                normed(l, 0)
                dve.wait_ge(s_adau, l * ADA_CHUNKS + ADA_CHUNKS)
                link(v.tensor_tensor(mod[:, :, :].rearrange("p a b -> p (a b)"), bank[3][:, 0:48], pcol("ada_b"), ALU.add))
                for w, name in ((0, "g_mix"), (1, "g_ffn")):
                    ins = v.scalar_tensor_tensor(gs[:, w, :], mod[:, 3 * w + 1, :], 1.0, pcol(name), ALU.add, ALU.mult)
                link(ins)
                modulated(0)
                rhs_lo(l, 1)
                dve.wait_ge(s_dtm, l + 1)
                q = lambda n: tiny[:, n, :]
                bias = pcol("dt_bias").unsqueeze(1).broadcast_to([P, NT, HEADS])
                link(v.tensor_tensor(q(1).rearrange("p (t h) -> p t h", t=NT),
                                     bank[4][:, 0:32].rearrange("p (t h) -> p t h", t=NT), bias, ALU.add))
                v.scalar_tensor_tensor(q(2), q(1), -1.0, q(1), ALU.mult, ALU.min).then_inc(s_dt1, 1)
                dve.wait_ge(s_dt2, l + 1)
                v.tensor_scalar(q(5), q(3), 1.0, None, ALU.add).then_inc(s_dt3, 1)
                dve.wait_ge(s_dt4, l + 1)
                link(v.tensor_scalar(q(14), q(5), -1.0, None, ALU.add))
                link(v.tensor_scalar(q(15), q(14), 0.0, None, ALU.is_equal))
                link(v.tensor_tensor(q(14), q(14), q(15), ALU.add))
                link(v.tensor_tensor(q(15), q(6), q(15), ALU.add))
                link(v.reciprocal(q(14), q(14)))
                link(v.tensor_tensor(q(15), q(15), q(14), ALU.mult))
                link(v.tensor_tensor(q(15), q(15), q(3), ALU.mult))
                link(v.scalar_tensor_tensor(q(1), q(1), 0.0, q(15), ALU.max, ALU.add))
                ea = tiny[:, 4, 0:HEADS].unsqueeze(1).broadcast_to([P, NT, HEADS])
                v.scalar_tensor_tensor(q(7).rearrange("p (t h) -> p t h", t=NT),
                                       q(1).rearrange("p (t h) -> p t h", t=NT), -1.0, ea,
                                       ALU.mult, ALU.mult).then_inc(s_dta, 1)
                with dve.Fori(0, N_IN // 2) as i:
                    for s in range(2):
                        lo(l, i + 1, s, i * 2 + s)
                dve.wait_ge(s_acs, l + 1)
                link(v.tensor_copy(q(8), bank[5][:, 0:32]))
                v.tensor_copy(q(12), bank[5][:, 32:64])
                v.tensor_tensor(q(10), bank[5][:, 32:64], q(8), ALU.subtract).then_inc(s_acv, 1)
                dve.wait_ge(s_taken, l * STREAM + N_IN + 2)
                cw = pcol("conv_w").rearrange("p (j w) -> p j w", j=6)
                for j in range(6):
                    src = lambda w: pj[:, XS0 + j, PAD - 3 + w:PJW - 3 + w]
                    link(v.tensor_scalar(xbc[:, j, :], src(0), cw[:, j, 0:1], pcol("conv_b")[:, j:j + 1],
                                         ALU.mult, ALU.add))
                    for w in (1, 2):
                        link(v.scalar_tensor_tensor(xbc[:, j, :], src(w), cw[:, j, w:w + 1], xbc[:, j, :],
                                                    ALU.mult, ALU.add))
                    v.scalar_tensor_tensor(xbc[:, j, :], src(3), cw[:, j, 3:4], xbc[:, j, :],
                                           ALU.mult, ALU.add).then_inc(s_conv, 1)
                def by_head(n, tt):
                    return tiny[:, n, tt * HEADS:(tt + 1) * HEADS].unsqueeze(2).broadcast_to([P, HEADS, HD])

                def heads(ap):
                    return ap.rearrange("p (h c) -> p h c", c=HD)

                for tt in range(NT):
                    dve.wait_ge(s_tr, l * 5 + tt + 1)
                    v.tensor_tensor(heads(xdt[:, tt, :]), heads(bank[2 + tt % 2][:, :]), by_head(1, tt),
                                    ALU.mult).then_inc(s_trv, 1)
                dve.wait_ge(s_tr, l * 5 + 5)
                v.tensor_copy(b_tok[:, :, :].rearrange("p a b -> p (a b)"), bank[4][:, :]).then_inc(s_trv, 1)
                for g in range(2):
                    dve.wait_ge(s_cb, l * 2 + g + 1)
                    v.tensor_tensor(cbm[:, g, :, :], bank[5 + g][:, :].rearrange("p (t c) -> p t c", t=NT),
                                    tri_le[:, :].unsqueeze(1).broadcast_to([P, NT, P]), ALU.mult).then_inc(s_cbv, 1)
                dve.wait_ge(s_dec, l + 1)
                dve.wait_ge(s_trv, l * 5 + 5)
                dve.wait_ge(s_cbv, l * 2 + 2)
                for tt in range(NT):
                    for g in range(2):
                        dve.wait_ge(s_r, l * 8 + tt * 2 + g + 1)
                        if tt >= 1:
                            dve.wait_ge(s_sm, l * 8 + tt * 2 + g - 1)
                        sums = tiny[:, 8, tt * HEADS + 4 * g:tt * HEADS + 4 * g + 4].unsqueeze(2).broadcast_to([P, 4, P])
                        link(v.tensor_tensor(seg[:, g, :].rearrange("p (h c) -> p h c", h=4),
                                             bank[7 if g == 0 else 2][:, :].rearrange("p (h c) -> p h c", h=4),
                                             sums, ALU.subtract))
                        v.tensor_scalar(seg[:, g, :], seg[:, g, :], 0.0, None, ALU.min).then_inc(s_seg, 1)
                    if tt < NT - 1:
                        if tt >= 1:
                            dve.wait_ge(s_y, l * NT + tt)
                        v.tensor_tensor(heads(xdd[:, :]), heads(xdt[:, tt, :]), by_head(11, tt), ALU.mult).then_inc(s_xdd, 1)
                    for g in range(2):
                        dve.wait_ge(s_exp, l * 8 + tt * 2 + g + 1)
                        if tt >= 1:
                            dve.wait_ge(s_y, l * NT + tt)
                        v.tensor_tensor(smat[:, g, :].rearrange("p (h c) -> p h c", h=4),
                                        seg[:, g, :].rearrange("p (h c) -> p h c", h=4),
                                        cbm[:, g, tt, :].unsqueeze(1).broadcast_to([P, 4, P]), ALU.mult).then_inc(s_sm, 1)
                    dve.wait_ge(s_y, l * NT + tt + 1)
                    if tt < NT - 1:
                        for g in range(2):
                            r = slice(64 * g, 64 * g + 64)
                            st = state[r, :].rearrange("p (h c) -> p h c", c=HD)
                            gain = bank[5][r, 0:256].rearrange("p (h c) -> p h c", c=HD)
                            if tt == 0:
                                ins = v.tensor_copy(st, gain)
                            else:
                                total = tiny[r, 13, tt * HEADS + 4 * g:tt * HEADS + 4 * g + 4].unsqueeze(2).broadcast_to([64, 4, HD])
                                link(v.tensor_tensor(st, st, total, ALU.mult))
                                ins = v.tensor_tensor(st, st, gain, ALU.add)
                            if g == 1:
                                ins.then_inc(s_st, 1)
                    if tt == 0:
                        v.tensor_copy(y_tok[:, tt, :], bank[3][:, :]).then_inc(s_yv, 1)
                    else:
                        for g in range(2):
                            ins = v.tensor_tensor(heads(y_tok[:, tt, g * 256:(g + 1) * 256]), heads(bank[4 + 2 * g][:, 0:256]),
                                                  by_head(9, tt)[:, 4 * g:4 * g + 4, :], ALU.mult)
                        link(ins)
                        v.tensor_tensor(y_tok[:, tt, :], y_tok[:, tt, :], bank[3][:, :], ALU.add).then_inc(s_yv, 1)
                dve.wait_ge(s_zs, l + 1)
                for j in range(4):
                    dve.wait_ge(s_yt, l * 4 + j + 1)
                    link(v.scalar_tensor_tensor(xbc[:, j, :], xbc[:, j, :], pcol("d_skip")[:, j:j + 1],
                                                bank[2 + j][:, :], ALU.mult, ALU.add))
                    v.tensor_tensor(xbc[:, j, :], xbc[:, j, :], pj[:, Z0 + j, PAD:PJW], ALU.mult).then_inc(s_ygv, 1)
                for g in range(2):
                    dve.wait_ge(s_yss, l * 2 + g + 1)
                    inv_root(bank[6 + g][:, :], 2 * P, s_yvar, s_yroot, l * 2 + g + 1)
                    for j in (2 * g, 2 * g + 1):
                        ins = v.scalar_tensor_tensor(mixed[:, j, :], xbc[:, j, :], pcol("ssd_g")[:, j:j + 1],
                                                     nrm[:, 2, :], ALU.mult, ALU.mult)
                    link(ins)
                xp = pj[:, XP0:XP0 + 2, :]
                link(v.tensor_tensor(pool_a[:, :, 1:], xp[:, :, 1:], xp[:, :, :PJW - 1], ALU.add))
                link(v.tensor_tensor(pool_b[:, :, 3:], pool_a[:, :, 3:], pool_a[:, :, 1:PJW - 2], ALU.add))
                for p0, j, src in ((0, 0, pool_a), (64, 0, pool_b)):
                    v.tensor_tensor(pooled[p0:p0 + 64, j, :], src[p0:p0 + 64, j, PAD:], inv_count[p0:p0 + 64, j, :], ALU.mult)
                link(v.tensor_tensor(pool_c[:, 1, 7:], pool_b[:, 1, 7:], pool_b[:, 1, 3:PJW - 4], ALU.add))
                link(v.tensor_tensor(pool_a[:, 1, 15:], pool_c[:, 1, 15:], pool_c[:, 1, 7:PJW - 8], ALU.add))
                for p0, j, src in ((0, 1, pool_c), (64, 1, pool_a)):
                    ins = v.tensor_tensor(pooled[p0:p0 + 64, j, :], src[p0:p0 + 64, j, PAD:], inv_count[p0:p0 + 64, j, :], ALU.mult)
                link(ins)
                v.tensor_tensor(pooled[:, :, :], pooled[:, :, :], xp[:, :, PAD:], ALU.subtract).then_inc(s_pool, 1)
                for j in range(2):
                    dve.wait_ge(s_pm, l * 2 + j + 1)
                    ins = v.tensor_scalar(mixed[:, 4 + j, :], bank[2 + j][:, :], pcol("pool_scale")[:, j:j + 1], None, ALU.mult)
                link(ins)
                dve.wait_ge(s_vt, l + 1)
                for j in range(2):
                    ins = v.tensor_copy(v_tok[:, :, j * P:(j + 1) * P], bank[4 + j][:, :].rearrange("p (t c) -> p t c", t=NT))
                ins.then_inc(s_vtv, 1)
                for h in range(SB_HEADS):
                    r = slice(64 * (h % 2), 64 * (h % 2) + 64)
                    dve.wait_ge(s_z, l * 4 + h + 1)
                    for b, n, o in ((2, 512, 0), (3, 384, 512), (4, 384, 896)):
                        ins = v.tensor_scalar(zs[:, o:o + n], bank[b][:, 0:n], HD ** -0.5, None, ALU.mult)
                    ins.then_inc(s_zv, 1)
                    dve.wait_ge(s_lg, l * 4 + h + 1)
                    link(v.scalar_tensor_tensor(nlk[:, :], zs[:, :], 0.0, ez[:, :], ALU.max, ALU.add))
                    for i in range(NT):
                        ins = v.tensor_tensor(nlk[:, O4[i]:O4[i] + P], nlk[:, O4[i]:O4[i] + P], tri_lt[:, :], ALU.mult)
                    ins.then_inc(s_nlk, 1)
                    dve.wait_ge(s_cum, l * 4 + h + 1)
                    for b, n, o in ((5, 512, 0), (6, 384, 512), (7, 384, 896)):
                        ins = v.tensor_tensor(arg[:, o:o + n], zs[:, o:o + n], bank[b][:, 0:n], ALU.subtract)
                    link(ins)
                    for i in range(NT):
                        ins = v.tensor_scalar(arg[:, O4[i]:O4[i] + P], arg[:, O4[i]:O4[i] + P], 0.0, None, ALU.min)
                    ins.then_inc(s_arg, 1)
                    dve.wait_ge(s_w, l * 4 + h + 1)
                    for i in range(NT):
                        ins = v.tensor_tensor(arg[:, O4[i]:O4[i] + P], arg[:, O4[i]:O4[i] + P], tri_lt[:, :], ALU.mult)
                    ins.then_inc(s_wm, 1)
                    dve.wait_ge(s_ay, l * 4 + h + 1)
                    v.tensor_copy(mixed[r, 6 + h // 2, :], bank[2][r, :]).then_inc(s_ayv, 1)
                rhs_lo(l, 2)
                with dve.Fori(0, N_OUT // 2) as i:
                    for s in range(2):
                        lo(l, i + (OUT0 // 2 + 1), s, i * 2 + (OUT0 + s))
                        k = i * 2 + s
                        xk = x[:, bass.ds(k, 1), :].rearrange("p a t -> p (a t)")
                        v.scalar_tensor_tensor(xk, bank[s][:, :], mod[:, 2, bass.ds(k, 1)], xk,
                                               ALU.mult, ALU.add).then_inc(s_taken, 1)
                normed(l, 1)
                modulated(1)
                rhs_lo(l, 3)
                with dve.Fori(0, N_Q // 2) as i:
                    with steps.loop(i, N_Q // 2, 2 * 5):
                        for s in range(2):
                            lo(l, i + (WQ0 // 2 + 1), s, i * 2 + (WQ0 + s))
                            dve.wait_ge(s_sc, l * N_Q + i * 2 + (s + 3))
                            steps.settle()
                            sc = lambda tt: bank[2 + s][:, tt * P:(tt + 1) * P]
                            each = lambda f: [f(tt) for tt in range(NT)][-1]
                            link(each(lambda tt: v.max(v16[:, tt, 0:8], sc(tt))))
                            steps.settle()
                            each(lambda tt: v.max_index(i16[:, tt, 0:8], v16[:, tt, 0:8], sc(tt)))
                            ins = each(lambda tt: v.match_replace(sc2[:, tt, :], v16[:, tt, 0:8], sc(tt), -3.0e38))
                            ins.then_inc(s_scv, 1)
                            dve.wait_ge(s_scv, l * N_Q + i * 2 + (s + 3))
                            steps.settle()
                            link(each(lambda tt: v.max(v16[:, tt, 8:16], sc2[:, tt, :])))
                            steps.settle()
                            link(each(lambda tt: v.max_index(i16[:, tt, 8:16], v16[:, tt, 8:16], sc2[:, tt, :])))
                            link(v.tensor_copy(topv[:, :, bass.ds(i * 2 + s, 1), :].rearrange("p t a k -> p t (a k)"), v16[:, :, :]))
                            link(v.tensor_copy(topi[:, :, bass.ds(i * 2 + s, 1), :].rearrange("p t a k -> p t (a k)"), i16[:, :, :]))
                with dve.Fori(0, NT) as tt:
                    with steps.loop(tt, NT, 16):
                        tv = topv[:, bass.ds(tt, 1), :, :].rearrange("p t (h i) k -> p (t h) i k", i=2)
                        ti = topi[:, bass.ds(tt, 1), :, :].rearrange("p t (h i) k -> p (t h) i k", i=2)
                        full = [P, PH, TOPK, TOPK]
                        link(v.tensor_tensor(cand[:, :, :].rearrange("p h (a b) -> p h a b", a=TOPK),
                                             tv[:, :, 0, :].unsqueeze(3).broadcast_to(full),
                                             tv[:, :, 1, :].unsqueeze(2).broadcast_to(full), ALU.add))
                        steps.settle()
                        each = lambda f: [f(h) for h in range(PH)][-1]
                        link(each(lambda h: v.max(bestv[:, h, 0:8], cand[:, h, :])))
                        steps.settle()
                        each(lambda h: v.max_index(bestp[:, h, 0:8], bestv[:, h, 0:8], cand[:, h, :]))
                        link(each(lambda h: v.match_replace(cand2[:, h, :], bestv[:, h, 0:8], cand[:, h, :], -3.0e38)))
                        steps.settle()
                        link(each(lambda h: v.max(bestv[:, h, 8:16], cand2[:, h, :])))
                        steps.settle()
                        link(each(lambda h: v.max_index(bestp[:, h, 8:16], bestv[:, h, 8:16], cand2[:, h, :])))
                        flat = bestp[:, :, :].rearrange("p h k -> p (h k)")
                        v.tensor_scalar(posu[:, 0, :], flat, 4, None, ALU.logical_shift_right)
                        link(v.tensor_scalar(posu[:, 1, :], flat, 15, None, ALU.bitwise_and))
                        link(v.tensor_copy(gsum[:, 0, :], bestv[:, :, 0]))
                        v.tensor_tensor(bestv[:, :, :], bestv[:, :, :],
                                        gsum[:, 0, :].unsqueeze(2).broadcast_to([P, PH, TOPK]),
                                        ALU.subtract).then_inc(s_shift, 1)
                        link(v.tensor_copy(posf[:, :, :], posu[:, :, :]))
                        for a in range(2):
                            pk = pick[:, :, :]
                            link(v.tensor_tensor(pk, posf[:, a, :].unsqueeze(2).broadcast_to([P, HK, TOPK]),
                                                 iota[:, 0:TOPK].unsqueeze(1).broadcast_to([P, HK, TOPK]), ALU.is_equal))
                            pk4 = pick[:, :, :].rearrange("p (h k) j -> p h k j", h=PH)
                            link(v.tensor_tensor(pk4, pk4, ti[:, :, a, :].unsqueeze(2).broadcast_to(full), ALU.mult))
                            link(v.reduce_sum(route[:, a, :], pk, AX.X))
                        dve.wait_ge(s_gexp, l * NT + tt + 1)
                        link(v.reduce_sum(gsum[:, 0, :], bestv[:, :, :], AX.X))
                        link(v.reciprocal(gsum[:, 1, :], gsum[:, 0, :]))
                        v.tensor_tensor(route[:, 2, :].rearrange("p (h k) -> p h k", h=PH), bestv[:, :, :],
                                        gsum[:, 1, :].unsqueeze(2).broadcast_to([P, PH, TOPK]),
                                        ALU.mult).then_inc(s_rt, 1)
                        dve.wait_ge(s_idx, l * NT + tt + 1)
                with dve.Fori(0, QUADS // 2) as i:
                    for u in range(2):
                        dve.wait_ge(s_gm, l * QUADS + i * 2 + (u + 1))
                        for q_ in range(QUAD):
                            t = i * (2 * QUAD) + (u * QUAD + q_)
                            v.tensor_scalar(oneh[:, u, q_, :], iota[:, :], idxT[:, 0, bass.ds(t, 1)], None, ALU.is_equal)
                            ins = v.tensor_scalar(gateh[:, u, q_, :], iota[:, :], idxT[:, 1, bass.ds(t, 1)],
                                                  idxT[:, 2, bass.ds(t, 1)], ALU.is_equal, ALU.mult)
                        ins.then_inc(s_oh, 1)

                def lo_v(g, j):
                    dve.wait_ge(s_vh, l * N_U + g * GROUP + (j + 1))
                    v.tensor_tensor(v_lo[:, j, :], v_raw[:, j, :], v_hi[:, j, :].bitcast(F32),
                                    ALU.subtract).then_inc(s_vl, 1)

                def u_phase(gi, s, split_v=True, tail=False):
                    g = gi * 2 + s
                    for j in range(GROUP):
                        if not (tail and j >= 2):
                            lo(l, g * (GROUP // 2) + (U0 // 2 + j // 2 + 1), j % 2, g * GROUP + (U0 + j))
                        if j == 0:
                            dve.wait_ge(s_gin[s], (l * (GROUPS // 2) + gi + 1) * 16)
                        dve.wait_ge(s_taken, l * STREAM + g * GROUP + (U0 + j + 3))
                        link(v.tensor_tensor(coef[:, j % 2, :].rearrange("p (c t) -> p c t", c=GCHUNKS),
                                             act_g[:, j % 2, :].rearrange("p (c t) -> p c t", c=GCHUNKS),
                                             gates[s][:, :, j, :], ALU.mult))
                        link(v.tensor_copy(c_hi[s][:, j, :], coef[:, j % 2, :]))
                        v.tensor_tensor(c_lo[s][:, j, :], coef[:, j % 2, :], c_hi[s][:, j, :].bitcast(F32),
                                        ALU.subtract).then_inc(s_coef, 1)
                        if split_v:
                            lo_v(g - 1, j)

                def v_phase(g):
                    for k in range(KT):
                        dve.wait_ge(s_out, l * OUTS + g * KT + (k + 2))
                        v.scalar_tensor_tensor(x[:, k, :], bank[2 + k % 4][:, :], mod[:, 5, k:k + 1], x[:, k, :],
                                               ALU.mult, ALU.add).then_inc(s_add, 1)

                U_STEPS = 2 * GROUP
                u_phase(0, 0, split_v=False)
                with dve.Fori(0, GROUPS // 2 - 1) as i:
                    with steps.loop(i, GROUPS // 2 - 1, 2 * U_STEPS):
                        u_phase(i, 1)
                        v_phase(i * 2)
                        u_phase(i + 1, 0)
                        v_phase(i * 2 + 1)
                u_phase(GROUPS // 2 - 1, 1, tail=True)
                v_phase(GROUPS - 2)
                for j in range(GROUP):
                    lo_v(GROUPS - 1, j)
                v_phase(GROUPS - 1)
                dve.wait_ge(s_add, l * OUTS + (OUTS + 4))
                v.memset(tiny[:, 15, 0:1], 0.0).then_inc(s_gate, 1)
                assert steps.n == DVE_STEPS, steps.n
            steps.base, steps.n = LAYERS * DVE_STEPS, 0
            normed(LAYERS, 0)
            for k in range(KT):
                ins = v.tensor_scalar(x[:, k, :], h32[:, k, :], fin_g[:, k:k + 1], None, ALU.mult)
            ins.then_inc(s_fin, 1)


def kernel(**inputs):
    import numpy as np
    import concourse.bacc as bacc
    from concourse.bass_utils import run_bass_kernel_spmd

    a = {k: np.asarray(v) for k, v in inputs.items()}
    L = LAYERS

    def cols(v, n=KT):
        return v.reshape(L, n, P).transpose(0, 2, 1)

    def tiles(w):
        return w.reshape(L, KT, P, -1, P).transpose(0, 3, 2, 1, 4)

    w_in = a["w_in"]
    dt0 = 1280
    w_cols = np.concatenate([w_in[:, :, :dt0], w_in[:, :, dt0 + HEADS:]], axis=2)
    w_dt = w_in[:, :, dt0:dt0 + HEADS].reshape(L, KT, P, HEADS).transpose(0, 2, 1, 3).reshape(L, P, KT * HEADS)
    u = a["peer_u"].reshape(L, N_KEYS, N_KEYS, KT, P).transpose(0, 2, 4, 3, 1)
    stream = np.concatenate([tiles(w_cols), tiles(a["w_out"]), tiles(a["peer_wq"]), u], axis=1).reshape(L, STREAM, P, D)
    vt = a["peer_v"].reshape(L, N_KEYS, GROUPS, GROUP, D).transpose(0, 2, 1, 3, 4)
    ada = a["ada_w"].reshape(L, KT, P, ADA_CHUNKS, ADA_CHUNK).transpose(0, 3, 2, 1, 4)
    pw = np.zeros((L, 2, P, P), np.float32)
    for j in range(4):
        o = 64 * (j % 2)
        pw[:, j // 2, o:o + 64, o:o + 64] = a["pool_w"][:, j]
    wide = lambda v: np.broadcast_to(v[:, None, :], (L, P, HEADS))
    packed = {
        "ada_b": cols(a["ada_b"], 48), "g_mix": cols(a["mix_norm_g"]), "g_ffn": cols(a["ffn_norm_g"]),
        "conv_w": a["conv_w"].reshape(L, 4, 6, P).transpose(0, 3, 2, 1).reshape(L, P, 24),
        "conv_b": cols(a["conv_b"], 6), "ssd_g": cols(a["ssd_norm_g"], 4), "pool_scale": cols(a["pool_scale"], 2),
        "d_skip": cols(np.repeat(a["d_skip"], HD, axis=1), 4), "dt_bias": wide(a["dt_bias"]), "a_log": wide(a["a_log"]),
        "w_dt": w_dt, "pool_w": pw.transpose(0, 2, 1, 3).reshape(L, P, 2 * P),
    }
    arrays = {
        "xT": a["x"][0].T.reshape(KT, P, T).transpose(1, 0, 2),
        "cT": a["c"][0].reshape(KT, P).T,
        "final_g": a["final_norm_g"].reshape(KT, P).T,
        "adaw": ada, "wst": stream, "vst": vt,
        "params": np.concatenate([packed[n] for n, _ in PARAMS], axis=2),
        "keysT": a["peer_keys"].transpose(0, 4, 1, 2, 3).reshape(L, P, SEGS, N_KEYS),
    }
    arrays = {k: np.ascontiguousarray(v) for k, v in arrays.items()}
    nc = bacc.Bacc("TRN2", target_bir_lowering=False, num_devices=1)
    aps = [nc.dram_tensor(k, v.shape, F32, kind="ExternalInput").ap() for k, v in arrays.items()]
    g_dram = nc.dram_tensor("gate_matrices", (GCHUNKS, P, N_KEYS, GCHUNK), F32).ap()
    out = nc.dram_tensor("outT", (P, KT, T), F32, kind="ExternalOutput").ap()
    build(nc, *aps, g_dram, out)
    r = run_bass_kernel_spmd(nc, [arrays], core_ids=[0])
    got = r.results[0]["outT"]
    return got.transpose(2, 1, 0).reshape(1, T, D)
```

```python
from contextlib import ExitStack, contextmanager

import concourse.bass as bass
from concourse import mybir

F32 = mybir.dt.float32
F32R = mybir.dt.float32r
U32 = mybir.dt.uint32
ALU = mybir.AluOpType
ACT = mybir.ActivationFunctionType
AX = mybir.AxisListType

P = 128
LAYERS = 2
D = 1024
KT = D // P
T = 512
NT = T // P
EPS = 1e-6

HEADS = 8
HD = 64
SB_HEADS = 4

Z0, XS0, B0, C0, XP0, Q0, K0, V0 = 0, 4, 8, 9, 10, 12, 14, 16
N_IN = 18
N_OUT = KT
N_Q = 16
N_KEYS = 128
OUT0 = N_IN
WQ0 = OUT0 + N_OUT
U0 = WQ0 + N_Q
EV0 = U0 + N_KEYS
STREAM = EV0 + N_KEYS
TAKEN = EV0
assert EV0 % 2 == 0 and U0 % 2 == 0 and WQ0 % 2 == 0 and OUT0 % 2 == 0

PAD = 16
PJW = PAD + T

ADA_CHUNK = 512
ADA_CHUNKS = 6 * D // ADA_CHUNK
ADA_TILES = ADA_CHUNK // P

SEGS = 16
PH = 8
TOPK = 16
HK = PH * TOPK
assert HK == P

GROUP = 4
GROUPS = N_KEYS // GROUP
GCHUNK = 64
GCHUNKS = T // GCHUNK
QUAD = 4
QUADS = T // QUAD
G_PICK = 3
G_GATE0 = NT * G_PICK
TILE_QUADS = 2
G_GATE = QUADS // (TILE_QUADS * GROUP)
G_REST0 = G_GATE0 + G_GATE
G_CHUNK = GCHUNK // (QUAD * TILE_QUADS * GROUP)
assert G_REST0 + 2 <= GROUPS

PARAMS = [("ada_b", 48), ("g_mix", KT), ("g_ffn", KT), ("conv_w", 24), ("conv_b", 6), ("ssd_g", 4),
          ("pool_scale", 2), ("d_skip", 4), ("dt_bias", HEADS), ("a_log", HEADS),
          ("w_dt", KT * HEADS), ("pool_w", 2 * P)]
PCOL = {}
_c = 0
for _n, _w in PARAMS:
    PCOL[_n] = (_c, _w)
    _c += _w
NPAR = _c

DVE_STEPS = 495
ACT_STEPS = 8


class Steps:

    def __init__(self, eng, sem, settled=None):
        self.eng, self.sem, self.settled, self.base, self.n = eng, sem, settled, 0, 0

    def settle(self):
        self.eng.sem_inc(self.settled, 1)

    def link(self, ins):
        ins.then_inc(self.sem, 1)
        self.n += 1
        self.eng.wait_ge(self.sem, self.base + self.n)

    @contextmanager
    def loop(self, i, times, per):
        base, n = self.base, self.n
        self.base, self.n = base + n + i * per, 0
        yield
        assert self.n == per, (self.n, per)
        self.base, self.n = base, n + times * per


def build(nc, xT, cT, final_g, adaw, wst, params, keysT, g_dram, a_dram, outT):
    ctx = ExitStack()
    with ctx:
        def sb(name, shape, dt=F32, where=ctx):
            return where.enter_context(nc.sbuf_tensor(name, shape, dt))

        def sem(name):
            return ctx.enter_context(nc.semaphore(name))

        ident = sb("ident", [P, P])
        tri_le = sb("tri_le", [P, P])
        tri_ge = sb("tri_ge", [P, P])
        tri_lt = sb("tri_lt", [P, P])
        ones = sb("ones", [P, P])
        iota = sb("iota", [P, P])
        inv_count = sb("inv_count", [P, 2, T])
        x = sb("x", [P, KT, T])
        cond = sb("cond", [P, KT])
        fin_g = sb("fin_g", [P, KT])
        par = sb("par", [P, NPAR])
        mod = sb("mod", [P, 6, KT])
        gs = sb("gs", [P, 2, KT])
        hH = sb("hH", [P, KT, T], F32R)
        hL = sb("hL", [P, KT, T], F32R)
        w_raw = sb("w_raw", [P, 2, D])
        w_hi = [sb(f"w_hi{s}", [P, KT, P], F32R) for s in range(2)]
        w_lo = [sb(f"w_lo{s}", [P, KT, P], F32R) for s in range(2)]
        tiny = sb("tiny", [P, 16, 32])

        def pcol(name, n=None):
            a, w = PCOL[name]
            return par[:, a:a + w]

        mixer = ExitStack()
        pj = sb("pj", [P, N_IN, PJW], where=mixer)
        h32 = sb("h32", [P, KT, T], where=mixer)
        nrm = sb("nrm", [P, 4, T], where=mixer)
        ada_stack = ExitStack()
        ada_buf = sb("ada_buf", [P, 2, KT, ADA_CHUNK], where=ada_stack)
        ada_stack.close()
        scan = ExitStack()
        xbc = sb("xbc", [P, 6, T], where=scan)
        xdt = sb("xdt", [P, NT, T], where=scan)
        y_tok = sb("y_tok", [P, NT, T], where=scan)
        xdd = sb("xdd", [P, T], where=scan)
        b_tok = sb("b_tok", [P, NT, P], where=scan)
        cbm = sb("cbm", [P, 2, NT, P], where=scan)
        state = sb("state", [P, 4 * HD], where=scan)
        seg = sb("seg", [P, 2, T], where=scan)
        smat = sb("smat", [P, 2, T], where=scan)
        scan.close()
        W4 = [T - P * i for i in range(NT)]
        O4 = [sum(W4[:i]) for i in range(NT)]
        WA = sum(W4)
        v_tok = sb("v_tok", [P, NT, 2 * P], where=mixer)
        zs = sb("zs", [P, WA], where=mixer)
        ez = sb("ez", [P, WA], where=mixer)
        nlk = sb("nlk", [P, WA], where=mixer)
        arg = sb("arg", [P, WA], where=mixer)
        pool_a = sb("pool_a", [P, 2, PJW], where=mixer)
        pool_b = sb("pool_b", [P, 2, PJW], where=mixer)
        pool_c = sb("pool_c", [P, 2, PJW], where=mixer)
        pooled = sb("pooled", [P, 2, T], where=mixer)
        mixer.close()
        mixed = h32

        router = ExitStack()
        sb("r_pad", [P, N_IN * PJW], where=router)
        sb("r_h32", [P, KT * T], where=router)
        sb("r_nrm", [P, 4 * T], where=router)
        keys = sb("keys", [P, SEGS, N_KEYS], where=router)
        qT = sb("qT", [P, 2, T], where=router)
        idxT = sb("idxT", [P, 3, T], where=router)
        topv = sb("topv", [P, NT, SEGS, TOPK], where=router)
        topi = sb("topi", [P, NT, SEGS, TOPK], where=router)
        act_out = sb("act_out", [P, 2, 2, T], where=router)
        router.close()
        r2 = ExitStack()
        v16 = sb("v16", [P, NT, TOPK], where=r2)
        i16 = sb("i16", [P, NT, TOPK], U32, where=r2)
        sc2 = sb("sc2", [P, NT, N_KEYS], where=r2)
        cand = sb("cand", [P, PH, TOPK * TOPK], where=r2)
        cand2 = sb("cand2", [P, PH, TOPK * TOPK], where=r2)
        bestv = sb("bestv", [P, PH, TOPK], where=r2)
        bestp = sb("bestp", [P, PH, TOPK], U32, where=r2)
        posu = sb("posu", [P, 2, HK], U32, where=r2)
        posf = sb("posf", [P, 2, HK], where=r2)
        pick = sb("pick", [P, HK, TOPK], where=r2)
        route = sb("route", [P, 3, HK], where=r2)
        gsum = sb("gsum", [P, 2, PH], where=r2)
        r2.close()
        r3 = ExitStack()
        oneh = sb("oneh", [P, 2, QUAD, P], where=r3)
        gateh = sb("gateh", [P, 2, QUAD, P], where=r3)
        stage = [sb(f"stage{s}", [P, N_KEYS, GCHUNK], where=r3) for s in range(2)]
        r3.close()

        ex = ExitStack()
        gates = [sb(f"gates{s}", [P, GCHUNKS, GROUP, GCHUNK], where=ex) for s in range(2)]
        act_in = [sb(f"act_in{s}", [P, 2, 2, T], where=ex) for s in range(2)]
        coef = sb("coef", [P, 2, T], where=ex)
        c_hi = sb("c_hi", [P, GROUP, T], F32R, where=ex)
        c_lo = sb("c_lo", [P, GROUP, T], F32R, where=ex)
        ex.close()

        bank = [ctx.enter_context(nc.psum_tensor(f"bank{i}", [P, T], F32)) for i in range(8)]

        s_const = sem("const_ready")
        s_in = sem("inputs_in")
        s_cond = sem("cond_ready")
        s_gate = sem("layer_may_start")
        s_par = sem("params_in")
        s_keys = sem("keys_in")
        s_ada = [sem(f"ada_in{s}") for s in range(2)]
        s_adau = sem("ada_used")
        s_mod = sem("mod_ready")
        s_raw = [sem(f"w_raw_in{s}") for s in range(2)]
        s_wh = sem("w_hi_ready")
        s_wl = sem("w_lo_ready")
        s_tile = sem("tile_done")
        s_taken = sem("tile_taken")
        s_sq = sem("squares_ready")
        s_ssum = sem("square_sum_done")
        s_var = sem("variance_ready")
        s_root = sem("root_ready")
        s_h32 = sem("normed_ready")
        s_hh = sem("rhs_hi_ready")
        s_rhs = sem("rhs_ready")
        s_dve = sem("dve_steps")
        s_act = sem("act_steps")
        s_dset = sem("dve_waits_settled")
        s_pset = sem("pe_waits_settled")
        s_dtm = sem("dt_done")
        s_dt1 = sem("dt_abs_ready")
        s_dt2 = sem("dt_exp_ready")
        s_dt3 = sem("dt_one_plus_ready")
        s_dt4 = sem("dt_log_ready")
        s_dta = sem("dta_ready")
        s_acs = sem("decay_sums_done")
        s_acv = sem("decay_diffs_ready")
        s_dec = sem("decays_ready")
        s_conv = sem("conv_ready")
        s_xbc = sem("xbc_ready")
        s_tr = sem("transposes_done")
        s_trv = sem("transposes_taken")
        s_cb = sem("cb_done")
        s_cbv = sem("cb_taken")
        s_r = sem("decay_rows_done")
        s_seg = sem("segments_ready")
        s_exp = sem("segment_exp_ready")
        s_sm = sem("scan_matrix_ready")
        s_xdd = sem("decayed_x_ready")
        s_y = sem("y_done")
        s_yv = sem("y_taken")
        s_st = sem("state_ready")
        s_yt = sem("y_transposed")
        s_ygv = sem("y_gated")
        s_zs = sem("z_silu_ready")
        s_ysq = sem("y_squares_ready")
        s_yss = sem("y_square_sum_done")
        s_yvar = sem("y_variance_ready")
        s_yroot = sem("y_root_ready")
        s_pool = sem("pooled_ready")
        s_pm = sem("pool_mixed_done")
        s_vt = sem("v_tokens_done")
        s_vtv = sem("v_tokens_ready")
        s_z = sem("att_scores_done")
        s_zv = sem("att_scores_ready")
        s_lg = sem("att_log_ready")
        s_nlk = sem("att_keep_ready")
        s_cum = sem("att_sums_done")
        s_arg = sem("att_exponent_ready")
        s_w = sem("att_exp_ready")
        s_wm = sem("att_weights_ready")
        s_ay = sem("att_out_done")
        s_ayv = sem("att_out_taken")
        s_sc = sem("key_scores_done")
        s_scv = sem("key_scores_taken")
        s_shift = sem("gate_exponent_ready")
        s_gexp = sem("gate_exp_ready")
        s_rt = sem("route_ready")
        s_rtt = sem("route_transposed")
        s_idx = sem("route_rows_ready")
        s_oh = sem("one_hots_ready")
        s_gm = sem("gate_matrices_done")
        s_gv = sem("gate_matrices_taken")
        s_gst = [sem(f"gates_stored{s}") for s in range(2)]
        s_gin = [sem(f"gates_in{s}") for s in range(2)]
        s_ast = [sem(f"act_stored{s}") for s in range(2)]
        s_ain = [sem(f"act_in{s}") for s in range(2)]
        s_coef = sem("coef_ready")
        s_out = sem("out_sum_done")
        s_fin = sem("result_ready")
        s_ret = sem("result_stored")

        block = ctx.enter_context(nc.Block())
        @block.sync
        def _(sp):
            sp.dma_start(x[:, :, :], xT).then_inc(s_in, 16)
            sp.dma_start(cond[:, :], cT).then_inc(s_in, 16)
            sp.dma_start(fin_g[:, :], final_g).then_inc(s_in, 16)

            def load_w(l, n, s):
                sp.dma_start(w_raw[:, s, :], wst[l, n]).then_inc(s_raw[s], 16)

            def next_w(l, n, s):
                sp.wait_ge(s_wh, l * STREAM + n + 1)
                sp.wait_ge(s_wl, l * STREAM + n + 1)
                load_w(l, n + 2, s)

            def store_act(l, p, s):
                sp.wait_ge(s_taken, l * TAKEN + p * 2 + (U0 + 4))
                sp.dma_start(a_dram[p], act_out[:, s, :, :]).then_inc(s_ast[s], 16)

            def load_group(l, g, h, s):
                for q in range(2):
                    sp.wait_ge(s_ast[q], (l * GROUPS + g + 2) * 16)
                sp.dma_start(act_in[s][:, :, :, :], a_dram[bass.ds(g * 2, 2)].rearrange("q p b t -> p q b t")
                             ).then_inc(s_ain[s], 16)
                sp.dma_start(gates[s][:, :, :, :],
                             g_dram[:, :, bass.ds(g * GROUP, GROUP), :].rearrange("c p b t -> p c b t")
                             ).then_inc(s_gin[s], 16)

            with sp.Fori(0, LAYERS) as l:
                sp.wait_ge(s_gate, l + 1)
                sp.dma_start(par[:, :], params[l]).then_inc(s_par, 16)
                load_w(l, 0, 0)
                load_w(l, 1, 1)
                for c in range(ADA_CHUNKS):
                    if c >= 2:
                        sp.wait_ge(s_adau, l * ADA_CHUNKS + c - 1)
                    sp.dma_start(ada_buf[:, c % 2, :, :], adaw[l, c]).then_inc(s_ada[c % 2], 16)
                with sp.Fori(0, OUT0 // 2) as i:
                    for s in range(2):
                        next_w(l, i * 2 + s, s)
                with sp.Fori(0, N_OUT // 2) as i:
                    for s in range(2):
                        next_w(l, i * 2 + OUT0 + s, s)
                sp.wait_ge(s_rhs, l * 3 + 2)
                sp.dma_start(keys[:, :, :], keysT[l]).then_inc(s_keys, 16)
                with sp.Fori(0, N_Q // 2) as i:
                    for s in range(2):
                        next_w(l, i * 2 + WQ0 + s, s)
                def groups(first, times):
                    with sp.Fori(first, first + times) as g:
                        for s in range(2):
                            for j in range(2):
                                next_w(l, g * GROUP + (U0 + 2 + 2 * s + j), j)
                            store_act(l, g * 2 + s, s)

                next_w(l, U0, 0)
                next_w(l, U0 + 1, 1)
                groups(0, GROUPS - 2)
                for s in range(2):
                    sp.wait_ge(s_gst[s], (l * (GCHUNKS // 2) + GCHUNKS // 2) * 16)
                for s in range(2):
                    load_group(l, s, 0, s)
                groups(GROUPS - 2, 1)
                for j in range(2):
                    next_w(l, (EV0 - 2) + j, j)
                store_act(l, N_KEYS // 2 - 2, 0)
                store_act(l, N_KEYS // 2 - 1, 1)
                with sp.Fori(0, GROUPS // 2 - 1) as h:
                    for s in range(2):
                        for j in range(GROUP):
                            next_w(l, h * (2 * GROUP) + (EV0 + s * GROUP + j), j % 2)
                        sp.wait_ge(s_coef, l * N_KEYS + h * (2 * GROUP) + (s * GROUP + GROUP))
                        load_group(l, h * 2 + (2 + s), h + 1, s)
                for j in range(2 * GROUP - 2):
                    next_w(l, (STREAM - 2 * GROUP) + j, j % 2)
            sp.wait_ge(s_fin, 1)
            sp.dma_start(outT, x[:, :, :]).then_inc(s_ret, 16)
            sp.wait_ge(s_ret, 16)

        @block.gpsimd
        def _(pool):
            pool.memset(ones[:, :], 1.0).then_inc(s_const, 1)
            pool.memset(ident[:, :], 0.0).then_inc(s_const, 1)
            pool.memset(tri_le[:, :], 1.0).then_inc(s_const, 1)
            pool.memset(tri_ge[:, :], 1.0).then_inc(s_const, 1)
            pool.memset(tri_lt[:, :], 1.0).then_inc(s_const, 1)
            pool.iota(iota[:, :], pattern=[[1, P]], base=0, channel_multiplier=0,
                      allow_small_or_imprecise_dtypes=True).then_inc(s_const, 1)
            pool.iota(inv_count[:, :, :], pattern=[[0, 2], [1, T]], base=1, channel_multiplier=0,
                      allow_small_or_imprecise_dtypes=True).then_inc(s_const, 1)
            pool.wait_ge(s_const, 7)
            pool.affine_select(out=ident[:, :], in_=ident[:, :], compare_op=ALU.not_equal, fill=1.0,
                               base=0, pattern=[[-1, P]], channel_multiplier=1).then_inc(s_const, 1)
            pool.affine_select(out=tri_le[:, :], in_=tri_le[:, :], compare_op=ALU.is_ge, fill=0.0,
                               base=0, pattern=[[1, P]], channel_multiplier=-1).then_inc(s_const, 1)
            pool.affine_select(out=tri_ge[:, :], in_=tri_ge[:, :], compare_op=ALU.is_ge, fill=0.0,
                               base=0, pattern=[[-1, P]], channel_multiplier=1).then_inc(s_const, 1)
            pool.affine_select(out=tri_lt[:, :], in_=tri_lt[:, :], compare_op=ALU.is_gt, fill=0.0,
                               base=0, pattern=[[1, P]], channel_multiplier=-1).then_inc(s_const, 1)

        @block.scalar
        def _(act):
            steps = Steps(act, s_act)

            def hi(l, half, s, n=None):
                act.wait_ge(s_raw[s], (l * (STREAM // 2) + half + 1) * 16)
                if n is not None:
                    act.wait_ge(s_tile, l * STREAM + n + 1)
                nc.scalar.activation(w_hi[s][:, :, :].rearrange("p a b -> p (a b)"), w_raw[:, s, :],
                                     ACT.Copy).then_inc(s_wh, 1)

            def norm_squares(gate_sem, gate_val):
                act.wait_ge(gate_sem, gate_val)
                for q in range(2):
                    ins = nc.scalar.activation(h32[:, 4 * q:4 * q + 4, :], x[:, 4 * q:4 * q + 4, :], ACT.Square)
                ins.then_inc(s_sq, 1)

            def root(sem_in, val, src, dst, sem_out):
                act.wait_ge(sem_in, val)
                nc.scalar.activation(dst, src, ACT.Sqrt).then_inc(sem_out, 1)

            def rhs_hi(sem_in, val):
                act.wait_ge(sem_in, val)
                for q in range(2):
                    ins = nc.scalar.activation(hH[:, 4 * q:4 * q + 4, :], h32[:, 4 * q:4 * q + 4, :], ACT.Copy)
                ins.then_inc(s_hh, 1)

            act.wait_ge(s_in, 48)
            nc.scalar.activation(tiny[:, 0, 0:KT], cond[:, :], ACT.Silu).then_inc(s_cond, 1)

            with act.Fori(0, LAYERS) as l:
                steps.base, steps.n = l * ACT_STEPS, 0
                hi(l, 0, 0)
                hi(l, 0, 1)
                norm_squares(s_gate, l + 1)
                root(s_var, l * 2 + 1, nrm[:, 0, :], nrm[:, 1, :], s_root)
                rhs_hi(s_h32, l * 2 + 1)
                act.wait_ge(s_dt1, l + 1)
                nc.scalar.activation(tiny[:, 3, :], tiny[:, 2, :], ACT.Exp)
                nc.scalar.activation(tiny[:, 4, 0:HEADS], pcol("a_log"), ACT.Exp).then_inc(s_dt2, 1)
                act.wait_ge(s_dt3, l + 1)
                nc.scalar.activation(tiny[:, 6, :], tiny[:, 5, :], ACT.Ln).then_inc(s_dt4, 1)
                with act.Fori(0, N_IN // 2) as i:
                    for s in range(2):
                        hi(l, i + 1, s, i * 2 + s)
                        nc.scalar.activation(pj[:, i * 2 + s, PAD:PJW], bank[s][:, :], ACT.Copy).then_inc(s_taken, 1)
                act.wait_ge(s_acv, l + 1)
                nc.scalar.activation(tiny[:, 9, :], tiny[:, 8, :], ACT.Exp)
                nc.scalar.activation(tiny[:, 11, :], tiny[:, 10, :], ACT.Exp)
                nc.scalar.activation(tiny[:, 13, :], tiny[:, 12, :], ACT.Exp).then_inc(s_dec, 1)
                for j in range(6):
                    act.wait_ge(s_conv, l * 6 + j + 1)
                    nc.scalar.activation(xbc[:, j, :], xbc[:, j, :], ACT.Silu).then_inc(s_xbc, 1)
                act.wait_ge(s_taken, l * TAKEN + N_IN + 2)
                for j in range(4):
                    ins = nc.scalar.activation(pj[:, Z0 + j, PAD:PJW], pj[:, Z0 + j, PAD:PJW], ACT.Silu)
                ins.then_inc(s_zs, 1)
                for tt in range(NT):
                    for g in range(2):
                        act.wait_ge(s_seg, l * 8 + tt * 2 + g + 1)
                        nc.scalar.activation(seg[:, g, :], seg[:, g, :], ACT.Exp).then_inc(s_exp, 1)
                act.wait_ge(s_ygv, l * 4 + 4)
                nc.scalar.activation(y_tok[:, :, :], xbc[:, 0:4, :], ACT.Square).then_inc(s_ysq, 1)
                root(s_yvar, l * 2 + 1, nrm[:, 0, :], nrm[:, 1, :], s_yroot)
                root(s_yvar, l * 2 + 2, nrm[:, 0, :], nrm[:, 1, :], s_yroot)
                for h in range(SB_HEADS):
                    act.wait_ge(s_zv, l * 4 + h + 1)
                    steps.link(nc.scalar.activation(ez[:, :], zs[:, :], ACT.Abs))
                    steps.link(nc.scalar.activation(ez[:, :], ez[:, :], ACT.Exp, scale=-1.0))
                    nc.scalar.activation(ez[:, :], ez[:, :], ACT.Ln, bias=ones[:, 0:1]).then_inc(s_lg, 1)
                    act.wait_ge(s_arg, l * 4 + h + 1)
                    nc.scalar.activation(arg[:, :], arg[:, :], ACT.Exp).then_inc(s_w, 1)
                rhs_hi(s_ayv, l * 4 + 4)
                with act.Fori(0, N_OUT // 2) as i:
                    for s in range(2):
                        hi(l, i + (OUT0 // 2 + 1), s, i * 2 + (OUT0 + s))
                norm_squares(s_taken, l * TAKEN + WQ0 + 2)
                root(s_var, l * 2 + 2, nrm[:, 0, :], nrm[:, 1, :], s_root)
                rhs_hi(s_h32, l * 2 + 2)
                with act.Fori(0, N_Q // 2) as i:
                    for s in range(2):
                        hi(l, i + (WQ0 // 2 + 1), s, i * 2 + (WQ0 + s))
                        act.wait_ge(s_sc, l * N_Q + i * 2 + s + 1)
                        nc.scalar.activation(qT[:, s, :], bank[s][:, :], ACT.Copy).then_inc(s_taken, 1)
                def u_block(g, j):
                    hi(l, g * (GROUP // 2) + (U0 // 2 + j // 2 + 1), j % 2, g * GROUP + (U0 + j))
                    if j % 2 == 0:
                        act.wait_ge(s_ast[j // 2], (l * GROUPS + g + 1) * 16)
                    nc.scalar.activation(act_out[:, j // 2, j % 2, :], bank[j % 2][:, :], ACT.Gelu).then_inc(s_taken, 1)

                with act.Fori(0, NT) as tt:
                    for m in range(G_PICK * GROUP):
                        u_block(tt * G_PICK + m // GROUP, m % GROUP)
                        if m == 6:
                            act.wait_ge(s_shift, l * NT + tt + 1)
                            nc.scalar.activation(bestv[:, :, :], bestv[:, :, :], ACT.Exp).then_inc(s_gexp, 1)
                    act.wait_ge(s_rtt, l * NT + tt + 1)
                    nc.scalar.activation(idxT[:, :, bass.ds(tt * P, P)],
                                         bank[2][:, 0:3 * P].rearrange("p (a b) -> p a b", a=3),
                                         ACT.Copy).then_inc(s_idx, 1)
                def store_chunk(c2, s, first):
                    if not first:
                        act.wait_ge(s_gst[s], (l * (GCHUNKS // 2) + c2) * 16)
                    with act.Fori(0, G_CHUNK) as i:
                        for j in range(GROUP):
                            u_block(c2 * (2 * G_CHUNK) + i + (G_GATE0 + s * G_CHUNK), j)
                            for u in range(TILE_QUADS):
                                q = i * (GROUP * TILE_QUADS) + (j * TILE_QUADS + u)
                                act.wait_ge(s_gm, l * QUADS + c2 * (2 * GCHUNK // QUAD) + (s * (GCHUNK // QUAD) + 3) + q)
                                nc.scalar.activation(
                                    stage[s][:, :, bass.ds(q * QUAD, QUAD)].rearrange("p e t -> p t e"),
                                    bank[2 + u][:, :].rearrange("p (t e) -> p t e", t=QUAD),
                                    ACT.Copy).then_inc(s_gv, 1)
                    act.wait_ge(s_gv, l * QUADS + c2 * (2 * GCHUNK // QUAD) + ((s + 1) * (GCHUNK // QUAD)) + 2)
                    act.dma_start(g_dram[c2 * 2 + s].rearrange("p e t -> p (e t)"),
                                  stage[s][:, :, :].rearrange("p e t -> p (e t)")).then_inc(s_gst[s], 16)

                store_chunk(0, 0, True)
                store_chunk(0, 1, True)
                with act.Fori(1, GCHUNKS // 2) as c2:
                    store_chunk(c2, 0, False)
                    store_chunk(c2, 1, False)

                with act.Fori(G_REST0, GROUPS) as g:
                    for j in range(GROUP):
                        u_block(g, j)
                with act.Fori(0, N_KEYS // 2 - 1) as i:
                    for s in range(2):
                        hi(l, i + (EV0 // 2 + 1), s, i * 2 + (EV0 + s))
                assert steps.n == ACT_STEPS, steps.n
            norm_squares(s_gate, LAYERS + 1)
            root(s_var, LAYERS * 2 + 1, nrm[:, 0, :], nrm[:, 1, :], s_root)

        @block.tensor
        def _(pe):
            mm = nc.tensor.matmul
            steps = Steps(pe, None, s_pset)

            def project(l, n, s):
                pe.wait_ge(s_wh, l * STREAM + n + 1)
                pe.wait_ge(s_wl, l * STREAM + n + 1)
                pe.wait_ge(s_taken, l * TAKEN + n + 1)
                for k in range(KT):
                    for a, b in ((w_hi, hH), (w_hi, hL), (w_lo, hH)):
                        last = mm(bank[s][:, :], a[s][:, k, :], b[:, k, :],
                                  start=(k == 0 and a is w_hi and b is hH),
                                  stop=(k == KT - 1 and a is w_lo))
                last.then_inc(s_tile, 1)

            def norm_sum(val):
                pe.wait_ge(s_sq, val)
                for k in range(KT):
                    last = mm(bank[2][:, :], ones[:, :], h32[:, k, :], start=(k == 0), stop=(k == KT - 1))
                last.then_inc(s_ssum, 1)

            pe.sem_inc(s_taken, 2)
            pe.sem_inc(s_scv, 2)
            pe.sem_inc(s_sc, 2)
            pe.sem_inc(s_gv, 2)
            pe.sem_inc(s_gm, 2)
            pe.sem_inc(s_ast[0], 16)
            pe.sem_inc(s_ast[1], 16)
            pe.wait_ge(s_const, 11)
            pe.wait_ge(s_cond, 1)

            with pe.Fori(0, LAYERS) as l:
                norm_sum(l * 2 + 1)
                for c in range(ADA_CHUNKS):
                    pe.wait_ge(s_ada[c % 2], (l * (ADA_CHUNKS // 2) + c // 2 + 1) * 16)
                    for j in range(ADA_TILES):
                        col = c * ADA_TILES + j
                        for k in range(KT):
                            last = mm(bank[3][:, col:col + 1], ada_buf[:, c % 2, k, j * P:(j + 1) * P],
                                      tiny[:, 0, k:k + 1], start=(k == 0), stop=(k == KT - 1))
                    last.then_inc(s_adau, 1)
                pe.wait_ge(s_h32, l * 2 + 1)
                w_dt = pcol("w_dt").rearrange("p (k h) -> p k h", k=KT)
                for tt in range(NT):
                    for k in range(KT):
                        last = mm(bank[4][:, tt * HEADS:(tt + 1) * HEADS], h32[:, k, tt * P:(tt + 1) * P],
                                  w_dt[:, k, :], start=(k == 0), stop=(k == KT - 1))
                last.then_inc(s_dtm, 1)
                pe.wait_ge(s_rhs, l * 3 + 1)
                steps.settle()
                with pe.Fori(0, N_IN // 2) as i:
                    for s in range(2):
                        project(l, i * 2 + s, s)
                pe.wait_ge(s_dta, l + 1)
                mm(bank[5][:, 0:32], tri_le[:, :], tiny[:, 7, :], start=True, stop=True)
                mm(bank[5][:, 32:64], ones[:, :], tiny[:, 7, :], start=True, stop=True).then_inc(s_acs, 1)
                pe.wait_ge(s_xbc, l * 6 + 6)
                for tt in range(NT):
                    if tt >= 2:
                        pe.wait_ge(s_trv, l * 5 + tt - 1)
                    for j in range(4):
                        last = nc.tensor.transpose(bank[2 + tt % 2][:, j * P:(j + 1) * P],
                                                   xbc[:, j, tt * P:(tt + 1) * P], ident[:, :])
                    last.then_inc(s_tr, 1)
                for tt in range(NT):
                    last = nc.tensor.transpose(bank[4][:, tt * P:(tt + 1) * P],
                                               xbc[:, 4, tt * P:(tt + 1) * P], ident[:, :])
                last.then_inc(s_tr, 1)
                pe.wait_ge(s_acv, l + 1)
                for g in range(2):
                    r = slice(64 * g, 64 * g + 64)
                    for tt in range(NT):
                        t = slice(tt * P, (tt + 1) * P)
                        last = mm(bank[5 + g][:, t], xbc[r, 4, t], xbc[r, 5, t], start=True, stop=True)
                    last.then_inc(s_cb, 1)
                dta = tiny[:, 7, :].rearrange("p (t h) -> p t h", t=NT)

                def decay_rows(tt, g):
                    for h in range(4):
                        last = mm(bank[7 if g == 0 else 2][:, h * P:(h + 1) * P],
                                  dta[:, tt, 4 * g + h:4 * g + h + 1].broadcast_to([P, P]), tri_le[:, :],
                                  start=True, stop=True)
                    last.then_inc(s_r, 1)

                pe.wait_ge(s_trv, l * 5 + 5)
                for tt in range(NT):
                    for g in range(2):
                        if tt >= 1:
                            pe.wait_ge(s_seg, l * 8 + tt * 2 + g - 1)
                        decay_rows(tt, g)
                    if tt == 0:
                        pe.wait_ge(s_cbv, l * 2 + 2)
                    else:
                        pe.wait_ge(s_yv, l * NT + tt)
                    for g in range(2):
                        pe.wait_ge(s_sm, l * 8 + tt * 2 + g + 1)
                        for h in range(4):
                            hh = 4 * g + h
                            last = mm(bank[3][:, hh * HD:(hh + 1) * HD], smat[:, g, h * P:(h + 1) * P],
                                      xdt[:, tt, hh * HD:(hh + 1) * HD], start=True, stop=True)
                    if tt >= 1:
                        pe.wait_ge(s_st, l * 3 + tt)
                        for g in range(2):
                            r = slice(64 * g, 64 * g + 64)
                            last = mm(bank[4 + 2 * g][:, 0:256], xbc[r, 5, tt * P:(tt + 1) * P],
                                      state[r, :], start=True, stop=True)
                    if tt < NT - 1:
                        pe.wait_ge(s_xdd, l * 3 + tt + 1)
                        for g in range(2):
                            r = slice(64 * g, 64 * g + 64)
                            last = mm(bank[5][r, 0:256], b_tok[:, tt, r], xdd[:, g * 256:(g + 1) * 256],
                                      start=True, stop=True)
                    last.then_inc(s_y, 1)
                pe.wait_ge(s_yv, l * NT + NT)
                pe.wait_ge(s_seg, l * 8 + 8)
                for j in range(4):
                    b = (2, 3, 4, 5)[j]
                    for tt in range(NT):
                        last = nc.tensor.transpose(bank[b][:, tt * P:(tt + 1) * P],
                                                   y_tok[:, tt, j * P:(j + 1) * P], ident[:, :])
                    last.then_inc(s_yt, 1)
                pe.wait_ge(s_ysq, l + 1)
                for g in range(2):
                    for k in range(2):
                        last = mm(bank[6 + g][:, :], ones[:, :], y_tok[:, 2 * g + k, :], start=(k == 0), stop=(k == 1))
                    last.then_inc(s_yss, 1)
                pe.wait_ge(s_pool, l + 1)
                pw = pcol("pool_w").rearrange("p (j c) -> p j c", j=2)
                for j in range(2):
                    mm(bank[2 + j][:, :], pw[:, j, :], pooled[:, j, :], start=True, stop=True).then_inc(s_pm, 1)
                for j in range(2):
                    for tt in range(NT):
                        last = nc.tensor.transpose(bank[4 + j][:, tt * P:(tt + 1) * P],
                                                   pj[:, V0 + j, PAD + tt * P:PAD + (tt + 1) * P], ident[:, :])
                last.then_inc(s_vt, 1)
                pe.wait_ge(s_vtv, l + 1)
                zb = [(2, 0), (3, 0), (4, 0), (4, 256)]
                cb = [(5, 0), (6, 0), (7, 0), (7, 256)]
                for h in range(SB_HEADS):
                    r = slice(64 * (h % 2), 64 * (h % 2) + 64)
                    for i in range(NT):
                        b, o = zb[i]
                        last = mm(bank[b][:, o:o + W4[i]], pj[r, K0 + h // 2, PAD + i * P:PAD + (i + 1) * P],
                                  pj[r, Q0 + h // 2, PAD + i * P:PJW], start=True, stop=True)
                    last.then_inc(s_z, 1)
                    pe.wait_ge(s_nlk, l * 4 + h + 1)
                    for i in range(NT):
                        b, o = cb[i]
                        for j in range(i, NT):
                            last = mm(bank[b][:, o + (j - i) * P:o + W4[i]], tri_ge[:, :] if j == i else ones[:, :],
                                      nlk[:, O4[j]:O4[j] + W4[j]], start=(j == i), stop=(j == NT - 1))
                    last.then_inc(s_cum, 1)
                    pe.wait_ge(s_wm, l * 4 + h + 1)
                    for i in range(NT):
                        last = mm(bank[2][r, i * P:T], v_tok[:, i, h * HD:(h + 1) * HD], arg[:, O4[i]:O4[i] + W4[i]],
                                  start=(i == 0), stop=(i == NT - 1))
                    last.then_inc(s_ay, 1)
                    pe.wait_ge(s_ayv, l * 4 + h + 1)
                pe.wait_ge(s_rhs, l * 3 + 2)
                steps.settle()
                with pe.Fori(0, N_OUT // 2) as i:
                    for s in range(2):
                        project(l, i * 2 + (OUT0 + s), s)
                norm_sum(l * 2 + 2)
                pe.wait_ge(s_rhs, l * 3 + 3)
                pe.wait_ge(s_keys, (l + 1) * 16)
                steps.settle()
                with pe.Fori(0, N_Q // 2) as i:
                    for s in range(2):
                        project(l, i * 2 + (WQ0 + s), s)
                        pe.wait_ge(s_taken, l * TAKEN + i * 2 + (WQ0 + s + 3))
                        pe.wait_ge(s_scv, l * N_Q + i * 2 + (s + 1))
                        for tt in range(NT):
                            last = mm(bank[2 + s][:, tt * P:(tt + 1) * P], qT[:, s, tt * P:(tt + 1) * P],
                                      keys[:, bass.ds(i * 2 + s, 1), :].rearrange("p a b -> p (a b)"),
                                      start=True, stop=True)
                        last.then_inc(s_sc, 1)
                with pe.Fori(0, NT) as tt:
                    for m in range(G_PICK * GROUP):
                        project(l, tt * (G_PICK * GROUP) + (U0 + m), m % 2)
                    pe.wait_ge(s_rt, l * NT + tt + 1)
                    for a in range(3):
                        last = nc.tensor.transpose(bank[2][:, a * P:(a + 1) * P], route[:, a, :], ident[:, :])
                    last.then_inc(s_rtt, 1)
                pe.wait_ge(s_idx, l * NT + NT)
                steps.settle()
                with pe.Fori(0, G_GATE) as i:
                    for j in range(GROUP):
                        project(l, i * GROUP + (U0 + G_GATE0 * GROUP + j), j % 2)
                        for u in range(TILE_QUADS):
                            q = i * (GROUP * TILE_QUADS) + (j * TILE_QUADS + u)
                            pe.wait_ge(s_oh, l * QUADS + 1 + q)
                            pe.wait_ge(s_gv, l * QUADS + 1 + q)
                            for t in range(QUAD):
                                last = mm(bank[2 + u][:, t * P:(t + 1) * P], oneh[:, u, t, :], gateh[:, u, t, :],
                                          start=True, stop=True)
                            last.then_inc(s_gm, 1)
                with pe.Fori(G_REST0, GROUPS) as g:
                    for j in range(GROUP):
                        project(l, g * GROUP + (U0 + j), j % 2)

                def v_block(b, j, first=False, final=False):
                    pe.wait_ge(s_wh, l * STREAM + b + (EV0 + 1))
                    pe.wait_ge(s_wl, l * STREAM + b + (EV0 + 1))
                    pe.wait_ge(s_coef, l * N_KEYS + b + 1)
                    for k in range(KT):
                        for w, c in ((w_hi, c_hi), (w_hi, c_lo), (w_lo, c_hi)):
                            last = mm(bank[k][:, :], w[j % 2][:, k, :], c[:, j, :],
                                      start=(first and w is w_hi and c is c_hi), stop=(final and w is w_lo))
                        if final and k < KT - 1:
                            last.then_inc(s_out, 1)
                    last.then_inc(s_tile, 1)

                pe.wait_ge(s_taken, l * TAKEN + TAKEN + 2)
                pe.wait_ge(s_gv, l * QUADS + QUADS + 2)
                for j in range(GROUP):
                    v_block(j, j, first=(j == 0))
                with pe.Fori(1, GROUPS - 1) as g:
                    for j in range(GROUP):
                        v_block(g * GROUP + j, j)
                for j in range(GROUP):
                    v_block(N_KEYS - GROUP + j, j, final=(j == GROUP - 1))
            norm_sum(LAYERS * 2 + 1)

        @block.vector
        def _(dve):
            steps = Steps(dve, s_dve, s_dset)
            link = steps.link
            v = nc.vector

            def lo(l, half, s, n=None):
                if n is not None:
                    dve.wait_ge(s_tile, l * STREAM + n + 1)
                dve.wait_ge(s_wh, l * STREAM + half * 2 + (s + 1))
                v.tensor_tensor(w_lo[s][:, :, :].rearrange("p a b -> p (a b)"), w_raw[:, s, :],
                                w_hi[s][:, :, :].rearrange("p a b -> p (a b)").bitcast(F32),
                                ALU.subtract).then_inc(s_wl, 1)

            def inv_root(psum, count, sem_var, sem_root, root_val):
                v.tensor_scalar(nrm[:, 0, :], psum, 1.0 / count, EPS, ALU.mult, ALU.add).then_inc(sem_var, 1)
                dve.wait_ge(sem_root, root_val)
                link(v.reciprocal(nrm[:, 2, :], nrm[:, 1, :]))
                link(v.tensor_tensor(nrm[:, 3, :], nrm[:, 2, :], nrm[:, 2, :], ALU.mult))
                link(v.tensor_tensor(nrm[:, 3, :], nrm[:, 3, :], nrm[:, 0, :], ALU.mult))
                link(v.tensor_scalar(nrm[:, 3, :], nrm[:, 3, :], -0.5, 1.5, ALU.mult, ALU.add))
                link(v.tensor_tensor(nrm[:, 2, :], nrm[:, 2, :], nrm[:, 3, :], ALU.mult))

            def normed(l, which):
                dve.wait_ge(s_ssum, l * 2 + which + 1)
                inv_root(bank[2][:, :], D, s_var, s_root, l * 2 + which + 1)
                link(v.tensor_tensor(h32[:, :, :], x[:, :, :],
                                     nrm[:, 2, :].unsqueeze(1).broadcast_to([P, KT, T]), ALU.mult))

            def modulated(which):
                for k in range(KT):
                    ins = v.tensor_scalar(h32[:, k, :], h32[:, k, :], gs[:, which, k:k + 1],
                                          mod[:, 3 * which, k:k + 1], ALU.mult, ALU.add)
                ins.then_inc(s_h32, 1)

            def rhs_lo(l, which):
                dve.wait_ge(s_hh, l * 3 + which)
                v.tensor_tensor(hL[:, :, :], h32[:, :, :], hH[:, :, :].bitcast(F32),
                                ALU.subtract).then_inc(s_rhs, 1)

            dve.wait_ge(s_const, 11)
            for j, p0, w in ((0, 0, 2), (0, 64, 4), (1, 0, 8), (1, 64, 16)):
                ins = v.tensor_scalar(inv_count[p0:p0 + 64, j, :], inv_count[p0:p0 + 64, j, :], float(w), None, ALU.min)
            ins.then_inc(s_const, 1)
            dve.wait_ge(s_const, 12)
            v.reciprocal(inv_count[:, :, :], inv_count[:, :, :]).then_inc(s_const, 1)
            dve.wait_ge(s_const, 13)
            dve.wait_ge(s_in, 48)
            v.memset(tiny[:, 15, 0:1], 0.0).then_inc(s_gate, 1)

            with dve.Fori(0, LAYERS) as l:
                steps.base, steps.n = l * DVE_STEPS, 0
                lo(l, 0, 0)
                lo(l, 0, 1)
                dve.wait_ge(s_par, (l + 1) * 16)
                v.memset(pj[:, :, 0:PAD], 0.0)
                normed(l, 0)
                dve.wait_ge(s_adau, l * ADA_CHUNKS + ADA_CHUNKS)
                link(v.tensor_tensor(mod[:, :, :].rearrange("p a b -> p (a b)"), bank[3][:, 0:48], pcol("ada_b"), ALU.add))
                for w, name in ((0, "g_mix"), (1, "g_ffn")):
                    ins = v.scalar_tensor_tensor(gs[:, w, :], mod[:, 3 * w + 1, :], 1.0, pcol(name), ALU.add, ALU.mult)
                link(ins)
                modulated(0)
                rhs_lo(l, 1)
                dve.wait_ge(s_dtm, l + 1)
                q = lambda n: tiny[:, n, :]
                bias = pcol("dt_bias").unsqueeze(1).broadcast_to([P, NT, HEADS])
                link(v.tensor_tensor(q(1).rearrange("p (t h) -> p t h", t=NT),
                                     bank[4][:, 0:32].rearrange("p (t h) -> p t h", t=NT), bias, ALU.add))
                v.scalar_tensor_tensor(q(2), q(1), -1.0, q(1), ALU.mult, ALU.min).then_inc(s_dt1, 1)
                dve.wait_ge(s_dt2, l + 1)
                v.tensor_scalar(q(5), q(3), 1.0, None, ALU.add).then_inc(s_dt3, 1)
                dve.wait_ge(s_dt4, l + 1)
                link(v.tensor_scalar(q(14), q(5), -1.0, None, ALU.add))
                link(v.tensor_scalar(q(15), q(14), 0.0, None, ALU.is_equal))
                link(v.tensor_tensor(q(14), q(14), q(15), ALU.add))
                link(v.tensor_tensor(q(15), q(6), q(15), ALU.add))
                link(v.reciprocal(q(14), q(14)))
                link(v.tensor_tensor(q(15), q(15), q(14), ALU.mult))
                link(v.tensor_tensor(q(15), q(15), q(3), ALU.mult))
                link(v.scalar_tensor_tensor(q(1), q(1), 0.0, q(15), ALU.max, ALU.add))
                ea = tiny[:, 4, 0:HEADS].unsqueeze(1).broadcast_to([P, NT, HEADS])
                v.scalar_tensor_tensor(q(7).rearrange("p (t h) -> p t h", t=NT),
                                       q(1).rearrange("p (t h) -> p t h", t=NT), -1.0, ea,
                                       ALU.mult, ALU.mult).then_inc(s_dta, 1)
                with dve.Fori(0, N_IN // 2) as i:
                    for s in range(2):
                        lo(l, i + 1, s, i * 2 + s)
                dve.wait_ge(s_acs, l + 1)
                link(v.tensor_copy(q(8), bank[5][:, 0:32]))
                v.tensor_copy(q(12), bank[5][:, 32:64])
                v.tensor_tensor(q(10), bank[5][:, 32:64], q(8), ALU.subtract).then_inc(s_acv, 1)
                dve.wait_ge(s_taken, l * TAKEN + N_IN + 2)
                cw = pcol("conv_w").rearrange("p (j w) -> p j w", j=6)
                for j in range(6):
                    src = lambda w: pj[:, XS0 + j, PAD - 3 + w:PJW - 3 + w]
                    link(v.tensor_scalar(xbc[:, j, :], src(0), cw[:, j, 0:1], pcol("conv_b")[:, j:j + 1],
                                         ALU.mult, ALU.add))
                    for w in (1, 2):
                        link(v.scalar_tensor_tensor(xbc[:, j, :], src(w), cw[:, j, w:w + 1], xbc[:, j, :],
                                                    ALU.mult, ALU.add))
                    v.scalar_tensor_tensor(xbc[:, j, :], src(3), cw[:, j, 3:4], xbc[:, j, :],
                                           ALU.mult, ALU.add).then_inc(s_conv, 1)
                def by_head(n, tt):
                    return tiny[:, n, tt * HEADS:(tt + 1) * HEADS].unsqueeze(2).broadcast_to([P, HEADS, HD])

                def heads(ap):
                    return ap.rearrange("p (h c) -> p h c", c=HD)

                for tt in range(NT):
                    dve.wait_ge(s_tr, l * 5 + tt + 1)
                    v.tensor_tensor(heads(xdt[:, tt, :]), heads(bank[2 + tt % 2][:, :]), by_head(1, tt),
                                    ALU.mult).then_inc(s_trv, 1)
                dve.wait_ge(s_tr, l * 5 + 5)
                v.tensor_copy(b_tok[:, :, :].rearrange("p a b -> p (a b)"), bank[4][:, :]).then_inc(s_trv, 1)
                for g in range(2):
                    dve.wait_ge(s_cb, l * 2 + g + 1)
                    v.tensor_tensor(cbm[:, g, :, :], bank[5 + g][:, :].rearrange("p (t c) -> p t c", t=NT),
                                    tri_le[:, :].unsqueeze(1).broadcast_to([P, NT, P]), ALU.mult).then_inc(s_cbv, 1)
                dve.wait_ge(s_dec, l + 1)
                dve.wait_ge(s_trv, l * 5 + 5)
                dve.wait_ge(s_cbv, l * 2 + 2)
                for tt in range(NT):
                    for g in range(2):
                        dve.wait_ge(s_r, l * 8 + tt * 2 + g + 1)
                        if tt >= 1:
                            dve.wait_ge(s_sm, l * 8 + tt * 2 + g - 1)
                        sums = tiny[:, 8, tt * HEADS + 4 * g:tt * HEADS + 4 * g + 4].unsqueeze(2).broadcast_to([P, 4, P])
                        link(v.tensor_tensor(seg[:, g, :].rearrange("p (h c) -> p h c", h=4),
                                             bank[7 if g == 0 else 2][:, :].rearrange("p (h c) -> p h c", h=4),
                                             sums, ALU.subtract))
                        v.tensor_scalar(seg[:, g, :], seg[:, g, :], 0.0, None, ALU.min).then_inc(s_seg, 1)
                    if tt < NT - 1:
                        if tt >= 1:
                            dve.wait_ge(s_y, l * NT + tt)
                        v.tensor_tensor(heads(xdd[:, :]), heads(xdt[:, tt, :]), by_head(11, tt), ALU.mult).then_inc(s_xdd, 1)
                    for g in range(2):
                        dve.wait_ge(s_exp, l * 8 + tt * 2 + g + 1)
                        if tt >= 1:
                            dve.wait_ge(s_y, l * NT + tt)
                        v.tensor_tensor(smat[:, g, :].rearrange("p (h c) -> p h c", h=4),
                                        seg[:, g, :].rearrange("p (h c) -> p h c", h=4),
                                        cbm[:, g, tt, :].unsqueeze(1).broadcast_to([P, 4, P]), ALU.mult).then_inc(s_sm, 1)
                    dve.wait_ge(s_y, l * NT + tt + 1)
                    if tt < NT - 1:
                        for g in range(2):
                            r = slice(64 * g, 64 * g + 64)
                            st = state[r, :].rearrange("p (h c) -> p h c", c=HD)
                            gain = bank[5][r, 0:256].rearrange("p (h c) -> p h c", c=HD)
                            if tt == 0:
                                ins = v.tensor_copy(st, gain)
                            else:
                                total = tiny[r, 13, tt * HEADS + 4 * g:tt * HEADS + 4 * g + 4].unsqueeze(2).broadcast_to([64, 4, HD])
                                link(v.tensor_tensor(st, st, total, ALU.mult))
                                ins = v.tensor_tensor(st, st, gain, ALU.add)
                            if g == 1:
                                ins.then_inc(s_st, 1)
                    if tt == 0:
                        v.tensor_copy(y_tok[:, tt, :], bank[3][:, :]).then_inc(s_yv, 1)
                    else:
                        for g in range(2):
                            ins = v.tensor_tensor(heads(y_tok[:, tt, g * 256:(g + 1) * 256]), heads(bank[4 + 2 * g][:, 0:256]),
                                                  by_head(9, tt)[:, 4 * g:4 * g + 4, :], ALU.mult)
                        link(ins)
                        v.tensor_tensor(y_tok[:, tt, :], y_tok[:, tt, :], bank[3][:, :], ALU.add).then_inc(s_yv, 1)
                dve.wait_ge(s_zs, l + 1)
                for j in range(4):
                    dve.wait_ge(s_yt, l * 4 + j + 1)
                    link(v.scalar_tensor_tensor(xbc[:, j, :], xbc[:, j, :], pcol("d_skip")[:, j:j + 1],
                                                bank[2 + j][:, :], ALU.mult, ALU.add))
                    v.tensor_tensor(xbc[:, j, :], xbc[:, j, :], pj[:, Z0 + j, PAD:PJW], ALU.mult).then_inc(s_ygv, 1)
                for g in range(2):
                    dve.wait_ge(s_yss, l * 2 + g + 1)
                    inv_root(bank[6 + g][:, :], 2 * P, s_yvar, s_yroot, l * 2 + g + 1)
                    for j in (2 * g, 2 * g + 1):
                        ins = v.scalar_tensor_tensor(mixed[:, j, :], xbc[:, j, :], pcol("ssd_g")[:, j:j + 1],
                                                     nrm[:, 2, :], ALU.mult, ALU.mult)
                    link(ins)
                xp = pj[:, XP0:XP0 + 2, :]
                link(v.tensor_tensor(pool_a[:, :, 1:], xp[:, :, 1:], xp[:, :, :PJW - 1], ALU.add))
                link(v.tensor_tensor(pool_b[:, :, 3:], pool_a[:, :, 3:], pool_a[:, :, 1:PJW - 2], ALU.add))
                for p0, j, src in ((0, 0, pool_a), (64, 0, pool_b)):
                    v.tensor_tensor(pooled[p0:p0 + 64, j, :], src[p0:p0 + 64, j, PAD:], inv_count[p0:p0 + 64, j, :], ALU.mult)
                link(v.tensor_tensor(pool_c[:, 1, 7:], pool_b[:, 1, 7:], pool_b[:, 1, 3:PJW - 4], ALU.add))
                link(v.tensor_tensor(pool_a[:, 1, 15:], pool_c[:, 1, 15:], pool_c[:, 1, 7:PJW - 8], ALU.add))
                for p0, j, src in ((0, 1, pool_c), (64, 1, pool_a)):
                    ins = v.tensor_tensor(pooled[p0:p0 + 64, j, :], src[p0:p0 + 64, j, PAD:], inv_count[p0:p0 + 64, j, :], ALU.mult)
                link(ins)
                v.tensor_tensor(pooled[:, :, :], pooled[:, :, :], xp[:, :, PAD:], ALU.subtract).then_inc(s_pool, 1)
                for j in range(2):
                    dve.wait_ge(s_pm, l * 2 + j + 1)
                    ins = v.tensor_scalar(mixed[:, 4 + j, :], bank[2 + j][:, :], pcol("pool_scale")[:, j:j + 1], None, ALU.mult)
                link(ins)
                dve.wait_ge(s_vt, l + 1)
                for j in range(2):
                    ins = v.tensor_copy(v_tok[:, :, j * P:(j + 1) * P], bank[4 + j][:, :].rearrange("p (t c) -> p t c", t=NT))
                ins.then_inc(s_vtv, 1)
                for h in range(SB_HEADS):
                    r = slice(64 * (h % 2), 64 * (h % 2) + 64)
                    dve.wait_ge(s_z, l * 4 + h + 1)
                    for b, n, o in ((2, 512, 0), (3, 384, 512), (4, 384, 896)):
                        ins = v.tensor_scalar(zs[:, o:o + n], bank[b][:, 0:n], HD ** -0.5, None, ALU.mult)
                    ins.then_inc(s_zv, 1)
                    dve.wait_ge(s_lg, l * 4 + h + 1)
                    link(v.scalar_tensor_tensor(nlk[:, :], zs[:, :], 0.0, ez[:, :], ALU.max, ALU.add))
                    for i in range(NT):
                        ins = v.tensor_tensor(nlk[:, O4[i]:O4[i] + P], nlk[:, O4[i]:O4[i] + P], tri_lt[:, :], ALU.mult)
                    ins.then_inc(s_nlk, 1)
                    dve.wait_ge(s_cum, l * 4 + h + 1)
                    for b, n, o in ((5, 512, 0), (6, 384, 512), (7, 384, 896)):
                        ins = v.tensor_tensor(arg[:, o:o + n], zs[:, o:o + n], bank[b][:, 0:n], ALU.subtract)
                    link(ins)
                    for i in range(NT):
                        ins = v.tensor_scalar(arg[:, O4[i]:O4[i] + P], arg[:, O4[i]:O4[i] + P], 0.0, None, ALU.min)
                    ins.then_inc(s_arg, 1)
                    dve.wait_ge(s_w, l * 4 + h + 1)
                    for i in range(NT):
                        ins = v.tensor_tensor(arg[:, O4[i]:O4[i] + P], arg[:, O4[i]:O4[i] + P], tri_lt[:, :], ALU.mult)
                    ins.then_inc(s_wm, 1)
                    dve.wait_ge(s_ay, l * 4 + h + 1)
                    v.tensor_copy(mixed[r, 6 + h // 2, :], bank[2][r, :]).then_inc(s_ayv, 1)
                rhs_lo(l, 2)
                with dve.Fori(0, N_OUT // 2) as i:
                    for s in range(2):
                        lo(l, i + (OUT0 // 2 + 1), s, i * 2 + (OUT0 + s))
                        k = i * 2 + s
                        xk = x[:, bass.ds(k, 1), :].rearrange("p a t -> p (a t)")
                        v.scalar_tensor_tensor(xk, bank[s][:, :], mod[:, 2, bass.ds(k, 1)], xk,
                                               ALU.mult, ALU.add).then_inc(s_taken, 1)
                normed(l, 1)
                modulated(1)
                rhs_lo(l, 3)
                with dve.Fori(0, N_Q // 2) as i:
                    with steps.loop(i, N_Q // 2, 2 * 5):
                        for s in range(2):
                            lo(l, i + (WQ0 // 2 + 1), s, i * 2 + (WQ0 + s))
                            dve.wait_ge(s_sc, l * N_Q + i * 2 + (s + 3))
                            steps.settle()
                            sc = lambda tt: bank[2 + s][:, tt * P:(tt + 1) * P]
                            each = lambda f: [f(tt) for tt in range(NT)][-1]
                            link(each(lambda tt: v.max(v16[:, tt, 0:8], sc(tt))))
                            steps.settle()
                            each(lambda tt: v.max_index(i16[:, tt, 0:8], v16[:, tt, 0:8], sc(tt)))
                            ins = each(lambda tt: v.match_replace(sc2[:, tt, :], v16[:, tt, 0:8], sc(tt), -3.0e38))
                            ins.then_inc(s_scv, 1)
                            dve.wait_ge(s_scv, l * N_Q + i * 2 + (s + 3))
                            steps.settle()
                            link(each(lambda tt: v.max(v16[:, tt, 8:16], sc2[:, tt, :])))
                            steps.settle()
                            link(each(lambda tt: v.max_index(i16[:, tt, 8:16], v16[:, tt, 8:16], sc2[:, tt, :])))
                            link(v.tensor_copy(topv[:, :, bass.ds(i * 2 + s, 1), :].rearrange("p t a k -> p t (a k)"), v16[:, :, :]))
                            link(v.tensor_copy(topi[:, :, bass.ds(i * 2 + s, 1), :].rearrange("p t a k -> p t (a k)"), i16[:, :, :]))
                def u_lo(g, j):
                    lo(l, g * (GROUP // 2) + (U0 // 2 + j // 2 + 1), j % 2, g * GROUP + (U0 + j))

                with dve.Fori(0, NT) as tt:
                    with steps.loop(tt, NT, 16):
                        def u_next(m):
                            u_lo(tt * G_PICK + m // GROUP, m % GROUP)

                        tv = topv[:, bass.ds(tt, 1), :, :].rearrange("p t (h i) k -> p (t h) i k", i=2)
                        ti = topi[:, bass.ds(tt, 1), :, :].rearrange("p t (h i) k -> p (t h) i k", i=2)
                        full = [P, PH, TOPK, TOPK]
                        each = lambda f: [f(h) for h in range(PH)][-1]
                        u_next(0)
                        link(v.tensor_tensor(cand[:, :, :].rearrange("p h (a b) -> p h a b", a=TOPK),
                                             tv[:, :, 0, :].unsqueeze(3).broadcast_to(full),
                                             tv[:, :, 1, :].unsqueeze(2).broadcast_to(full), ALU.add))
                        u_next(1)
                        link(each(lambda h: v.max(bestv[:, h, 0:8], cand[:, h, :])))
                        u_next(2)
                        each(lambda h: v.max_index(bestp[:, h, 0:8], bestv[:, h, 0:8], cand[:, h, :]))
                        u_next(3)
                        link(each(lambda h: v.match_replace(cand2[:, h, :], bestv[:, h, 0:8], cand[:, h, :], -3.0e38)))
                        u_next(4)
                        link(each(lambda h: v.max(bestv[:, h, 8:16], cand2[:, h, :])))
                        u_next(5)
                        link(each(lambda h: v.max_index(bestp[:, h, 8:16], bestv[:, h, 8:16], cand2[:, h, :])))
                        link(v.tensor_copy(gsum[:, 0, :], bestv[:, :, 0]))
                        v.tensor_tensor(bestv[:, :, :], bestv[:, :, :],
                                        gsum[:, 0, :].unsqueeze(2).broadcast_to([P, PH, TOPK]),
                                        ALU.subtract).then_inc(s_shift, 1)
                        u_next(6)
                        flat = bestp[:, :, :].rearrange("p h k -> p (h k)")
                        v.tensor_scalar(posu[:, 0, :], flat, 4, None, ALU.logical_shift_right)
                        link(v.tensor_scalar(posu[:, 1, :], flat, 15, None, ALU.bitwise_and))
                        link(v.tensor_copy(posf[:, :, :], posu[:, :, :]))
                        for a in range(2):
                            pk = pick[:, :, :]
                            pk4 = pick[:, :, :].rearrange("p (h k) j -> p h k j", h=PH)
                            link(v.tensor_tensor(pk, posf[:, a, :].unsqueeze(2).broadcast_to([P, HK, TOPK]),
                                                 iota[:, 0:TOPK].unsqueeze(1).broadcast_to([P, HK, TOPK]), ALU.is_equal))
                            u_next(7 + 2 * a)
                            link(v.tensor_tensor(pk4, pk4, ti[:, :, a, :].unsqueeze(2).broadcast_to(full), ALU.mult))
                            u_next(8 + 2 * a)
                            link(v.reduce_sum(route[:, a, :], pk, AX.X))
                        dve.wait_ge(s_gexp, l * NT + tt + 1)
                        link(v.reduce_sum(gsum[:, 0, :], bestv[:, :, :], AX.X))
                        link(v.reciprocal(gsum[:, 1, :], gsum[:, 0, :]))
                        v.tensor_tensor(route[:, 2, :].rearrange("p (h k) -> p h k", h=PH), bestv[:, :, :],
                                        gsum[:, 1, :].unsqueeze(2).broadcast_to([P, PH, TOPK]),
                                        ALU.mult).then_inc(s_rt, 1)
                        u_next(11)
                        dve.wait_ge(s_idx, l * NT + tt + 1)
                with dve.Fori(0, G_GATE) as i:
                    for j in range(GROUP):
                        for u in range(TILE_QUADS):
                            q = i * (GROUP * TILE_QUADS) + (j * TILE_QUADS + u)
                            dve.wait_ge(s_gm, l * QUADS + 1 + q)
                            for q_ in range(QUAD):
                                t = q * QUAD + q_
                                v.tensor_scalar(oneh[:, u, q_, :], iota[:, :], idxT[:, 0, bass.ds(t, 1)], None, ALU.is_equal)
                                ins = v.tensor_scalar(gateh[:, u, q_, :], iota[:, :], idxT[:, 1, bass.ds(t, 1)],
                                                      idxT[:, 2, bass.ds(t, 1)], ALU.is_equal, ALU.mult)
                            ins.then_inc(s_oh, 1)
                        u_lo(i + G_GATE0, j)
                with dve.Fori(G_REST0, GROUPS - 1) as g:
                    for j in range(GROUP):
                        u_lo(g, j)

                def coefs(h, s, j):
                    if j == 0:
                        dve.wait_ge(s_gin[s], (l * (GROUPS // 2) + h + 1) * 16)
                        dve.wait_ge(s_ain[s], (l * (GROUPS // 2) + h + 1) * 16)
                    link(v.tensor_tensor(coef[:, j % 2, :].rearrange("p (c t) -> p c t", c=GCHUNKS),
                                         act_in[s][:, j // 2, j % 2, :].rearrange("p (c t) -> p c t", c=GCHUNKS),
                                         gates[s][:, :, j, :], ALU.mult))
                    link(v.tensor_copy(c_hi[:, j, :], coef[:, j % 2, :]))
                    v.tensor_tensor(c_lo[:, j, :], coef[:, j % 2, :], c_hi[:, j, :].bitcast(F32),
                                    ALU.subtract).then_inc(s_coef, 1)

                for j in range(GROUP):
                    if j >= 2:
                        coefs(0, 0, j - 2)
                    u_lo(GROUPS - 1, j)
                def v_group(h, s, ahead=True):
                    for j in range(GROUP if ahead else 2):
                        if j < 2:
                            coefs(h, s, j + 2)
                        else:
                            coefs(h + s, 1 - s, j - 2)
                        b = h * (2 * GROUP) + (s * GROUP + j)
                        lo(l, h * GROUP + (EV0 // 2 + s * 2 + j // 2 + 1), j % 2, b + EV0)

                with dve.Fori(0, GROUPS // 2 - 1) as h:
                    with steps.loop(h, GROUPS // 2 - 1, 2 * 2 * GROUP):
                        v_group(h, 0)
                        v_group(h, 1)
                v_group(GROUPS // 2 - 1, 0)
                v_group(GROUPS // 2 - 1, 1, ahead=False)
                for k in range(KT):
                    if k < KT - 1:
                        dve.wait_ge(s_out, l * (KT - 1) + k + 1)
                    else:
                        dve.wait_ge(s_tile, l * STREAM + STREAM)
                    link(v.scalar_tensor_tensor(x[:, k, :], bank[k][:, :], mod[:, 5, k:k + 1], x[:, k, :],
                                                ALU.mult, ALU.add))
                v.memset(tiny[:, 15, 0:1], 0.0).then_inc(s_gate, 1)
                assert steps.n == DVE_STEPS, steps.n
            steps.base, steps.n = LAYERS * DVE_STEPS, 0
            normed(LAYERS, 0)
            for k in range(KT):
                ins = v.tensor_scalar(x[:, k, :], h32[:, k, :], fin_g[:, k:k + 1], None, ALU.mult)
            ins.then_inc(s_fin, 1)


def kernel(**inputs):
    import numpy as np
    import concourse.bacc as bacc
    from concourse.bass_utils import run_bass_kernel_spmd

    a = {k: np.asarray(v) for k, v in inputs.items()}
    L = LAYERS

    def cols(v, n=KT):
        return v.reshape(L, n, P).transpose(0, 2, 1)

    def tiles(w):
        return w.reshape(L, KT, P, -1, P).transpose(0, 3, 2, 1, 4)

    w_in = a["w_in"]
    dt0 = 1280
    w_cols = np.concatenate([w_in[:, :, :dt0], w_in[:, :, dt0 + HEADS:]], axis=2)
    w_dt = w_in[:, :, dt0:dt0 + HEADS].reshape(L, KT, P, HEADS).transpose(0, 2, 1, 3).reshape(L, P, KT * HEADS)
    u = a["peer_u"].reshape(L, N_KEYS, N_KEYS, KT, P).transpose(0, 2, 4, 3, 1)
    ev = a["peer_v"].reshape(L, N_KEYS, N_KEYS, D).transpose(0, 2, 1, 3).reshape(L, N_KEYS, P, KT, P)
    stream = np.concatenate([tiles(w_cols), tiles(a["w_out"]), tiles(a["peer_wq"]), u, ev],
                            axis=1).reshape(L, STREAM, P, D)
    ada = a["ada_w"].reshape(L, KT, P, ADA_CHUNKS, ADA_CHUNK).transpose(0, 3, 2, 1, 4)
    pw = np.zeros((L, 2, P, P), np.float32)
    for j in range(4):
        o = 64 * (j % 2)
        pw[:, j // 2, o:o + 64, o:o + 64] = a["pool_w"][:, j]
    wide = lambda v: np.broadcast_to(v[:, None, :], (L, P, HEADS))
    packed = {
        "ada_b": cols(a["ada_b"], 48), "g_mix": cols(a["mix_norm_g"]), "g_ffn": cols(a["ffn_norm_g"]),
        "conv_w": a["conv_w"].reshape(L, 4, 6, P).transpose(0, 3, 2, 1).reshape(L, P, 24),
        "conv_b": cols(a["conv_b"], 6), "ssd_g": cols(a["ssd_norm_g"], 4), "pool_scale": cols(a["pool_scale"], 2),
        "d_skip": cols(np.repeat(a["d_skip"], HD, axis=1), 4), "dt_bias": wide(a["dt_bias"]), "a_log": wide(a["a_log"]),
        "w_dt": w_dt, "pool_w": pw.transpose(0, 2, 1, 3).reshape(L, P, 2 * P),
    }
    arrays = {
        "xT": a["x"][0].T.reshape(KT, P, T).transpose(1, 0, 2),
        "cT": a["c"][0].reshape(KT, P).T,
        "final_g": a["final_norm_g"].reshape(KT, P).T,
        "adaw": ada, "wst": stream,
        "params": np.concatenate([packed[n] for n, _ in PARAMS], axis=2),
        "keysT": a["peer_keys"].transpose(0, 4, 1, 2, 3).reshape(L, P, SEGS, N_KEYS),
    }
    arrays = {k: np.ascontiguousarray(v) for k, v in arrays.items()}
    nc = bacc.Bacc("TRN2", target_bir_lowering=False, num_devices=1)
    aps = [nc.dram_tensor(k, v.shape, F32, kind="ExternalInput").ap() for k, v in arrays.items()]
    g_dram = nc.dram_tensor("gate_matrices", (GCHUNKS, P, N_KEYS, GCHUNK), F32).ap()
    a_dram = nc.dram_tensor("activations", (N_KEYS // 2, P, 2, T), F32).ap()
    out = nc.dram_tensor("outT", (P, KT, T), F32, kind="ExternalOutput").ap()
    build(nc, *aps, g_dram, a_dram, out)
    r = run_bass_kernel_spmd(nc, [arrays], core_ids=[0])
    got = r.results[0]["outT"]
    return got.transpose(2, 1, 0).reshape(1, T, D)
```

```python
from contextlib import ExitStack, contextmanager

import concourse.bass as bass
from concourse import mybir

F32 = mybir.dt.float32
F32R = mybir.dt.float32r
U32 = mybir.dt.uint32
ALU = mybir.AluOpType
ACT = mybir.ActivationFunctionType
AX = mybir.AxisListType

P = 128
LAYERS = 2
D = 1024
KT = D // P
T = 512
NT = T // P
EPS = 1e-6

HEADS = 8
HD = 64
SB_HEADS = 4

XS0, B0, C0, XP0, Z0, Q0, K0, V0 = 0, 4, 5, 6, 8, 12, 14, 16
N_IN = 18
DT_TILE = 8
LOOSE = XP0
N_OUT = KT
N_Q = 16
N_KEYS = 128
OUT0 = N_IN
WQ0 = OUT0 + N_OUT
U0 = WQ0 + N_Q
EV0 = U0 + N_KEYS
STREAM = EV0 + N_KEYS
TAKEN = EV0
assert EV0 % 2 == 0 and U0 % 2 == 0 and WQ0 % 2 == 0 and OUT0 % 2 == 0

PAD = 16
PJW = PAD + T

ADA_W = 6 * D * KT // N_KEYS
ADA_BLOCKS = 6 * D // ADA_W
ADA_ROWS = KT // 2
ADA_TERMS = ADA_BLOCKS * KT
assert ADA_BLOCKS == N_KEYS // 8 and ADA_TERMS == N_KEYS

SEGS = 16
PH = 8
TOPK = 16
HK = PH * TOPK
assert HK == P

GROUP = 4
GROUPS = N_KEYS // GROUP
GCHUNK = 64
GCHUNKS = T // GCHUNK
QUAD = 4
QUADS = T // QUAD
G_PICK = 3
G_GATE0 = NT * G_PICK
TILE_QUADS = 2
G_GATE = QUADS // (TILE_QUADS * GROUP)
G_REST0 = G_GATE0 + G_GATE
G_CHUNK = GCHUNK // (QUAD * TILE_QUADS * GROUP)
assert G_REST0 + 2 <= GROUPS

PARAMS = [("ada_b", 48), ("g_mix", KT), ("g_ffn", KT), ("conv_w", 24), ("conv_b", 6), ("ssd_g", 4),
          ("pool_scale", 2), ("d_skip", 4), ("dt_bias", HEADS), ("a_log", HEADS),
          ("w_dt", KT * HEADS), ("pool_w", 2 * P)]
PCOL = {}
_c = 0
for _n, _w in PARAMS:
    PCOL[_n] = (_c, _w)
    _c += _w
NPAR = _c

DVE_STEPS = 462
RHS_PARTS = 2 * KT + 1
HI_PARTS = 2 * KT + 2
ACT_STEPS = 8


class Steps:

    def __init__(self, eng, sem, settled=None):
        self.eng, self.sem, self.settled, self.base, self.n = eng, sem, settled, 0, 0

    def settle(self):
        self.eng.sem_inc(self.settled, 1)

    def link(self, ins):
        ins.then_inc(self.sem, 1)
        self.n += 1
        self.eng.wait_ge(self.sem, self.base + self.n)

    @contextmanager
    def loop(self, i, times, per):
        base, n = self.base, self.n
        self.base, self.n = base + n + i * per, 0
        yield
        assert self.n == per, (self.n, per)
        self.base, self.n = base, n + times * per


def build(nc, xT, cT, final_g, adaw, wst, params, keysT, g_dram, a_dram, outT):
    ctx = ExitStack()
    with ctx:
        def sb(name, shape, dt=F32, where=ctx):
            return where.enter_context(nc.sbuf_tensor(name, shape, dt))

        def sem(name):
            return ctx.enter_context(nc.semaphore(name))

        ident = sb("ident", [P, P])
        tri_le = sb("tri_le", [P, P])
        tri_ge = sb("tri_ge", [P, P])
        tri_lt = sb("tri_lt", [P, P])
        ones = sb("ones", [P, P])
        iota = sb("iota", [P, P])
        inv_count = sb("inv_count", [P, 2, T])
        x = sb("x", [P, KT, T])
        cond = sb("cond", [P, KT])
        fin_g = sb("fin_g", [P, KT])
        par = sb("par", [P, NPAR])
        mod = sb("mod", [P, 6, KT])
        gs = sb("gs", [P, 2, KT])
        hH = sb("hH", [P, KT, T], F32R)
        hL = sb("hL", [P, KT, T], F32R)
        w_raw = sb("w_raw", [P, 2, D])
        w_hi = [sb(f"w_hi{s}", [P, KT, P], F32R) for s in range(2)]
        w_lo = [sb(f"w_lo{s}", [P, KT, P], F32R) for s in range(2)]
        tiny = sb("tiny", [P, 16, 32])

        def pcol(name):
            a, w = PCOL[name]
            return par[:, a:a + w]

        mixer = ExitStack()
        pj = sb("pj", [P, N_IN, PJW], where=mixer)
        h32 = sb("h32", [P, KT, T], where=mixer)
        nrm = sb("nrm", [P, 4, T], where=mixer)
        W4 = [T - P * i for i in range(NT)]
        O4 = [sum(W4[:i]) for i in range(NT)]
        WA = sum(W4)
        scan = ExitStack()
        xbc = sb("xbc", [P, 6, T], where=scan)
        xdt = sb("xdt", [P, NT, T], where=scan)
        y_tok = sb("y_tok", [P, NT, T], where=scan)
        xdd = sb("xdd", [P, T], where=scan)
        b_tok = sb("b_tok", [P, NT, P], where=scan)
        cbm = sb("cbm", [P, 2, NT, P], where=scan)
        state = sb("state", [P, 4 * HD], where=scan)
        seg = sb("seg", [P, 2, T], where=scan)
        smat = sb("smat", [P, 2, T], where=scan)
        v_tok = sb("v_tok", [P, NT, 2 * P], where=scan)
        zs = [sb(f"zs{s}", [P, WA], where=scan) for s in range(2)]
        scan.close()
        logs = ExitStack()
        sb("before_seg", [P, 6 * T + 2 * NT * T + T + NT * P + 2 * NT * P + 4 * HD], where=logs)
        ez = sb("ez", [P, WA], where=logs)
        logs.close()
        pools = ExitStack()
        sb("xbc_xdt", [P, 6 * T + NT * T], where=pools)
        pool_a = sb("pool_a", [P, 2, PJW], where=pools)
        pool_b = sb("pool_b", [P, 2, PJW], where=pools)
        pool_c = sb("pool_c", [P, 2, PJW], where=pools)
        pooled = sb("pooled", [P, 2, T], where=pools)
        pools.close()
        arg = [sb(f"arg{s}", [P, WA], where=mixer) for s in range(2)]
        sb("to_xdt", [P, 6 * T - 2 * WA], where=mixer)
        nlk = [sb(f"nlk{s}", [P, WA], where=mixer) for s in range(2)]
        mixer.close()
        mixed = h32

        router = ExitStack()
        sb("r_pad", [P, N_IN * PJW], where=router)
        sb("r_h32", [P, KT * T], where=router)
        sb("r_nrm", [P, 4 * T], where=router)
        keys = sb("keys", [P, SEGS, N_KEYS], where=router)
        qT = sb("qT", [P, 2, T], where=router)
        idxT = sb("idxT", [P, 3, T], where=router)
        topv = sb("topv", [P, NT, SEGS, TOPK], where=router)
        topi = sb("topi", [P, NT, SEGS, TOPK], where=router)
        act_out = sb("act_out", [P, 2, 2, T], where=router)
        router.close()
        r2 = ExitStack()
        v16 = sb("v16", [P, 2, NT, TOPK], where=r2)
        i16 = sb("i16", [P, 2, NT, TOPK], U32, where=r2)
        sc2 = sb("sc2", [P, NT, N_KEYS], where=r2)
        cand = sb("cand", [P, PH, TOPK * TOPK], where=r2)
        cand2 = sb("cand2", [P, PH, TOPK * TOPK], where=r2)
        bestv = sb("bestv", [P, PH, TOPK], where=r2)
        bestp = sb("bestp", [P, PH, TOPK], U32, where=r2)
        posu = sb("posu", [P, 2, HK], U32, where=r2)
        posf = sb("posf", [P, 2, HK], where=r2)
        pick = sb("pick", [P, HK, TOPK], where=r2)
        route = sb("route", [P, 3, HK], where=r2)
        gsum = sb("gsum", [P, 2, PH], where=r2)
        r2.close()
        r3 = ExitStack()
        oneh = sb("oneh", [P, 2, QUAD, P], where=r3)
        gateh = sb("gateh", [P, 2, QUAD, P], where=r3)
        stage = [sb(f"stage{s}", [P, N_KEYS, GCHUNK], where=r3) for s in range(2)]
        r3.close()

        ex = ExitStack()
        gates = [sb(f"gates{s}", [P, GCHUNKS, GROUP, GCHUNK], where=ex) for s in range(2)]
        act_in = [sb(f"act_in{s}", [P, 2, 2, T], where=ex) for s in range(2)]
        coef = sb("coef", [P, 2, T], where=ex)
        c_hi = sb("c_hi", [P, GROUP, T], F32R, where=ex)
        c_lo = sb("c_lo", [P, GROUP, T], F32R, where=ex)
        ex.close()
        late = ExitStack()
        sb("late_pad", [P, 16 * 1024], where=late)
        ada_buf = sb("ada_buf", [P, 4, ADA_ROWS, ADA_W], where=late)
        sb("late_pad2", [P, 2 * 1024], where=late)
        ada_acc = sb("ada_acc", [P, 6 * D], where=late)
        late.close()

        bank = [ctx.enter_context(nc.psum_tensor(f"bank{i}", [P, T], F32)) for i in range(8)]

        s_const = sem("const_ready")
        s_in = sem("inputs_in")
        s_cond = sem("cond_ready")
        s_gate = sem("layer_may_start")
        s_par = sem("params_in")
        s_keys = sem("keys_in")
        s_ada = [sem(f"ada_in{s}") for s in range(4)]
        s_adat = sem("ada_terms_summed")
        s_adam = sem("modulation_done")
        s_raw = [sem(f"w_raw_in{s}") for s in range(2)]
        s_wh = sem("w_hi_ready")
        s_wl = sem("w_lo_ready")
        s_tile = sem("tile_done")
        s_taken = sem("tile_taken")
        s_sq = sem("squares_ready")
        s_ssum = sem("square_sum_done")
        s_var = sem("variance_ready")
        s_root = sem("root_ready")
        s_nrm = sem("normed_ready")
        s_h32 = sem("modulated_ready")
        s_hh = sem("rhs_hi_ready")
        s_rhs = sem("rhs_ready")
        s_dve = sem("dve_steps")
        s_act = sem("act_steps")
        s_dset = sem("dve_waits_settled")
        s_pset = sem("pe_waits_settled")
        s_dtm = sem("dt_done")
        s_dt1 = sem("dt_abs_ready")
        s_dt2 = sem("dt_exp_ready")
        s_dt3 = sem("dt_one_plus_ready")
        s_dt4 = sem("dt_log_ready")
        s_dta = sem("dta_ready")
        s_acs = sem("decay_sums_done")
        s_acv = sem("decay_diffs_ready")
        s_dec = sem("decays_ready")
        s_conv = sem("conv_ready")
        s_xbc = sem("xbc_ready")
        s_tr = sem("transposes_done")
        s_trv = sem("transposes_taken")
        s_cb = sem("cb_done")
        s_cbv = sem("cb_taken")
        s_r = sem("decay_rows_done")
        s_seg = sem("segments_ready")
        s_exp = sem("segment_exp_ready")
        s_sm = sem("scan_matrix_ready")
        s_xdd = sem("decayed_x_ready")
        s_y = sem("y_done")
        s_yv = sem("y_taken")
        s_st = sem("state_ready")
        s_yt = sem("y_transposed")
        s_ygv = sem("y_gated")
        s_ysq = sem("y_squares_ready")
        s_yss = sem("y_square_sum_done")
        s_yvar = sem("y_variance_ready")
        s_ymix = sem("y_and_pool_mixed_ready")
        s_yroot = sem("y_root_ready")
        s_pool = sem("pooled_ready")
        s_pm = sem("pool_mixed_done")
        s_pmv = sem("pool_mixed_taken")
        s_vt = sem("v_tokens_done")
        s_vtv = sem("v_tokens_ready")
        s_z = sem("att_scores_done")
        s_zv = sem("att_scores_ready")
        s_lg = sem("att_log_ready")
        s_nlk = sem("att_keep_ready")
        s_cum = sem("att_sums_done")
        s_arg = sem("att_exponent_ready")
        s_w = sem("att_exp_ready")
        s_wm = sem("att_weights_ready")
        s_ay = sem("att_out_done")
        s_ayv = sem("att_out_taken")
        s_sc = sem("key_scores_done")
        s_scv = sem("key_scores_taken")
        s_shift = sem("gate_exponent_ready")
        s_gexp = sem("gate_exp_ready")
        s_rt = sem("route_ready")
        s_rtt = sem("route_transposed")
        s_idx = sem("route_rows_ready")
        s_oh = sem("one_hots_ready")
        s_gm = sem("gate_matrices_done")
        s_gv = sem("gate_matrices_taken")
        s_gst = [sem(f"gates_stored{s}") for s in range(2)]
        s_gin = [sem(f"gates_in{s}") for s in range(2)]
        s_ast = [sem(f"act_stored{s}") for s in range(2)]
        s_ain = [sem(f"act_in{s}") for s in range(2)]
        s_coef = sem("coef_ready")
        s_out = sem("out_sum_done")
        s_fin = sem("result_ready")
        s_ret = sem("result_stored")

        block = ctx.enter_context(nc.Block())
        @block.sync
        def _(sp):
            sp.dma_start(x[:, :, :], xT).then_inc(s_in, 16)
            sp.dma_start(cond[:, :], cT).then_inc(s_in, 16)
            sp.dma_start(fin_g[:, :], final_g).then_inc(s_in, 16)

            def load_w(l, n, s):
                sp.dma_start(w_raw[:, s, :], wst[l, n]).then_inc(s_raw[s], 16)

            def next_w(l, n, s):
                sp.wait_ge(s_wh, l * STREAM + n + 1)
                sp.wait_ge(s_wl, l * STREAM + n + 1)
                load_w(l, n + 2, s)

            def store_act(l, p, s):
                sp.wait_ge(s_taken, l * TAKEN + p * 2 + (U0 + 4))
                sp.dma_start(a_dram[p], act_out[:, s, :, :]).then_inc(s_ast[s], 16)

            def load_group(l, g, h, s):
                for q in range(2):
                    sp.wait_ge(s_ast[q], (l * GROUPS + g + 2) * 16)
                sp.dma_start(act_in[s][:, :, :, :], a_dram[bass.ds(g * 2, 2)].rearrange("q p b t -> p q b t")
                             ).then_inc(s_ain[s], 16)
                sp.dma_start(gates[s][:, :, :, :],
                             g_dram[:, :, bass.ds(g * GROUP, GROUP), :].rearrange("c p b t -> p c b t")
                             ).then_inc(s_gin[s], 16)

            def load_ada(src, cb, half, slot):
                sp.dma_start(ada_buf[:, slot, :, :], adaw[src, cb * 2 + half]).then_inc(s_ada[slot], 16)

            for c in range(4):
                load_ada(LAYERS - 1, c // 2, c % 2, c)
            with sp.Fori(1, ADA_BLOCKS // 2) as i:
                for c in range(4):
                    sp.wait_ge(s_adat, i * (4 * ADA_ROWS) + (c - 3) * ADA_ROWS)
                    load_ada(LAYERS - 1, i * 2 + c // 2, c % 2, c)

            with sp.Fori(0, LAYERS) as l:
                sp.wait_ge(s_gate, l + 1)
                sp.dma_start(par[:, :], params[l]).then_inc(s_par, 16)
                load_w(l, 0, 0)
                load_w(l, 1, 1)
                with sp.Fori(0, OUT0 // 2) as i:
                    for s in range(2):
                        next_w(l, i * 2 + s, s)
                with sp.Fori(0, N_OUT // 2) as i:
                    for s in range(2):
                        next_w(l, i * 2 + OUT0 + s, s)
                sp.wait_ge(s_rhs, l * RHS_PARTS + KT + 1)
                sp.dma_start(keys[:, :, :], keysT[l]).then_inc(s_keys, 16)
                with sp.Fori(0, N_Q // 2) as i:
                    for s in range(2):
                        next_w(l, i * 2 + WQ0 + s, s)
                def groups(first, times):
                    with sp.Fori(first, first + times) as g:
                        for s in range(2):
                            for j in range(2):
                                next_w(l, g * GROUP + (U0 + 2 + 2 * s + j), j)
                            store_act(l, g * 2 + s, s)

                next_w(l, U0, 0)
                next_w(l, U0 + 1, 1)
                groups(0, G_REST0 + 1)
                for s in range(2):
                    sp.wait_ge(s_gst[s], (l * (GCHUNKS // 2) + GCHUNKS // 2) * 16)
                load_group(l, 0, 0, 0)
                groups(G_REST0 + 1, 1)
                load_ada(l, 0, 0, 0)
                load_group(l, 1, 0, 1)
                groups(G_REST0 + 2, GROUPS - 1 - (G_REST0 + 2))
                load_ada(l, 0, 1, 1)
                for j in range(2):
                    next_w(l, (EV0 - 2) + j, j)
                store_act(l, N_KEYS // 2 - 2, 0)
                store_act(l, N_KEYS // 2 - 1, 1)
                with sp.Fori(0, GROUPS // 2 - 1) as h:
                    for s in range(2):
                        for j in range(GROUP):
                            next_w(l, h * (2 * GROUP) + (EV0 + s * GROUP + j), j % 2)
                        sp.wait_ge(s_coef, l * N_KEYS + h * (2 * GROUP) + (s * GROUP + GROUP))
                        load_group(l, h * 2 + (2 + s), h + 1, s)
                        sp.wait_ge(s_adat, (l + 1) * ADA_TERMS + h * KT + (s + 1) * ADA_ROWS)
                        load_ada(l, h + 1, s, s)
                for j in range(2 * GROUP - 2):
                    next_w(l, (STREAM - 2 * GROUP) + j, j % 2)
            sp.wait_ge(s_fin, 1)
            sp.dma_start(outT, x[:, :, :]).then_inc(s_ret, 16)
            sp.wait_ge(s_ret, 16)

        @block.gpsimd
        def _(pool):
            pool.memset(ones[:, :], 1.0).then_inc(s_const, 1)
            pool.memset(ident[:, :], 0.0).then_inc(s_const, 1)
            pool.memset(tri_le[:, :], 1.0).then_inc(s_const, 1)
            pool.memset(tri_ge[:, :], 1.0).then_inc(s_const, 1)
            pool.memset(tri_lt[:, :], 1.0).then_inc(s_const, 1)
            pool.iota(iota[:, :], pattern=[[1, P]], base=0, channel_multiplier=0,
                      allow_small_or_imprecise_dtypes=True).then_inc(s_const, 1)
            pool.iota(inv_count[:, :, :], pattern=[[0, 2], [1, T]], base=1, channel_multiplier=0,
                      allow_small_or_imprecise_dtypes=True).then_inc(s_const, 1)
            pool.wait_ge(s_const, 7)
            pool.affine_select(out=ident[:, :], in_=ident[:, :], compare_op=ALU.not_equal, fill=1.0,
                               base=0, pattern=[[-1, P]], channel_multiplier=1).then_inc(s_const, 1)
            pool.affine_select(out=tri_le[:, :], in_=tri_le[:, :], compare_op=ALU.is_ge, fill=0.0,
                               base=0, pattern=[[1, P]], channel_multiplier=-1).then_inc(s_const, 1)
            pool.affine_select(out=tri_ge[:, :], in_=tri_ge[:, :], compare_op=ALU.is_ge, fill=0.0,
                               base=0, pattern=[[-1, P]], channel_multiplier=1).then_inc(s_const, 1)
            pool.affine_select(out=tri_lt[:, :], in_=tri_lt[:, :], compare_op=ALU.is_gt, fill=0.0,
                               base=0, pattern=[[1, P]], channel_multiplier=-1).then_inc(s_const, 1)

        @block.scalar
        def _(act):
            steps = Steps(act, s_act)

            def hi(l, half, s, n=None):
                act.wait_ge(s_raw[s], (l * (STREAM // 2) + half + 1) * 16)
                if n is not None:
                    act.wait_ge(s_tile, l * STREAM + n + 1)
                nc.scalar.activation(w_hi[s][:, :, :].rearrange("p a b -> p (a b)"), w_raw[:, s, :],
                                     ACT.Copy).then_inc(s_wh, 1)

            def norm_squares(k0, k1):
                nc.scalar.activation(h32[:, k0:k1, :], x[:, k0:k1, :], ACT.Square).then_inc(s_sq, 1)

            def root(sem_in, val, src, dst, sem_out):
                act.wait_ge(sem_in, val)
                nc.scalar.activation(dst, src, ACT.Sqrt).then_inc(sem_out, 1)

            def normed_hi(l, which):
                for k in range(KT):
                    act.wait_ge(s_nrm, l * 2 * KT + (which * KT + k + 1))
                    nc.scalar.activation(hH[:, k, :], h32[:, k, :], ACT.Identity,
                                         bias=mod[:, 3 * which, k:k + 1]).then_inc(s_hh, 1)

            act.wait_ge(s_in, 48)
            nc.scalar.activation(tiny[:, 0, 0:KT], cond[:, :], ACT.Silu).then_inc(s_cond, 1)

            with act.Fori(0, LAYERS) as l:
                steps.base, steps.n = l * ACT_STEPS, 0
                act.wait_ge(s_gate, l + 1)
                for k in range(0, KT, 2):
                    norm_squares(k, k + 2)
                hi(l, 0, 0)
                hi(l, 0, 1)
                root(s_var, l * 2 + 1, nrm[:, 0, :], nrm[:, 1, :], s_root)
                normed_hi(l, 0)
                def in_tile(half, s, n, fn=ACT.Copy):
                    hi(l, half + 1, s, n)
                    nc.scalar.activation(pj[:, n, PAD:PJW], bank[s][:, :], fn).then_inc(s_taken, 1)

                with act.Fori(0, LOOSE // 2) as i:
                    for s in range(2):
                        in_tile(i, s, i * 2 + s)
                for n in range(LOOSE, N_IN):
                    in_tile(n // 2, n % 2, n, ACT.Silu if Z0 <= n < Z0 + 4 else ACT.Copy)
                    if LOOSE < n <= LOOSE + 6:
                        j = n - LOOSE - 1
                        act.wait_ge(s_conv, l * 6 + j + 1)
                        nc.scalar.activation(xbc[:, j, :], xbc[:, j, :], ACT.Silu).then_inc(s_xbc, 1)
                    if n == DT_TILE + 1:
                        act.wait_ge(s_dt1, l + 1)
                        nc.scalar.activation(tiny[:, 3, :], tiny[:, 2, :], ACT.Exp)
                        nc.scalar.activation(tiny[:, 4, 0:HEADS], pcol("a_log"), ACT.Exp).then_inc(s_dt2, 1)
                        act.wait_ge(s_dt3, l + 1)
                        nc.scalar.activation(tiny[:, 6, :], tiny[:, 5, :], ACT.Ln).then_inc(s_dt4, 1)
                act.wait_ge(s_acv, l + 1)
                nc.scalar.activation(tiny[:, 9, :], tiny[:, 8, :], ACT.Exp)
                nc.scalar.activation(tiny[:, 11, :], tiny[:, 10, :], ACT.Exp)
                nc.scalar.activation(tiny[:, 13, :], tiny[:, 12, :], ACT.Exp).then_inc(s_dec, 1)
                for tt in range(NT):
                    for g in range(2):
                        act.wait_ge(s_seg, l * 8 + tt * 2 + g + 1)
                        nc.scalar.activation(seg[:, g, :], seg[:, g, :], ACT.Exp).then_inc(s_exp, 1)
                def att_logs(h):
                    act.wait_ge(s_zv, l * 4 + h + 1)
                    if h >= 1:
                        act.wait_ge(s_nlk, l * 4 + h)
                    steps.link(nc.scalar.activation(ez[:, :], zs[h % 2][:, :], ACT.Abs))
                    steps.link(nc.scalar.activation(ez[:, :], ez[:, :], ACT.Exp, scale=-1.0))
                    nc.scalar.activation(ez[:, :], ez[:, :], ACT.Ln, bias=ones[:, 0:1]).then_inc(s_lg, 1)

                act.wait_ge(s_ygv, l * 4 + 4)
                nc.scalar.activation(y_tok[:, :, :], xbc[:, 0:4, :], ACT.Square).then_inc(s_ysq, 1)
                att_logs(0)
                root(s_yvar, l * 2 + 1, nrm[:, 0, :], nrm[:, 1, :], s_yroot)
                root(s_yvar, l * 2 + 2, nrm[:, 0, :], nrm[:, 1, :], s_yroot)
                att_logs(1)
                act.wait_ge(s_ymix, l + 1)
                nc.scalar.activation(hH[:, 0:6, :], mixed[:, 0:6, :], ACT.Copy).then_inc(s_hh, 1)
                for h in range(SB_HEADS):
                    act.wait_ge(s_arg, l * 4 + h + 1)
                    nc.scalar.activation(arg[h % 2][:, :], arg[h % 2][:, :], ACT.Exp).then_inc(s_w, 1)
                    if h + 2 < SB_HEADS:
                        att_logs(h + 2)
                act.wait_ge(s_ayv, l * 4 + 4)
                nc.scalar.activation(hH[:, 6:8, :], mixed[:, 6:8, :], ACT.Copy).then_inc(s_hh, 1)
                for n in range(N_OUT):
                    hi(l, n // 2 + (OUT0 // 2 + 1), n % 2, OUT0 + n)
                    if n % 2 == 1:
                        act.wait_ge(s_rhs, l * RHS_PARTS + KT + 1)
                        if n >= 3:
                            act.wait_ge(s_taken, l * TAKEN + (OUT0 + n - 2 + 3))
                            norm_squares(n - 3, n - 1)
                act.wait_ge(s_taken, l * TAKEN + WQ0 + 2)
                norm_squares(N_OUT - 2, N_OUT)
                root(s_var, l * 2 + 2, nrm[:, 0, :], nrm[:, 1, :], s_root)
                normed_hi(l, 1)
                with act.Fori(0, N_Q // 2) as i:
                    for s in range(2):
                        hi(l, i + (WQ0 // 2 + 1), s, i * 2 + (WQ0 + s))
                        act.wait_ge(s_sc, l * N_Q + i * 2 + s + 1)
                        nc.scalar.activation(qT[:, s, :], bank[s][:, :], ACT.Copy).then_inc(s_taken, 1)
                def u_block(g, j):
                    hi(l, g * (GROUP // 2) + (U0 // 2 + j // 2 + 1), j % 2, g * GROUP + (U0 + j))
                    if j % 2 == 0:
                        act.wait_ge(s_ast[j // 2], (l * GROUPS + g + 1) * 16)
                    nc.scalar.activation(act_out[:, j // 2, j % 2, :], bank[j % 2][:, :], ACT.Gelu).then_inc(s_taken, 1)

                with act.Fori(0, NT) as tt:
                    for m in range(G_PICK * GROUP):
                        u_block(tt * G_PICK + m // GROUP, m % GROUP)
                        if m == 6:
                            act.wait_ge(s_shift, l * NT + tt + 1)
                            nc.scalar.activation(bestv[:, :, :], bestv[:, :, :], ACT.Exp).then_inc(s_gexp, 1)
                    act.wait_ge(s_rtt, l * NT + tt + 1)
                    nc.scalar.activation(idxT[:, :, bass.ds(tt * P, P)],
                                         bank[2][:, 0:3 * P].rearrange("p (a b) -> p a b", a=3),
                                         ACT.Copy).then_inc(s_idx, 1)
                def store_chunk(c2, s, first):
                    if not first:
                        act.wait_ge(s_gst[s], (l * (GCHUNKS // 2) + c2) * 16)
                    with act.Fori(0, G_CHUNK) as i:
                        for j in range(GROUP):
                            u_block(c2 * (2 * G_CHUNK) + i + (G_GATE0 + s * G_CHUNK), j)
                            for u in range(TILE_QUADS):
                                q = i * (GROUP * TILE_QUADS) + (j * TILE_QUADS + u)
                                act.wait_ge(s_gm, l * QUADS + c2 * (2 * GCHUNK // QUAD) + (s * (GCHUNK // QUAD) + 3) + q)
                                nc.scalar.activation(
                                    stage[s][:, :, bass.ds(q * QUAD, QUAD)].rearrange("p e t -> p t e"),
                                    bank[2 + u][:, :].rearrange("p (t e) -> p t e", t=QUAD),
                                    ACT.Copy).then_inc(s_gv, 1)
                    act.wait_ge(s_gv, l * QUADS + c2 * (2 * GCHUNK // QUAD) + ((s + 1) * (GCHUNK // QUAD)) + 2)
                    act.dma_start(g_dram[c2 * 2 + s].rearrange("p e t -> p (e t)"),
                                  stage[s][:, :, :].rearrange("p e t -> p (e t)")).then_inc(s_gst[s], 16)

                store_chunk(0, 0, True)
                store_chunk(0, 1, True)
                with act.Fori(1, GCHUNKS // 2) as c2:
                    store_chunk(c2, 0, False)
                    store_chunk(c2, 1, False)

                with act.Fori(G_REST0, GROUPS) as g:
                    for j in range(GROUP):
                        u_block(g, j)
                with act.Fori(0, N_KEYS // 2 - 1) as i:
                    for s in range(2):
                        hi(l, i + (EV0 // 2 + 1), s, i * 2 + (EV0 + s))
                assert steps.n == ACT_STEPS, steps.n
            act.wait_ge(s_gate, LAYERS + 1)
            for k in range(0, KT, 2):
                norm_squares(k, k + 2)
            root(s_var, LAYERS * 2 + 1, nrm[:, 0, :], nrm[:, 1, :], s_root)

        @block.tensor
        def _(pe):
            mm = nc.tensor.matmul
            steps = Steps(pe, None, s_pset)

            def project(l, n, s, rhs=None):
                pe.wait_ge(s_wh, l * STREAM + n + 1)
                pe.wait_ge(s_wl, l * STREAM + n + 1)
                pe.wait_ge(s_taken, l * TAKEN + n + 1)
                for k in range(KT):
                    if rhs is not None:
                        pe.wait_ge(s_rhs, rhs + k + 1)
                    for a, b in ((w_hi, hH), (w_hi, hL), (w_lo, hH)):
                        last = mm(bank[s][:, :], a[s][:, k, :], b[:, k, :],
                                  start=(k == 0 and a is w_hi and b is hH),
                                  stop=(k == KT - 1 and a is w_lo))
                last.then_inc(s_tile, 1)

            def norm_sum(first):
                for k in range(KT):
                    if k % 2 == 0:
                        pe.wait_ge(s_sq, first + k // 2 + 1)
                    last = mm(bank[2][:, :], ones[:, :], h32[:, k, :], start=(k == 0), stop=(k == KT - 1))
                last.then_inc(s_ssum, 1)

            pe.sem_inc(s_taken, 2)
            pe.sem_inc(s_scv, 2)
            pe.sem_inc(s_sc, 2)
            pe.sem_inc(s_gv, 2)
            pe.sem_inc(s_gm, 2)
            pe.sem_inc(s_ast[0], 16)
            pe.sem_inc(s_ast[1], 16)
            pe.wait_ge(s_const, 11)
            pe.wait_ge(s_cond, 1)

            with pe.Fori(0, LAYERS) as l:
                def modulation(b, first, last_col):
                    for c in range(first, last_col):
                        ins = mm(bank[b][:, c:c + 1], ada_acc[:, c * P:(c + 1) * P], ones[:, 0:1], start=True, stop=True)
                    ins.then_inc(s_adam, 1)

                pe.wait_ge(s_adat, (l + 1) * ADA_TERMS)
                pe.wait_ge(s_gate, l + 1)
                modulation(3, 0, 2 * KT)
                norm_sum(l * KT)
                modulation(5, 2 * KT, 4 * KT)
                project(l, 0, 0, rhs=l * RHS_PARTS)
                project(l, 1, 1)
                with pe.Fori(1, DT_TILE // 2) as i:
                    for s in range(2):
                        project(l, i * 2 + s, s)
                modulation(5, 4 * KT, 6 * KT)
                pe.wait_ge(s_h32, l + 1)
                w_dt = pcol("w_dt").rearrange("p (k h) -> p k h", k=KT)
                for tt in range(NT):
                    for k in range(KT):
                        last = mm(bank[4][:, tt * HEADS:(tt + 1) * HEADS], h32[:, k, tt * P:(tt + 1) * P],
                                  w_dt[:, k, :], start=(k == 0), stop=(k == KT - 1))
                last.then_inc(s_dtm, 1)
                with pe.Fori(DT_TILE // 2, N_IN // 2) as i:
                    for s in range(2):
                        project(l, i * 2 + s, s)
                pe.wait_ge(s_dta, l + 1)
                mm(bank[5][:, 0:32], tri_le[:, :], tiny[:, 7, :], start=True, stop=True)
                mm(bank[5][:, 32:64], ones[:, :], tiny[:, 7, :], start=True, stop=True).then_inc(s_acs, 1)
                pe.wait_ge(s_pool, l + 1)
                pw = pcol("pool_w").rearrange("p (j c) -> p j c", j=2)
                for j in range(2):
                    last = mm(bank[6 + j][:, :], pw[:, j, :], pooled[:, j, :], start=True, stop=True)
                last.then_inc(s_pm, 1)
                pe.wait_ge(s_xbc, l * 6 + 6)
                for tt in range(NT):
                    if tt >= 2:
                        pe.wait_ge(s_trv, l * 5 + tt - 1)
                    for j in range(4):
                        last = nc.tensor.transpose(bank[2 + tt % 2][:, j * P:(j + 1) * P],
                                                   xbc[:, j, tt * P:(tt + 1) * P], ident[:, :])
                    last.then_inc(s_tr, 1)
                for tt in range(NT):
                    last = nc.tensor.transpose(bank[4][:, tt * P:(tt + 1) * P],
                                               xbc[:, 4, tt * P:(tt + 1) * P], ident[:, :])
                last.then_inc(s_tr, 1)
                pe.wait_ge(s_taken, l * TAKEN + N_IN + 2)
                for j in range(2):
                    for tt in range(NT):
                        last = nc.tensor.transpose(bank[j][:, tt * P:(tt + 1) * P],
                                                   pj[:, V0 + j, PAD + tt * P:PAD + (tt + 1) * P], ident[:, :])
                last.then_inc(s_vt, 1)
                pe.wait_ge(s_pmv, l + 1)
                pe.wait_ge(s_acv, l + 1)
                for g in range(2):
                    r = slice(64 * g, 64 * g + 64)
                    for tt in range(NT):
                        t = slice(tt * P, (tt + 1) * P)
                        last = mm(bank[5 + g][:, t], xbc[r, 4, t], xbc[r, 5, t], start=True, stop=True)
                    last.then_inc(s_cb, 1)
                dta = tiny[:, 7, :].rearrange("p (t h) -> p t h", t=NT)

                def decay_rows(tt, g):
                    for h in range(4):
                        last = mm(bank[7 if g == 0 else 2][:, h * P:(h + 1) * P],
                                  dta[:, tt, 4 * g + h:4 * g + h + 1].broadcast_to([P, P]), tri_le[:, :],
                                  start=True, stop=True)
                    last.then_inc(s_r, 1)

                pe.wait_ge(s_trv, l * 5 + 5)
                for tt in range(NT):
                    for g in range(2):
                        if tt >= 1:
                            pe.wait_ge(s_seg, l * 8 + tt * 2 + g - 1)
                        decay_rows(tt, g)
                    if tt == 0:
                        pe.wait_ge(s_cbv, l * 2 + 2)
                    else:
                        pe.wait_ge(s_yv, l * NT + tt)
                    for g in range(2):
                        pe.wait_ge(s_sm, l * 8 + tt * 2 + g + 1)
                        for h in range(4):
                            hh = 4 * g + h
                            last = mm(bank[3][:, hh * HD:(hh + 1) * HD], smat[:, g, h * P:(h + 1) * P],
                                      xdt[:, tt, hh * HD:(hh + 1) * HD], start=True, stop=True)
                    if tt >= 1:
                        pe.wait_ge(s_st, l * 3 + tt)
                        for g in range(2):
                            r = slice(64 * g, 64 * g + 64)
                            last = mm(bank[4 + 2 * g][:, 0:256], xbc[r, 5, tt * P:(tt + 1) * P],
                                      state[r, :], start=True, stop=True)
                    if tt < NT - 1:
                        pe.wait_ge(s_xdd, l * 3 + tt + 1)
                        for g in range(2):
                            r = slice(64 * g, 64 * g + 64)
                            last = mm(bank[5][r, 0:256], b_tok[:, tt, r], xdd[:, g * 256:(g + 1) * 256],
                                      start=True, stop=True)
                    last.then_inc(s_y, 1)
                pe.wait_ge(s_yv, l * NT + NT)
                pe.wait_ge(s_seg, l * 8 + 8)
                for j in range(4):
                    b = (2, 3, 4, 5)[j]
                    for tt in range(NT):
                        last = nc.tensor.transpose(bank[b][:, tt * P:(tt + 1) * P],
                                                   y_tok[:, tt, j * P:(j + 1) * P], ident[:, :])
                    last.then_inc(s_yt, 1)
                zb = [(2, 0), (3, 0), (4, 0), (4, 256)]
                cb = [(5, 0), (6, 0), (7, 0), (7, 256)]

                def att_scores(h):
                    r = slice(64 * (h % 2), 64 * (h % 2) + 64)
                    if h >= 1:
                        pe.wait_ge(s_zv, l * 4 + h)
                    for i in range(NT):
                        b, o = zb[i]
                        last = mm(bank[b][:, o:o + W4[i]], pj[r, K0 + h // 2, PAD + i * P:PAD + (i + 1) * P],
                                  pj[r, Q0 + h // 2, PAD + i * P:PJW], start=True, stop=True)
                    last.then_inc(s_z, 1)

                def att_sums(h):
                    pe.wait_ge(s_nlk, l * 4 + h + 1)
                    if h >= 1:
                        pe.wait_ge(s_arg, l * 4 + h)
                    for i in range(NT):
                        b, o = cb[i]
                        for j in range(i, NT):
                            last = mm(bank[b][:, o + (j - i) * P:o + W4[i]], tri_ge[:, :] if j == i else ones[:, :],
                                      nlk[h % 2][:, O4[j]:O4[j] + W4[j]], start=(j == i), stop=(j == NT - 1))
                    last.then_inc(s_cum, 1)

                def att_out(h):
                    r = slice(64 * (h % 2), 64 * (h % 2) + 64)
                    pe.wait_ge(s_wm, l * 4 + h + 1)
                    if h == 0:
                        pe.wait_ge(s_ymix, l + 1)
                    if h >= 2:
                        pe.wait_ge(s_ayv, l * 4 + h - 1)
                    for i in range(NT):
                        last = mm(bank[h % 2][r, i * P:T], v_tok[:, i, h * HD:(h + 1) * HD],
                                  arg[h % 2][:, O4[i]:O4[i] + W4[i]], start=(i == 0), stop=(i == NT - 1))
                    last.then_inc(s_ay, 1)

                pe.wait_ge(s_ygv, l * 4 + 4)
                att_scores(0)
                pe.wait_ge(s_ysq, l + 1)
                pe.wait_ge(s_vtv, l + 1)
                for g in range(2):
                    for k in range(2):
                        last = mm(bank[g][:, :], ones[:, :], y_tok[:, 2 * g + k, :], start=(k == 0), stop=(k == 1))
                    last.then_inc(s_yss, 1)
                att_scores(1)
                for h in range(SB_HEADS):
                    att_sums(h)
                    if h + 2 < SB_HEADS:
                        att_scores(h + 2)
                    if h >= 1:
                        att_out(h - 1)
                att_out(SB_HEADS - 1)
                pe.wait_ge(s_rhs, l * RHS_PARTS + KT + 1)
                steps.settle()
                with pe.Fori(0, N_OUT // 2) as i:
                    for s in range(2):
                        project(l, i * 2 + (OUT0 + s), s)
                norm_sum(l * KT + KT // 2)
                pe.wait_ge(s_keys, (l + 1) * 16)
                def scores(n, s):
                    pe.wait_ge(s_taken, l * TAKEN + n + (WQ0 + 3))
                    pe.wait_ge(s_scv, l * N_Q + n + 1)
                    for tt in range(NT):
                        last = mm(bank[2 + s][:, tt * P:(tt + 1) * P], qT[:, s, tt * P:(tt + 1) * P],
                                  keys[:, bass.ds(n, 1), :].rearrange("p a b -> p (a b)"),
                                  start=True, stop=True)
                    last.then_inc(s_sc, 1)

                project(l, WQ0, 0, rhs=l * RHS_PARTS + KT + 1)
                with pe.Fori(0, N_Q // 2 - 1) as i:
                    for s in range(2):
                        project(l, i * 2 + (WQ0 + s + 1), 1 - s)
                        scores(i * 2 + s, s)
                project(l, WQ0 + N_Q - 1, 1)
                scores(N_Q - 2, 0)
                scores(N_Q - 1, 1)
                with pe.Fori(0, NT) as tt:
                    for m in range(G_PICK * GROUP):
                        project(l, tt * (G_PICK * GROUP) + (U0 + m), m % 2)
                    pe.wait_ge(s_rt, l * NT + tt + 1)
                    for a in range(3):
                        last = nc.tensor.transpose(bank[2][:, a * P:(a + 1) * P], route[:, a, :], ident[:, :])
                    last.then_inc(s_rtt, 1)
                pe.wait_ge(s_idx, l * NT + NT)
                steps.settle()
                with pe.Fori(0, G_GATE) as i:
                    for j in range(GROUP):
                        project(l, i * GROUP + (U0 + G_GATE0 * GROUP + j), j % 2)
                        for u in range(TILE_QUADS):
                            q = i * (GROUP * TILE_QUADS) + (j * TILE_QUADS + u)
                            pe.wait_ge(s_oh, l * QUADS + 1 + q)
                            pe.wait_ge(s_gv, l * QUADS + 1 + q)
                            for t in range(QUAD):
                                last = mm(bank[2 + u][:, t * P:(t + 1) * P], oneh[:, u, t, :], gateh[:, u, t, :],
                                          start=True, stop=True)
                            last.then_inc(s_gm, 1)
                with pe.Fori(G_REST0, GROUPS) as g:
                    for j in range(GROUP):
                        project(l, g * GROUP + (U0 + j), j % 2)

                def v_block(b, j, first=False, final=False):
                    pe.wait_ge(s_wh, l * STREAM + b + (EV0 + 1))
                    pe.wait_ge(s_wl, l * STREAM + b + (EV0 + 1))
                    pe.wait_ge(s_coef, l * N_KEYS + b + 1)
                    for k in range(KT):
                        for w, c in ((w_hi, c_hi), (w_hi, c_lo), (w_lo, c_hi)):
                            last = mm(bank[k][:, :], w[j % 2][:, k, :], c[:, j, :],
                                      start=(first and w is w_hi and c is c_hi), stop=(final and w is w_lo))
                        if final and k < KT - 1:
                            last.then_inc(s_out, 1)
                    last.then_inc(s_tile, 1)

                pe.wait_ge(s_taken, l * TAKEN + TAKEN + 2)
                pe.wait_ge(s_gv, l * QUADS + QUADS + 2)
                for j in range(GROUP):
                    v_block(j, j, first=(j == 0))
                with pe.Fori(1, GROUPS - 1) as g:
                    for j in range(GROUP):
                        v_block(g * GROUP + j, j)
                for j in range(GROUP):
                    v_block(N_KEYS - GROUP + j, j, final=(j == GROUP - 1))
            norm_sum(LAYERS * KT)

        @block.vector
        def _(dve):
            steps = Steps(dve, s_dve, s_dset)
            link = steps.link
            v = nc.vector

            def lo(l, half, s, n=None):
                if n is not None:
                    dve.wait_ge(s_tile, l * STREAM + n + 1)
                dve.wait_ge(s_wh, l * STREAM + half * 2 + (s + 1))
                v.tensor_tensor(w_lo[s][:, :, :].rearrange("p a b -> p (a b)"), w_raw[:, s, :],
                                w_hi[s][:, :, :].rearrange("p a b -> p (a b)").bitcast(F32),
                                ALU.subtract).then_inc(s_wl, 1)

            def inv_root(psum, count, sem_var, sem_root, root_val):
                v.tensor_scalar(nrm[:, 0, :], psum, 1.0 / count, EPS, ALU.mult, ALU.add).then_inc(sem_var, 1)
                dve.wait_ge(sem_root, root_val)
                link(v.reciprocal(nrm[:, 2, :], nrm[:, 1, :]))
                link(v.tensor_tensor(nrm[:, 3, :], nrm[:, 2, :], nrm[:, 2, :], ALU.mult))
                link(v.tensor_tensor(nrm[:, 3, :], nrm[:, 3, :], nrm[:, 0, :], ALU.mult))
                link(v.tensor_scalar(nrm[:, 3, :], nrm[:, 3, :], -0.5, 1.5, ALU.mult, ALU.add))
                link(v.tensor_tensor(nrm[:, 2, :], nrm[:, 2, :], nrm[:, 3, :], ALU.mult))

            def normed(l, which):
                dve.wait_ge(s_ssum, l * 2 + which + 1)
                inv_root(bank[2][:, :], D, s_var, s_root, l * 2 + which + 1)

            def modulated(l, which):
                for k in range(KT):
                    v.scalar_tensor_tensor(h32[:, k, :], x[:, k, :], gs[:, which, k:k + 1], nrm[:, 2, :],
                                           ALU.mult, ALU.mult).then_inc(s_nrm, 1)
                for k in range(KT):
                    dve.wait_ge(s_hh, l * HI_PARTS + (which * (KT + 2) + k + 1))
                    v.scalar_tensor_tensor(hL[:, k, :], h32[:, k, :], mod[:, 3 * which, k:k + 1],
                                           hH[:, k, :].bitcast(F32), ALU.add, ALU.subtract).then_inc(s_rhs, 1)

            dve.wait_ge(s_const, 11)
            for j, p0, w in ((0, 0, 2), (0, 64, 4), (1, 0, 8), (1, 64, 16)):
                ins = v.tensor_scalar(inv_count[p0:p0 + 64, j, :], inv_count[p0:p0 + 64, j, :], float(w), None, ALU.min)
            ins.then_inc(s_const, 1)
            dve.wait_ge(s_const, 12)
            v.reciprocal(inv_count[:, :, :], inv_count[:, :, :]).then_inc(s_const, 1)
            dve.wait_ge(s_const, 13)
            dve.wait_ge(s_in, 48)
            v.memset(tiny[:, 15, 0:1], 0.0).then_inc(s_gate, 1)

            def ada_term(done, chunks_in, cb, k, slot):
                q = k % ADA_ROWS
                if q == 0:
                    dve.wait_ge(s_ada[slot], chunks_in)
                acc = ada_acc[:, bass.ds(cb * ADA_W, ADA_W)]
                w, c = ada_buf[:, slot, q, :], tiny[:, 0, k:k + 1]
                if k == 0:
                    ins = v.tensor_scalar(acc, w, c, None, ALU.mult)
                else:
                    dve.wait_ge(s_adat, done)
                    ins = v.scalar_tensor_tensor(acc, w, c, acc, ALU.mult, ALU.add)
                ins.then_inc(s_adat, 1)

            dve.wait_ge(s_cond, 1)
            with dve.Fori(0, ADA_BLOCKS // 2) as i:
                for b in range(2):
                    for k in range(KT):
                        ada_term(i * (2 * KT) + (b * KT + k), (i + 1) * 16, i * 2 + b, k, 2 * b + k // ADA_ROWS)

            with dve.Fori(0, LAYERS) as l:
                steps.base, steps.n = l * DVE_STEPS, 0
                lo(l, 0, 0)
                lo(l, 0, 1)
                dve.wait_ge(s_par, (l + 1) * 16)
                v.memset(pj[:, :, 0:PAD], 0.0)
                normed(l, 0)
                dve.wait_ge(s_adam, l * 3 + 1)
                m1 = mod[:, 0:2, :].rearrange("p a b -> p (a b)")
                link(v.tensor_tensor(m1, bank[3][:, 0:2 * KT], pcol("ada_b")[:, 0:2 * KT], ALU.add))
                link(v.scalar_tensor_tensor(gs[:, 0, :], mod[:, 1, :], 1.0, pcol("g_mix"), ALU.add, ALU.mult))
                modulated(l, 0)
                dve.wait_ge(s_rhs, l * RHS_PARTS + KT)
                for k in range(KT):
                    ins = v.tensor_scalar(h32[:, k, :], h32[:, k, :], mod[:, 0, k:k + 1], None, ALU.add)
                ins.then_inc(s_h32, 1)
                q = lambda n: tiny[:, n, :]

                def in_lo(half, s, n):
                    lo(l, half + 1, s, n)

                def conv(j):
                    dve.wait_ge(s_taken, l * TAKEN + (XS0 + j + 3))
                    src = lambda w: pj[:, XS0 + j, PAD - 3 + w:PJW - 3 + w]
                    link(v.tensor_scalar(xbc[:, j, :], src(0), cw[:, j, 0:1], pcol("conv_b")[:, j:j + 1],
                                         ALU.mult, ALU.add))
                    for w in (1, 2):
                        link(v.scalar_tensor_tensor(xbc[:, j, :], src(w), cw[:, j, w:w + 1], xbc[:, j, :],
                                                    ALU.mult, ALU.add))
                    v.scalar_tensor_tensor(xbc[:, j, :], src(3), cw[:, j, 3:4], xbc[:, j, :],
                                           ALU.mult, ALU.add).then_inc(s_conv, 1)

                def time_step():
                    dve.wait_ge(s_dtm, l + 1)
                    bias = pcol("dt_bias").unsqueeze(1).broadcast_to([P, NT, HEADS])
                    link(v.tensor_tensor(q(1).rearrange("p (t h) -> p t h", t=NT),
                                         bank[4][:, 0:32].rearrange("p (t h) -> p t h", t=NT), bias, ALU.add))
                    v.scalar_tensor_tensor(q(2), q(1), -1.0, q(1), ALU.mult, ALU.min).then_inc(s_dt1, 1)
                    dve.wait_ge(s_dt2, l + 1)
                    v.tensor_scalar(q(5), q(3), 1.0, None, ALU.add).then_inc(s_dt3, 1)
                    dve.wait_ge(s_dt4, l + 1)
                    link(v.tensor_scalar(q(14), q(5), -1.0, None, ALU.add))
                    link(v.tensor_scalar(q(15), q(14), 0.0, None, ALU.is_equal))
                    link(v.tensor_tensor(q(14), q(14), q(15), ALU.add))
                    link(v.tensor_tensor(q(15), q(6), q(15), ALU.add))
                    link(v.reciprocal(q(14), q(14)))
                    link(v.tensor_tensor(q(15), q(15), q(14), ALU.mult))
                    link(v.tensor_tensor(q(15), q(15), q(3), ALU.mult))
                    link(v.scalar_tensor_tensor(q(1), q(1), 0.0, q(15), ALU.max, ALU.add))
                    ea = tiny[:, 4, 0:HEADS].unsqueeze(1).broadcast_to([P, NT, HEADS])
                    v.scalar_tensor_tensor(q(7).rearrange("p (t h) -> p t h", t=NT),
                                           q(1).rearrange("p (t h) -> p t h", t=NT), -1.0, ea,
                                           ALU.mult, ALU.mult).then_inc(s_dta, 1)

                with dve.Fori(0, LOOSE // 2) as i:
                    for s in range(2):
                        in_lo(i, s, i * 2 + s)
                cw = pcol("conv_w").rearrange("p (j w) -> p j w", j=6)
                xp = pj[:, XP0:XP0 + 2, :]
                for n in range(LOOSE, N_IN):
                    in_lo(n // 2, n % 2, n)
                    if n < LOOSE + 6:
                        conv(n - LOOSE)
                    if n == DT_TILE:
                        dve.wait_ge(s_adam, l * 3 + 3)
                        m2 = mod[:, 2:6, :].rearrange("p a b -> p (a b)")
                        link(v.tensor_tensor(m2, bank[5][:, 2 * KT:6 * KT], pcol("ada_b")[:, 2 * KT:6 * KT], ALU.add))
                        link(v.scalar_tensor_tensor(gs[:, 1, :], mod[:, 4, :], 1.0, pcol("g_ffn"), ALU.add, ALU.mult))
                        time_step()
                    if n == LOOSE + 6:
                        dve.wait_ge(s_taken, l * TAKEN + (XP0 + 1 + 3))
                        link(v.tensor_tensor(pool_a[:, :, 1:], xp[:, :, 1:], xp[:, :, :PJW - 1], ALU.add))
                        link(v.tensor_tensor(pool_b[:, :, 3:], pool_a[:, :, 3:], pool_a[:, :, 1:PJW - 2], ALU.add))
                    if n == LOOSE + 7:
                        for p0, j, src in ((0, 0, pool_a), (64, 0, pool_b)):
                            v.tensor_tensor(pooled[p0:p0 + 64, j, :], src[p0:p0 + 64, j, PAD:], inv_count[p0:p0 + 64, j, :], ALU.mult)
                        link(v.tensor_tensor(pool_c[:, 1, 7:], pool_b[:, 1, 7:], pool_b[:, 1, 3:PJW - 4], ALU.add))
                    if n == LOOSE + 8:
                        link(v.tensor_tensor(pool_a[:, 1, 15:], pool_c[:, 1, 15:], pool_c[:, 1, 7:PJW - 8], ALU.add))
                        for p0, j, src in ((0, 1, pool_c), (64, 1, pool_a)):
                            ins = v.tensor_tensor(pooled[p0:p0 + 64, j, :], src[p0:p0 + 64, j, PAD:], inv_count[p0:p0 + 64, j, :], ALU.mult)
                        link(ins)
                    if n == LOOSE + 9:
                        v.tensor_tensor(pooled[:, :, :], pooled[:, :, :], xp[:, :, PAD:], ALU.subtract).then_inc(s_pool, 1)
                dve.wait_ge(s_acs, l + 1)
                link(v.tensor_copy(q(8), bank[5][:, 0:32]))
                v.tensor_copy(q(12), bank[5][:, 32:64])
                v.tensor_tensor(q(10), bank[5][:, 32:64], q(8), ALU.subtract).then_inc(s_acv, 1)
                dve.wait_ge(s_pm, l + 1)
                for j in range(2):
                    ins = v.tensor_scalar(mixed[:, 4 + j, :], bank[6 + j][:, :], pcol("pool_scale")[:, j:j + 1], None, ALU.mult)
                ins.then_inc(s_pmv, 1)
                def by_head(n, tt):
                    return tiny[:, n, tt * HEADS:(tt + 1) * HEADS].unsqueeze(2).broadcast_to([P, HEADS, HD])

                def heads(ap):
                    return ap.rearrange("p (h c) -> p h c", c=HD)

                for tt in range(NT):
                    dve.wait_ge(s_tr, l * 5 + tt + 1)
                    v.tensor_tensor(heads(xdt[:, tt, :]), heads(bank[2 + tt % 2][:, :]), by_head(1, tt),
                                    ALU.mult).then_inc(s_trv, 1)
                dve.wait_ge(s_tr, l * 5 + 5)
                v.tensor_copy(b_tok[:, :, :].rearrange("p a b -> p (a b)"), bank[4][:, :]).then_inc(s_trv, 1)
                dve.wait_ge(s_vt, l + 1)
                for j in range(2):
                    ins = v.tensor_copy(v_tok[:, :, j * P:(j + 1) * P], bank[j][:, :].rearrange("p (t c) -> p t c", t=NT))
                ins.then_inc(s_vtv, 1)
                for g in range(2):
                    dve.wait_ge(s_cb, l * 2 + g + 1)
                    v.tensor_tensor(cbm[:, g, :, :], bank[5 + g][:, :].rearrange("p (t c) -> p t c", t=NT),
                                    tri_le[:, :].unsqueeze(1).broadcast_to([P, NT, P]), ALU.mult).then_inc(s_cbv, 1)
                dve.wait_ge(s_dec, l + 1)
                dve.wait_ge(s_trv, l * 5 + 5)
                dve.wait_ge(s_cbv, l * 2 + 2)
                for tt in range(NT):
                    for g in range(2):
                        dve.wait_ge(s_r, l * 8 + tt * 2 + g + 1)
                        if tt >= 1:
                            dve.wait_ge(s_sm, l * 8 + tt * 2 + g - 1)
                        sums = tiny[:, 8, tt * HEADS + 4 * g:tt * HEADS + 4 * g + 4].unsqueeze(2).broadcast_to([P, 4, P])
                        link(v.tensor_tensor(seg[:, g, :].rearrange("p (h c) -> p h c", h=4),
                                             bank[7 if g == 0 else 2][:, :].rearrange("p (h c) -> p h c", h=4),
                                             sums, ALU.subtract))
                        v.tensor_scalar(seg[:, g, :], seg[:, g, :], 0.0, None, ALU.min).then_inc(s_seg, 1)
                    if tt < NT - 1:
                        if tt >= 1:
                            dve.wait_ge(s_y, l * NT + tt)
                        v.tensor_tensor(heads(xdd[:, :]), heads(xdt[:, tt, :]), by_head(11, tt), ALU.mult).then_inc(s_xdd, 1)
                    for g in range(2):
                        dve.wait_ge(s_exp, l * 8 + tt * 2 + g + 1)
                        if tt >= 1:
                            dve.wait_ge(s_y, l * NT + tt)
                        v.tensor_tensor(smat[:, g, :].rearrange("p (h c) -> p h c", h=4),
                                        seg[:, g, :].rearrange("p (h c) -> p h c", h=4),
                                        cbm[:, g, tt, :].unsqueeze(1).broadcast_to([P, 4, P]), ALU.mult).then_inc(s_sm, 1)
                    dve.wait_ge(s_y, l * NT + tt + 1)
                    if tt < NT - 1:
                        for g in range(2):
                            r = slice(64 * g, 64 * g + 64)
                            st = state[r, :].rearrange("p (h c) -> p h c", c=HD)
                            gain = bank[5][r, 0:256].rearrange("p (h c) -> p h c", c=HD)
                            if tt == 0:
                                ins = v.tensor_copy(st, gain)
                            else:
                                total = tiny[r, 13, tt * HEADS + 4 * g:tt * HEADS + 4 * g + 4].unsqueeze(2).broadcast_to([64, 4, HD])
                                link(v.tensor_tensor(st, st, total, ALU.mult))
                                ins = v.tensor_tensor(st, st, gain, ALU.add)
                            if g == 1:
                                ins.then_inc(s_st, 1)
                    if tt == 0:
                        v.tensor_copy(y_tok[:, tt, :], bank[3][:, :]).then_inc(s_yv, 1)
                    else:
                        for g in range(2):
                            ins = v.tensor_tensor(heads(y_tok[:, tt, g * 256:(g + 1) * 256]), heads(bank[4 + 2 * g][:, 0:256]),
                                                  by_head(9, tt)[:, 4 * g:4 * g + 4, :], ALU.mult)
                        link(ins)
                        v.tensor_tensor(y_tok[:, tt, :], y_tok[:, tt, :], bank[3][:, :], ALU.add).then_inc(s_yv, 1)
                dve.wait_ge(s_taken, l * TAKEN + N_IN + 2)
                for j in range(4):
                    dve.wait_ge(s_yt, l * 4 + j + 1)
                    link(v.scalar_tensor_tensor(xbc[:, j, :], xbc[:, j, :], pcol("d_skip")[:, j:j + 1],
                                                bank[2 + j][:, :], ALU.mult, ALU.add))
                    v.tensor_tensor(xbc[:, j, :], xbc[:, j, :], pj[:, Z0 + j, PAD:PJW], ALU.mult).then_inc(s_ygv, 1)
                def att_scaled(h):
                    dve.wait_ge(s_z, l * 4 + h + 1)
                    for b, n, o in ((2, 512, 0), (3, 384, 512), (4, 384, 896)):
                        ins = v.tensor_scalar(zs[h % 2][:, o:o + n], bank[b][:, 0:n], HD ** -0.5, None, ALU.mult)
                    ins.then_inc(s_zv, 1)

                def att_keep(h):
                    dve.wait_ge(s_lg, l * 4 + h + 1)
                    lk = nlk[h % 2]
                    link(v.scalar_tensor_tensor(lk[:, :], zs[h % 2][:, :], 0.0, ez[:, :], ALU.max, ALU.add))
                    for i in range(NT):
                        ins = v.tensor_tensor(lk[:, O4[i]:O4[i] + P], lk[:, O4[i]:O4[i] + P], tri_lt[:, :], ALU.mult)
                    ins.then_inc(s_nlk, 1)

                def att_taken(h):
                    r = slice(64 * (h % 2), 64 * (h % 2) + 64)
                    dve.wait_ge(s_ay, l * 4 + h + 1)
                    v.tensor_copy(mixed[r, 6 + h // 2, :], bank[h % 2][r, :]).then_inc(s_ayv, 1)

                att_scaled(0)
                for g in range(2):
                    dve.wait_ge(s_yss, l * 2 + g + 1)
                    inv_root(bank[g][:, :], 2 * P, s_yvar, s_yroot, l * 2 + g + 1)
                    for j in (2 * g, 2 * g + 1):
                        ins = v.scalar_tensor_tensor(mixed[:, j, :], xbc[:, j, :], pcol("ssd_g")[:, j:j + 1],
                                                     nrm[:, 2, :], ALU.mult, ALU.mult)
                    if g == 0:
                        link(ins)
                        att_scaled(1)
                        att_keep(0)
                    else:
                        ins.then_inc(s_ymix, 1)
                dve.wait_ge(s_ymix, l + 1)
                att_keep(1)
                for h in range(SB_HEADS):
                    w = arg[h % 2]
                    dve.wait_ge(s_cum, l * 4 + h + 1)
                    for b, n, o in ((5, 512, 0), (6, 384, 512), (7, 384, 896)):
                        ins = v.tensor_tensor(w[:, o:o + n], zs[h % 2][:, o:o + n], bank[b][:, 0:n], ALU.subtract)
                    link(ins)
                    for i in range(NT):
                        ins = v.tensor_scalar(w[:, O4[i]:O4[i] + P], w[:, O4[i]:O4[i] + P], 0.0, None, ALU.min)
                    ins.then_inc(s_arg, 1)
                    if h + 2 < SB_HEADS:
                        att_scaled(h + 2)
                    dve.wait_ge(s_w, l * 4 + h + 1)
                    for i in range(NT):
                        ins = v.tensor_tensor(w[:, O4[i]:O4[i] + P], w[:, O4[i]:O4[i] + P], tri_lt[:, :], ALU.mult)
                    ins.then_inc(s_wm, 1)
                    if h + 2 < SB_HEADS:
                        att_keep(h + 2)
                    if h == 0:
                        dve.wait_ge(s_hh, l * HI_PARTS + (KT + 1))
                        v.tensor_tensor(hL[:, 0:6, :], mixed[:, 0:6, :], hH[:, 0:6, :].bitcast(F32), ALU.subtract)
                    if h >= 1:
                        att_taken(h - 1)
                att_taken(SB_HEADS - 1)
                dve.wait_ge(s_hh, l * HI_PARTS + (KT + 2))
                v.tensor_tensor(hL[:, 6:8, :], mixed[:, 6:8, :], hH[:, 6:8, :].bitcast(F32),
                                ALU.subtract).then_inc(s_rhs, 1)
                with dve.Fori(0, N_OUT // 2) as i:
                    for s in range(2):
                        lo(l, i + (OUT0 // 2 + 1), s, i * 2 + (OUT0 + s))
                        k = i * 2 + s
                        xk = x[:, bass.ds(k, 1), :].rearrange("p a t -> p (a t)")
                        v.scalar_tensor_tensor(xk, bank[s][:, :], mod[:, 2, bass.ds(k, 1)], xk,
                                               ALU.mult, ALU.add).then_inc(s_taken, 1)
                normed(l, 1)
                modulated(l, 1)
                each = lambda f: [f(tt) for tt in range(NT)][-1]

                def best_keys(n, s):
                    sc = lambda tt: bank[2 + s][:, tt * P:(tt + 1) * P]
                    dve.wait_ge(s_sc, l * N_Q + n + 3)
                    steps.settle()
                    link(each(lambda tt: v.max(v16[:, s, tt, 0:8], sc(tt))))
                    steps.settle()
                    each(lambda tt: v.max_index(i16[:, s, tt, 0:8], v16[:, s, tt, 0:8], sc(tt)))
                    ins = each(lambda tt: v.match_replace(sc2[:, tt, :], v16[:, s, tt, 0:8], sc(tt), -3.0e38))
                    ins.then_inc(s_scv, 1)
                    dve.wait_ge(s_scv, l * N_Q + n + 3)
                    steps.settle()
                    link(each(lambda tt: v.max(v16[:, s, tt, 8:16], sc2[:, tt, :])))
                    steps.settle()
                    link(each(lambda tt: v.max_index(i16[:, s, tt, 8:16], v16[:, s, tt, 8:16], sc2[:, tt, :])))
                    v.tensor_copy(topv[:, :, bass.ds(n, 1), :].rearrange("p t a k -> p t (a k)"), v16[:, s, :, :])
                    return v.tensor_copy(topi[:, :, bass.ds(n, 1), :].rearrange("p t a k -> p t (a k)"), i16[:, s, :, :])

                lo(l, WQ0 // 2 + 1, 0, WQ0)
                with dve.Fori(0, N_Q // 2 - 1) as i:
                    with steps.loop(i, N_Q // 2 - 1, 2 * 3):
                        for s in range(2):
                            lo(l, i + (WQ0 // 2 + 1 + s), 1 - s, i * 2 + (WQ0 + s + 1))
                            best_keys(i * 2 + s, s)
                lo(l, WQ0 // 2 + N_Q // 2, 1, WQ0 + N_Q - 1)
                best_keys(N_Q - 2, 0)
                link(best_keys(N_Q - 1, 1))
                steps.settle()
                def u_lo(g, j):
                    lo(l, g * (GROUP // 2) + (U0 // 2 + j // 2 + 1), j % 2, g * GROUP + (U0 + j))

                with dve.Fori(0, NT) as tt:
                    with steps.loop(tt, NT, 16):
                        def u_next(m):
                            u_lo(tt * G_PICK + m // GROUP, m % GROUP)

                        tv = topv[:, bass.ds(tt, 1), :, :].rearrange("p t (h i) k -> p (t h) i k", i=2)
                        ti = topi[:, bass.ds(tt, 1), :, :].rearrange("p t (h i) k -> p (t h) i k", i=2)
                        full = [P, PH, TOPK, TOPK]
                        each = lambda f: [f(h) for h in range(PH)][-1]
                        u_next(0)
                        link(v.tensor_tensor(cand[:, :, :].rearrange("p h (a b) -> p h a b", a=TOPK),
                                             tv[:, :, 0, :].unsqueeze(3).broadcast_to(full),
                                             tv[:, :, 1, :].unsqueeze(2).broadcast_to(full), ALU.add))
                        u_next(1)
                        link(each(lambda h: v.max(bestv[:, h, 0:8], cand[:, h, :])))
                        u_next(2)
                        each(lambda h: v.max_index(bestp[:, h, 0:8], bestv[:, h, 0:8], cand[:, h, :]))
                        u_next(3)
                        link(each(lambda h: v.match_replace(cand2[:, h, :], bestv[:, h, 0:8], cand[:, h, :], -3.0e38)))
                        u_next(4)
                        link(each(lambda h: v.max(bestv[:, h, 8:16], cand2[:, h, :])))
                        u_next(5)
                        link(each(lambda h: v.max_index(bestp[:, h, 8:16], bestv[:, h, 8:16], cand2[:, h, :])))
                        link(v.tensor_copy(gsum[:, 0, :], bestv[:, :, 0]))
                        v.tensor_tensor(bestv[:, :, :], bestv[:, :, :],
                                        gsum[:, 0, :].unsqueeze(2).broadcast_to([P, PH, TOPK]),
                                        ALU.subtract).then_inc(s_shift, 1)
                        u_next(6)
                        flat = bestp[:, :, :].rearrange("p h k -> p (h k)")
                        v.tensor_scalar(posu[:, 0, :], flat, 4, None, ALU.logical_shift_right)
                        link(v.tensor_scalar(posu[:, 1, :], flat, 15, None, ALU.bitwise_and))
                        link(v.tensor_copy(posf[:, :, :], posu[:, :, :]))
                        for a in range(2):
                            pk = pick[:, :, :]
                            pk4 = pick[:, :, :].rearrange("p (h k) j -> p h k j", h=PH)
                            link(v.tensor_tensor(pk, posf[:, a, :].unsqueeze(2).broadcast_to([P, HK, TOPK]),
                                                 iota[:, 0:TOPK].unsqueeze(1).broadcast_to([P, HK, TOPK]), ALU.is_equal))
                            u_next(7 + 2 * a)
                            link(v.tensor_tensor(pk4, pk4, ti[:, :, a, :].unsqueeze(2).broadcast_to(full), ALU.mult))
                            u_next(8 + 2 * a)
                            link(v.reduce_sum(route[:, a, :], pk, AX.X))
                        dve.wait_ge(s_gexp, l * NT + tt + 1)
                        link(v.reduce_sum(gsum[:, 0, :], bestv[:, :, :], AX.X))
                        link(v.reciprocal(gsum[:, 1, :], gsum[:, 0, :]))
                        v.tensor_tensor(route[:, 2, :].rearrange("p (h k) -> p h k", h=PH), bestv[:, :, :],
                                        gsum[:, 1, :].unsqueeze(2).broadcast_to([P, PH, TOPK]),
                                        ALU.mult).then_inc(s_rt, 1)
                        u_next(11)
                        dve.wait_ge(s_idx, l * NT + tt + 1)
                with dve.Fori(0, G_GATE) as i:
                    for j in range(GROUP):
                        for u in range(TILE_QUADS):
                            q = i * (GROUP * TILE_QUADS) + (j * TILE_QUADS + u)
                            dve.wait_ge(s_gm, l * QUADS + 1 + q)
                            for q_ in range(QUAD):
                                t = q * QUAD + q_
                                v.tensor_scalar(oneh[:, u, q_, :], iota[:, :], idxT[:, 0, bass.ds(t, 1)], None, ALU.is_equal)
                                ins = v.tensor_scalar(gateh[:, u, q_, :], iota[:, :], idxT[:, 1, bass.ds(t, 1)],
                                                      idxT[:, 2, bass.ds(t, 1)], ALU.is_equal, ALU.mult)
                            ins.then_inc(s_oh, 1)
                        u_lo(i + G_GATE0, j)
                with dve.Fori(G_REST0, GROUPS - 1) as g:
                    for j in range(GROUP):
                        u_lo(g, j)

                def coefs(h, s, j):
                    if j == 0:
                        dve.wait_ge(s_gin[s], (l * (GROUPS // 2) + h + 1) * 16)
                        dve.wait_ge(s_ain[s], (l * (GROUPS // 2) + h + 1) * 16)
                    link(v.tensor_tensor(coef[:, j % 2, :].rearrange("p (c t) -> p c t", c=GCHUNKS),
                                         act_in[s][:, j // 2, j % 2, :].rearrange("p (c t) -> p c t", c=GCHUNKS),
                                         gates[s][:, :, j, :], ALU.mult))
                    link(v.tensor_copy(c_hi[:, j, :], coef[:, j % 2, :]))
                    v.tensor_tensor(c_lo[:, j, :], coef[:, j % 2, :], c_hi[:, j, :].bitcast(F32),
                                    ALU.subtract).then_inc(s_coef, 1)

                for j in range(GROUP):
                    if j >= 2:
                        coefs(0, 0, j - 2)
                    u_lo(GROUPS - 1, j)
                def v_group(h, s, ahead=True):
                    for j in range(GROUP):
                        term = s * ADA_ROWS + j
                        ada_term(l * ADA_TERMS + h * KT + (ADA_TERMS + term),
                                 (l * ADA_BLOCKS + h + (ADA_BLOCKS // 2 + 1)) * 16, h, term, s)
                        if j >= 2 and not ahead:
                            continue
                        if j < 2:
                            coefs(h, s, j + 2)
                        else:
                            coefs(h + s, 1 - s, j - 2)
                        b = h * (2 * GROUP) + (s * GROUP + j)
                        lo(l, h * GROUP + (EV0 // 2 + s * 2 + j // 2 + 1), j % 2, b + EV0)

                with dve.Fori(0, GROUPS // 2 - 1) as h:
                    with steps.loop(h, GROUPS // 2 - 1, 2 * 2 * GROUP):
                        v_group(h, 0)
                        v_group(h, 1)
                v_group(GROUPS // 2 - 1, 0)
                v_group(GROUPS // 2 - 1, 1, ahead=False)
                for k in range(KT):
                    if k < KT - 1:
                        dve.wait_ge(s_out, l * (KT - 1) + k + 1)
                    else:
                        dve.wait_ge(s_tile, l * STREAM + STREAM)
                    link(v.scalar_tensor_tensor(x[:, k, :], bank[k][:, :], mod[:, 5, k:k + 1], x[:, k, :],
                                                ALU.mult, ALU.add))
                v.memset(tiny[:, 15, 0:1], 0.0).then_inc(s_gate, 1)
                assert steps.n == DVE_STEPS, steps.n
            steps.base, steps.n = LAYERS * DVE_STEPS, 0
            normed(LAYERS, 0)
            for k in range(KT):
                ins = v.scalar_tensor_tensor(x[:, k, :], x[:, k, :], fin_g[:, k:k + 1], nrm[:, 2, :], ALU.mult, ALU.mult)
            ins.then_inc(s_fin, 1)


def kernel(**inputs):
    import numpy as np
    import concourse.bacc as bacc
    from concourse.bass_utils import run_bass_kernel_spmd

    a = {k: np.asarray(v) for k, v in inputs.items()}
    L = LAYERS

    def cols(v, n=KT):
        return v.reshape(L, n, P).transpose(0, 2, 1)

    def tiles(w):
        return w.reshape(L, KT, P, -1, P).transpose(0, 3, 2, 1, 4)

    w_in = a["w_in"]
    dt0 = 1280
    z_end, xp_end = 4 * P, dt0 + HEADS + 2 * P
    w_cols = np.concatenate([w_in[:, :, z_end:dt0], w_in[:, :, dt0 + HEADS:xp_end], w_in[:, :, :z_end],
                             w_in[:, :, xp_end:]], axis=2)
    w_dt = w_in[:, :, dt0:dt0 + HEADS].reshape(L, KT, P, HEADS).transpose(0, 2, 1, 3).reshape(L, P, KT * HEADS)
    u = a["peer_u"].reshape(L, N_KEYS, N_KEYS, KT, P).transpose(0, 2, 4, 3, 1)
    ev = a["peer_v"].reshape(L, N_KEYS, N_KEYS, D).transpose(0, 2, 1, 3).reshape(L, N_KEYS, P, KT, P)
    stream = np.concatenate([tiles(w_cols), tiles(a["w_out"]), tiles(a["peer_wq"]), u, ev],
                            axis=1).reshape(L, STREAM, P, D)
    ada = np.roll(a["ada_w"], -1, axis=0).reshape(L, 2, ADA_ROWS, P, ADA_BLOCKS, ADA_W).transpose(0, 4, 1, 3, 2, 5)
    ada = ada.reshape(L, 2 * ADA_BLOCKS, P, ADA_ROWS, ADA_W)
    pw = np.zeros((L, 2, P, P), np.float32)
    for j in range(4):
        o = 64 * (j % 2)
        pw[:, j // 2, o:o + 64, o:o + 64] = a["pool_w"][:, j]
    wide = lambda v: np.broadcast_to(v[:, None, :], (L, P, HEADS))
    packed = {
        "ada_b": cols(a["ada_b"], 48), "g_mix": cols(a["mix_norm_g"]), "g_ffn": cols(a["ffn_norm_g"]),
        "conv_w": a["conv_w"].reshape(L, 4, 6, P).transpose(0, 3, 2, 1).reshape(L, P, 24),
        "conv_b": cols(a["conv_b"], 6), "ssd_g": cols(a["ssd_norm_g"], 4), "pool_scale": cols(a["pool_scale"], 2),
        "d_skip": cols(np.repeat(a["d_skip"], HD, axis=1), 4), "dt_bias": wide(a["dt_bias"]), "a_log": wide(a["a_log"]),
        "w_dt": w_dt, "pool_w": pw.transpose(0, 2, 1, 3).reshape(L, P, 2 * P),
    }
    arrays = {
        "xT": a["x"][0].T.reshape(KT, P, T).transpose(1, 0, 2),
        "cT": a["c"][0].reshape(KT, P).T,
        "final_g": a["final_norm_g"].reshape(KT, P).T,
        "adaw": ada, "wst": stream,
        "params": np.concatenate([packed[n] for n, _ in PARAMS], axis=2),
        "keysT": a["peer_keys"].transpose(0, 4, 1, 2, 3).reshape(L, P, SEGS, N_KEYS),
    }
    arrays = {k: np.ascontiguousarray(v) for k, v in arrays.items()}
    nc = bacc.Bacc("TRN2", target_bir_lowering=False, num_devices=1)
    aps = [nc.dram_tensor(k, v.shape, F32, kind="ExternalInput").ap() for k, v in arrays.items()]
    g_dram = nc.dram_tensor("gate_matrices", (GCHUNKS, P, N_KEYS, GCHUNK), F32).ap()
    a_dram = nc.dram_tensor("activations", (N_KEYS // 2, P, 2, T), F32).ap()
    out = nc.dram_tensor("outT", (P, KT, T), F32, kind="ExternalOutput").ap()
    build(nc, *aps, g_dram, a_dram, out)
    r = run_bass_kernel_spmd(nc, [arrays], core_ids=[0])
    got = r.results[0]["outT"]
    return got.transpose(2, 1, 0).reshape(1, T, D)
```
